# Optimizing a Trainium2 kernel written in Bass

```python
import math, functools
import jax, jax.numpy as jnp
from jax import lax
import numpy as np
import math

D_MODEL = 1024
BATCH = 1
SEQ = 256
DEPTH = 2

GRID_W = 64
CTX_LEN = 256
N_MIXERS = 2
N_A_LAYERS = (DEPTH + 1) // 2
N_B_LAYERS = DEPTH // 2
D_FF = 2816
N_MOD = 9
EPS = 1e-6
ROPE_BASE = 10000.0
Q_BLOCK = 128
NEG_INF = -1e30

A_HEADS = 8
A_HEAD_DIM = 64
A_V_DIM = 2 * A_HEAD_DIM
A_QKV_COLS = 3 * A_HEADS * A_V_DIM
A_WIDTH = A_HEADS * A_V_DIM

B_Q_HEADS = 16
B_KV_HEADS = 4
B_HEAD_DIM = 64
B_GROUP = B_Q_HEADS // B_KV_HEADS
B_QKV_COLS = (B_Q_HEADS + 2 * B_KV_HEADS) * B_HEAD_DIM
B_WIDTH = B_Q_HEADS * B_HEAD_DIM
WINDOW = 128
BAND_BLOCK = 128


def rms(x):
    xf = x.astype(jnp.float32)
    return (xf * lax.rsqrt(jnp.mean(xf * xf, axis=-1, keepdims=True) + EPS)).astype(x.dtype)

def rms_gain(x, g):
    return rms(x) * g

def modulate(h, shift, scale):
    return h * (1 + scale) + shift

def swiglu(h, wi, wo):
    g, u = jnp.split(h @ wi, 2, axis=-1)
    return (jax.nn.silu(g) * u) @ wo

def axial_rope_tables(rows, head_dim):
    nf = head_dim // 4
    inv = ROPE_BASE ** (-jnp.arange(nf, dtype=jnp.float32) / nf)
    row = jnp.broadcast_to(jnp.arange(rows, dtype=jnp.float32)[:, None], (rows, GRID_W)).reshape(-1)
    col = jnp.broadcast_to(jnp.arange(GRID_W, dtype=jnp.float32)[None, :], (rows, GRID_W)).reshape(-1)
    ang = jnp.stack([row[:, None] * inv, col[:, None] * inv], axis=1)
    ang = jnp.stack([ang, ang], axis=2).reshape(rows * GRID_W, head_dim)
    return jnp.cos(ang), jnp.sin(ang)

def apply_rope(x, cos, sin):
    dh = x.shape[-1]
    xr = x.reshape(x.shape[:-1] + (2, 2, dh // 4))
    rot = jnp.stack([-xr[..., 1, :], xr[..., 0, :]], axis=-2).reshape(x.shape)
    return (x * cos + rot * sin).astype(x.dtype)

def diff_attention(h_lat, h_ctx, w_qkv, w_o, q_gain, k_gain, lam_vec, subln_gain, lam_init, cos, sin, ctx_out):
    B, L, _ = h_lat.shape

    def project(h):
        q, k, v = jnp.split(h @ w_qkv, [A_WIDTH, 2 * A_WIDTH], axis=-1)
        q = rms_gain(q.reshape(B, -1, A_HEADS, 2, A_HEAD_DIM), q_gain)
        k = rms_gain(k.reshape(B, -1, A_HEADS, 2, A_HEAD_DIM), k_gain)
        return q, k, v.reshape(B, -1, A_HEADS, A_V_DIM)

    q_l, k_l, v_l = project(h_lat)
    q_c, k_c, v_c = project(h_ctx)
    rc, rs = cos[:, None, None, :], sin[:, None, None, :]
    q_l, k_l = apply_rope(q_l, rc, rs), apply_rope(k_l, rc, rs)

    lv = lam_vec.astype(jnp.float32)
    lam = jnp.exp(jnp.sum(lv[0] * lv[1])) - jnp.exp(jnp.sum(lv[2] * lv[3])) + lam_init
    scale = A_HEAD_DIM ** -0.5

    def attend(q, k, v):
        s = jnp.einsum('bqhcd,bkhcd->bhcqk', q, k).astype(jnp.float32) * scale
        p = jax.nn.softmax(s, axis=-1)
        a = (p[:, :, 0] - lam * p[:, :, 1]).astype(v.dtype)
        return jnp.einsum('bhqk,bkhe->bqhe', a, v)

    def finish(o):
        o = rms_gain(o, subln_gain) * (1.0 - lam_init)
        return o.reshape(o.shape[0], o.shape[1], A_WIDTH) @ w_o

    k_all = jnp.concatenate([k_l, k_c], axis=1)
    v_all = jnp.concatenate([v_l, v_c], axis=1)
    nb = L // Q_BLOCK
    qb = q_l.reshape(B, nb, Q_BLOCK, A_HEADS, 2, A_HEAD_DIM).transpose(1, 0, 2, 3, 4, 5)
    o_l = lax.map(lambda qblk: attend(qblk, k_all, v_all), qb)
    o_l = o_l.transpose(1, 0, 2, 3, 4).reshape(B, L, A_HEADS, A_V_DIM)
    out_l = finish(o_l)
    out_c = finish(attend(q_c, k_c, v_c)) if ctx_out else None
    return out_l, out_c

def window_gqa(h_lat, h_ctx, w_qkv, w_o, q_gain, k_gain, sink, cos, sin, ctx_out):
    B, L, _ = h_lat.shape
    nb = L // BAND_BLOCK
    BB = BAND_BLOCK

    def project(h):
        q, k, v = jnp.split(h @ w_qkv, [B_WIDTH, B_WIDTH + B_KV_HEADS * B_HEAD_DIM], axis=-1)
        q = rms_gain(q.reshape(B, -1, B_KV_HEADS, B_GROUP, B_HEAD_DIM), q_gain)
        k = rms_gain(k.reshape(B, -1, B_KV_HEADS, B_HEAD_DIM), k_gain)
        return q, k, v.reshape(B, -1, B_KV_HEADS, B_HEAD_DIM)

    q_l, k_l, v_l = project(h_lat)
    q_c, k_c, v_c = project(h_ctx)
    q_l = apply_rope(q_l, cos[:, None, None, :], sin[:, None, None, :])
    k_l = apply_rope(k_l, cos[:, None, :], sin[:, None, :])
    scale = B_HEAD_DIM ** -0.5
    sink_f = sink.astype(jnp.float32).reshape(B_KV_HEADS, B_GROUP)

    def band(t):
        tb = jnp.pad(t, ((0, 0), (BB, BB), (0, 0), (0, 0))).reshape(B, nb + 2, BB, B_KV_HEADS, B_HEAD_DIM)
        return jnp.concatenate([tb[:, :-2], tb[:, 1:-1], tb[:, 2:]], axis=2)

    k_w, v_w = band(k_l), band(v_l)
    qb = q_l.reshape(B, nb, BB, B_KV_HEADS, B_GROUP, B_HEAD_DIM)
    s_w = jnp.einsum('bnqhgd,bnkhd->bnhgqk', qb, k_w).astype(jnp.float32) * scale
    s_c = jnp.einsum('bnqhgd,bkhd->bnhgqk', qb, k_c).astype(jnp.float32) * scale
    qi = jnp.arange(BB)
    kj = jnp.arange(3 * BB)
    rel = kj[None, :] - BB - qi[:, None]
    kpos = jnp.arange(nb)[:, None] * BB - BB + kj[None, :]
    valid = (jnp.abs(rel) <= WINDOW)[None] & ((kpos >= 0) & (kpos < L))[:, None, :]
    s_w = jnp.where(valid[None, :, None, None], s_w, NEG_INF)
    sink_b = jnp.broadcast_to(sink_f[None, None, :, :, None, None], s_w.shape[:-1] + (1,))
    n_ctx = k_c.shape[1]
    p = jax.nn.softmax(jnp.concatenate([s_w, s_c, sink_b], axis=-1), axis=-1)
    p_w = p[..., :3 * BB].astype(v_w.dtype)
    p_c = p[..., 3 * BB:3 * BB + n_ctx].astype(v_c.dtype)
    o = jnp.einsum('bnhgqk,bnkhd->bnqhgd', p_w, v_w) + jnp.einsum('bnhgqk,bkhd->bnqhgd', p_c, v_c)
    out_l = o.reshape(B, L, B_WIDTH) @ w_o
    out_c = None
    if ctx_out:
        s = jnp.einsum('bqhgd,bkhd->bhgqk', q_c, k_c).astype(jnp.float32) * scale
        sb = jnp.broadcast_to(sink_f[None, :, :, None, None], s.shape[:-1] + (1,))
        pc = jax.nn.softmax(jnp.concatenate([s, sb], axis=-1), axis=-1)[..., :n_ctx].astype(v_c.dtype)
        oc = jnp.einsum('bhgqk,bkhd->bqhgd', pc, v_c)
        out_c = oc.reshape(B, n_ctx, B_WIDTH) @ w_o
    return out_l, out_c

def layer(x, xc, mod_l, mod_c, pre_wi, pre_wo, post_wi, post_wo, mixer, ctx_out):
    sh1, sc1, g1, sh2, sc2, g2, sh3, sc3, g3 = jnp.split(mod_l, N_MOD, axis=-1)
    ch1, cc1, cg1, ch2, cc2, cg2, ch3, cc3, cg3 = jnp.split(mod_c, N_MOD, axis=-1)

    def ffn_step(t, sh, sc, g, wi, wo):
        return t + 0.5 * g * swiglu(modulate(rms(t), sh, sc), wi, wo)

    x = ffn_step(x, sh1, sc1, g1, pre_wi, pre_wo)
    xc = ffn_step(xc, ch1, cc1, cg1, pre_wi, pre_wo)
    o_l, o_c = mixer(h_lat=modulate(rms(x), sh2, sc2), h_ctx=modulate(rms(xc), ch2, cc2), ctx_out=ctx_out)
    x = x + g2 * o_l
    x = ffn_step(x, sh3, sc3, g3, post_wi, post_wo)
    if ctx_out:
        xc = xc + cg2 * o_c
        xc = ffn_step(xc, ch3, cc3, cg3, post_wi, post_wo)
    return x, xc

def first_inputs(seed: int = 0) -> dict:
    key = jax.random.key(seed)
    ks = jax.random.split(key, 24)
    f32 = jnp.float32
    D = D_MODEL

    def nrm(k, shape, s):
        return jax.random.normal(k, shape, f32) * s

    return {
        "x": nrm(ks[0], (BATCH, SEQ, D), 1.0),
        "c": nrm(ks[1], (BATCH, D), 1.0),
        "ctx": nrm(ks[2], (BATCH, CTX_LEN, D), 1.0),
        "c_ctx": nrm(ks[3], (D,), 1.0),
        "ada_w": nrm(ks[4], (DEPTH, D, N_MOD * D), 0.5 * D ** -0.5),
        "ada_b": nrm(ks[5], (DEPTH, N_MOD * D), 0.02),
        "ffn_pre_wi": nrm(ks[6], (DEPTH, D, 2 * D_FF), D ** -0.5),
        "ffn_pre_wo": nrm(ks[7], (DEPTH, D_FF, D), D_FF ** -0.5),
        "ffn_post_wi": nrm(ks[8], (DEPTH, D, 2 * D_FF), D ** -0.5),
        "ffn_post_wo": nrm(ks[9], (DEPTH, D_FF, D), D_FF ** -0.5),
        "a_w_qkv": nrm(ks[10], (N_A_LAYERS, D, A_QKV_COLS), D ** -0.5),
        "a_w_o": nrm(ks[11], (N_A_LAYERS, A_WIDTH, D), A_WIDTH ** -0.5),
        "a_q_gain": 1.0 + nrm(ks[12], (N_A_LAYERS, A_HEAD_DIM), 0.1),
        "a_k_gain": 1.0 + nrm(ks[13], (N_A_LAYERS, A_HEAD_DIM), 0.1),
        "a_lambda": nrm(ks[14], (N_A_LAYERS, 4, A_HEAD_DIM), 0.1),
        "a_subln_gain": 1.0 + nrm(ks[15], (N_A_LAYERS, A_V_DIM), 0.1),
        "b_w_qkv": nrm(ks[16], (N_B_LAYERS, D, B_QKV_COLS), D ** -0.5),
        "b_w_o": nrm(ks[17], (N_B_LAYERS, B_WIDTH, D), B_WIDTH ** -0.5),
        "b_q_gain": 1.0 + nrm(ks[18], (N_B_LAYERS, B_HEAD_DIM), 0.1),
        "b_k_gain": 1.0 + nrm(ks[19], (N_B_LAYERS, B_HEAD_DIM), 0.1),
        "b_sink": nrm(ks[20], (N_B_LAYERS, B_Q_HEADS), 0.5),
    }

def first_block(x, c, ctx, c_ctx, ada_w, ada_b, ffn_pre_wi, ffn_pre_wo, ffn_post_wi, ffn_post_wo,
              a_w_qkv, a_w_o, a_q_gain, a_k_gain, a_lambda, a_subln_gain,
              b_w_qkv, b_w_o, b_q_gain, b_k_gain, b_sink):
    n_tok = x.shape[1]
    rows = n_tok // GRID_W
    cos, sin = axial_rope_tables(rows, A_HEAD_DIM)
    xc = ctx
    for i in range(DEPTH):
        mod_l = (jax.nn.silu(c) @ ada_w[i] + ada_b[i])[:, None, :]
        mod_c = jax.nn.silu(c_ctx) @ ada_w[i] + ada_b[i]
        ctx_out = i < DEPTH - 1
        j = i // N_MIXERS
        if i % N_MIXERS == 0:
            mixer = functools.partial(diff_attention, w_qkv=a_w_qkv[j], w_o=a_w_o[j], q_gain=a_q_gain[j],
                                      k_gain=a_k_gain[j], lam_vec=a_lambda[j], subln_gain=a_subln_gain[j],
                                      lam_init=0.8 - 0.6 * math.exp(-0.3 * i), cos=cos, sin=sin)
        else:
            mixer = functools.partial(window_gqa, w_qkv=b_w_qkv[j], w_o=b_w_o[j], q_gain=b_q_gain[j],
                                      k_gain=b_k_gain[j], sink=b_sink[j], cos=cos, sin=sin)
        x, xc = layer(x, xc, mod_l, mod_c, ffn_pre_wi[i], ffn_pre_wo[i], ffn_post_wi[i], ffn_post_wo[i],
                      mixer, ctx_out)
    return x


N_BRANCH = 4
A_HEADS_2 = 4
A_HEAD_DIM_2 = 128
A_WIDTH_2 = A_HEADS_2 * A_HEAD_DIM_2
IDX_HEADS = 4
IDX_DIM = 64
TOPK_MAX = 256
CB_WIDTH = 512
CB_CONV = 31
CC_WIDTH = 512
CC_CONV = 3
SB_HEADS = 4
SB_HEAD_DIM = 128
SB_WIDTH = SB_HEADS * SB_HEAD_DIM
FFN_CONV = 3
ROPE_THETA = 500000.0
ROT_FRACTION_DIV = 4
BLOCK_Q = 128
NORM_EPS = 1e-6

SPLIT_SIZES = (A_WIDTH_2, A_WIDTH_2, A_WIDTH_2, IDX_HEADS * IDX_DIM, IDX_DIM, IDX_HEADS,
               2 * CB_WIDTH, 3 * CC_WIDTH, 3 * SB_WIDTH, N_BRANCH * D_MODEL)
N_IN = sum(SPLIT_SIZES)


def _split_offsets(sizes):
    offs, acc = [], 0
    for s in sizes[:-1]:
        acc += s
        offs.append(acc)
    return offs

def rms_norm(x, g):
    xf = x.astype(jnp.float32)
    y = xf * lax.rsqrt(jnp.mean(xf * xf, axis=-1, keepdims=True) + NORM_EPS)
    return (y * g.astype(jnp.float32)).astype(x.dtype)

def layer_norm(x, g, b):
    xf = x.astype(jnp.float32)
    mu = jnp.mean(xf, axis=-1, keepdims=True)
    xc = xf - mu
    y = xc * lax.rsqrt(jnp.mean(xc * xc, axis=-1, keepdims=True) + NORM_EPS)
    return (y * g.astype(jnp.float32) + b.astype(jnp.float32)).astype(x.dtype)

def partial_rope(x, pos):
    d = x.shape[-1]
    rot = d // ROT_FRACTION_DIV
    half = rot // 2
    inv_freq = ROPE_THETA ** (-(jnp.arange(half, dtype=jnp.float32) * 2.0) / rot)
    ang = pos.astype(jnp.float32)[..., None] * inv_freq
    cos = jnp.cos(ang)[:, :, None, :]
    sin = jnp.sin(ang)[:, :, None, :]
    xf = x.astype(jnp.float32)
    x1, x2 = xf[..., :half], xf[..., half:rot]
    out = jnp.concatenate([x1 * cos - x2 * sin, x2 * cos + x1 * sin, xf[..., rot:]], axis=-1)
    return out.astype(x.dtype)

def causal_dwconv(x, w, b=None):
    width = w.shape[0]
    y = lax.conv_general_dilated(
        x, w.astype(x.dtype)[:, None, :], window_strides=(1,), padding=[(width - 1, 0)],
        dimension_numbers=('NWC', 'WIO', 'NWC'), feature_group_count=x.shape[-1])
    if b is not None:
        y = y + b.astype(x.dtype)
    return y

def _to_blocks(a, nb):
    return jnp.moveaxis(a.reshape((a.shape[0], nb, BLOCK_Q) + a.shape[2:]), 1, 0)

def _from_blocks(a):
    a = jnp.moveaxis(a, 0, 1)
    return a.reshape(a.shape[0], -1, a.shape[-2] * a.shape[-1])

def dsa_attention(q, k, v, q_idx, k_idx, w_idx):
    bsz, seq = q.shape[0], q.shape[1]
    nb = seq // BLOCK_Q
    k_sel = min(TOPK_MAX, seq // 4)
    kv = jnp.stack([k, v], axis=2)
    s_idx = jnp.arange(seq)
    k_idx_f = k_idx.astype(jnp.float32)

    def block(args):
        qb, qib, wb, tb = args
        rel = jax.nn.relu(jnp.einsum('bthd,bsd->bths', qib.astype(jnp.float32), k_idx_f) * IDX_DIM ** -0.5)
        score = jnp.einsum('bths,bth->bts', rel, wb.astype(jnp.float32)) * IDX_HEADS ** -0.5
        causal = s_idx[None, :] <= tb[:, None]
        score = jnp.where(causal[None], score, -jnp.inf)
        _, sel = lax.top_k(score, k_sel)
        valid = sel <= tb[None, :, None]
        kv_sel = jax.vmap(lambda a, i: a[i])(kv, sel)
        logits = jnp.einsum('bthd,btkhd->bthk', qb.astype(jnp.float32),
                            kv_sel[:, :, :, 0].astype(jnp.float32)) * A_HEAD_DIM_2 ** -0.5
        logits = jnp.where(valid[:, :, None, :], logits, -jnp.inf)
        p = jax.nn.softmax(logits, axis=-1)
        out = jnp.einsum('bthk,btkhd->bthd', p, kv_sel[:, :, :, 1].astype(jnp.float32))
        return out.astype(qb.dtype)

    t_blocks = jnp.arange(seq).reshape(nb, BLOCK_Q)
    out = lax.map(block, (_to_blocks(q, nb), _to_blocks(q_idx, nb), _to_blocks(w_idx, nb), t_blocks))
    return _from_blocks(out)

def stick_breaking_attention(q, k, v):
    seq = q.shape[1]
    nb = seq // BLOCK_Q
    s_idx = jnp.arange(seq)
    k_f = k.astype(jnp.float32)
    v_f = v.astype(jnp.float32)

    def block(args):
        qb, tb = args
        z = jnp.einsum('bthd,bshd->bhts', qb.astype(jnp.float32), k_f) * SB_HEAD_DIM ** -0.5
        mask = (s_idx[None, :] < tb[:, None])[None, None]
        log_keep = jnp.where(mask, jax.nn.log_sigmoid(-z), 0.0)
        between = lax.cumsum(log_keep, axis=3, reverse=True) - log_keep
        a = jnp.where(mask, jnp.exp(jax.nn.log_sigmoid(z) + between), 0.0)
        return jnp.einsum('bhts,bshd->bthd', a, v_f).astype(qb.dtype)

    t_blocks = jnp.arange(seq).reshape(nb, BLOCK_Q)
    out = lax.map(block, (_to_blocks(q, nb), t_blocks))
    return _from_blocks(out)

def second_inputs(seed: int = 0) -> dict:
    key = jax.random.key(seed)
    ks = jax.random.split(key, 24)
    f32 = jnp.float32

    def nrm(k, shape, scale):
        return jax.random.normal(k, shape, f32) * scale

    def gain(k, shape):
        return 1.0 + 0.05 * jax.random.normal(k, shape, f32)

    L, D = DEPTH, D_MODEL
    return {
        "x": jax.random.normal(ks[0], (BATCH, SEQ, D), f32),
        "positions": jnp.broadcast_to(jnp.arange(SEQ, dtype=jnp.int32), (BATCH, SEQ)),
        "g_mix": gain(ks[1], (L, D)),
        "w_in": nrm(ks[2], (L, D, N_IN), D ** -0.5),
        "b_gate": nrm(ks[3], (L, N_BRANCH * D), 0.1),
        "g_qa": gain(ks[4], (L, A_HEAD_DIM_2)),
        "g_ka": gain(ks[5], (L, A_HEAD_DIM_2)),
        "g_kidx": gain(ks[6], (L, IDX_DIM)),
        "w_oa": nrm(ks[7], (L, A_WIDTH_2, D), A_WIDTH_2 ** -0.5),
        "cb_conv_w": nrm(ks[8], (L, CB_CONV, CB_WIDTH), CB_CONV ** -0.5),
        "cb_conv_b": nrm(ks[9], (L, CB_WIDTH), 0.02),
        "cb_ln_g": gain(ks[10], (L, CB_WIDTH)),
        "cb_ln_b": nrm(ks[11], (L, CB_WIDTH), 0.02),
        "w_ob": nrm(ks[12], (L, CB_WIDTH, D), CB_WIDTH ** -0.5),
        "cc_conv_w": nrm(ks[13], (L, CC_CONV, CC_WIDTH), CC_CONV ** -0.5),
        "w_oc": nrm(ks[14], (L, CC_WIDTH, D), CC_WIDTH ** -0.5),
        "w_od": nrm(ks[15], (L, SB_WIDTH, D), SB_WIDTH ** -0.5),
        "w_merge": nrm(ks[16], (L, D, D), D ** -0.5),
        "g_ffn": gain(ks[17], (L, D)),
        "w_ffn_gate": nrm(ks[18], (L, D, D_FF), D ** -0.5),
        "w_ffn_up": nrm(ks[19], (L, D, D_FF), D ** -0.5),
        "ffn_conv_w": nrm(ks[20], (L, FFN_CONV, D_FF), FFN_CONV ** -0.5),
        "w_ffn_down": nrm(ks[21], (L, D_FF, D), D_FF ** -0.5),
    }

def second_block(x, positions, g_mix, w_in, b_gate, g_qa, g_ka, g_kidx, w_oa,
              cb_conv_w, cb_conv_b, cb_ln_g, cb_ln_b, w_ob, cc_conv_w, w_oc, w_od,
              w_merge, g_ffn, w_ffn_gate, w_ffn_up, ffn_conv_w, w_ffn_down):
    bsz, seq, dm = x.shape
    offs = _split_offsets(SPLIT_SIZES)
    for l in range(DEPTH):
        h = rms_norm(x, g_mix[l])
        proj = h @ w_in[l]
        aq, ak, av, iq, ik, iw, glu_in, cc_in, sb_in, gate_in = jnp.split(proj, offs, axis=-1)

        qa = partial_rope(rms_norm(aq.reshape(bsz, seq, A_HEADS_2, A_HEAD_DIM_2), g_qa[l]), positions)
        ka = partial_rope(rms_norm(ak.reshape(bsz, seq, A_HEADS_2, A_HEAD_DIM_2), g_ka[l]), positions)
        va = av.reshape(bsz, seq, A_HEADS_2, A_HEAD_DIM_2)
        qi = partial_rope(iq.reshape(bsz, seq, IDX_HEADS, IDX_DIM), positions)
        ki = partial_rope(rms_norm(ik, g_kidx[l])[:, :, None, :], positions)[:, :, 0]
        y_a = dsa_attention(qa, ka, va, qi, ki, iw) @ w_oa[l]

        glu_a, glu_b = jnp.split(glu_in, 2, axis=-1)
        u = causal_dwconv(glu_a * jax.nn.sigmoid(glu_b), cb_conv_w[l], cb_conv_b[l])
        y_b = jax.nn.silu(layer_norm(u, cb_ln_g[l], cb_ln_b[l])) @ w_ob[l]

        gb, gc, xc = jnp.split(cc_in, 3, axis=-1)
        y_c = (gb * causal_dwconv(gc * xc, cc_conv_w[l])) @ w_oc[l]

        sq, sk, sv = jnp.split(sb_in, 3, axis=-1)
        shp = (bsz, seq, SB_HEADS, SB_HEAD_DIM)
        y_d = stick_breaking_attention(sq.reshape(shp), sk.reshape(shp), sv.reshape(shp)) @ w_od[l]

        gates = jax.nn.sigmoid(gate_in + b_gate[l]).reshape(bsz, seq, N_BRANCH, dm)
        merged = (gates[:, :, 0] * y_a + gates[:, :, 1] * y_b
                  + gates[:, :, 2] * y_c + gates[:, :, 3] * y_d)
        x = x + merged @ w_merge[l]

        h2 = rms_norm(x, g_ffn[l])
        gt = causal_dwconv(h2 @ w_ffn_gate[l], ffn_conv_w[l])
        x = x + (jax.nn.silu(gt) * (h2 @ w_ffn_up[l])) @ w_ffn_down[l]
    return x


def setup_inputs(seed=0):
    out = dict(first_inputs(seed))
    for name, value in second_inputs(seed + 1).items():
        if name != "x":
            out[name + "_2"] = value
    return out


def reference(
    x, c, ctx, c_ctx, ada_w, ada_b, ffn_pre_wi, ffn_pre_wo, ffn_post_wi, ffn_post_wo, a_w_qkv,
    a_w_o, a_q_gain, a_k_gain, a_lambda, a_subln_gain, b_w_qkv, b_w_o, b_q_gain, b_k_gain,
    b_sink, positions_2, g_mix_2, w_in_2, b_gate_2, g_qa_2, g_ka_2, g_kidx_2, w_oa_2,
    cb_conv_w_2, cb_conv_b_2, cb_ln_g_2, cb_ln_b_2, w_ob_2, cc_conv_w_2, w_oc_2, w_od_2,
    w_merge_2, g_ffn_2, w_ffn_gate_2, w_ffn_up_2, ffn_conv_w_2, w_ffn_down_2,
):
    x = first_block(
        x, c, ctx, c_ctx, ada_w, ada_b, ffn_pre_wi, ffn_pre_wo, ffn_post_wi, ffn_post_wo,
        a_w_qkv, a_w_o, a_q_gain, a_k_gain, a_lambda, a_subln_gain, b_w_qkv, b_w_o, b_q_gain,
        b_k_gain, b_sink,
    )
    return second_block(
        x, positions_2, g_mix_2, w_in_2, b_gate_2, g_qa_2, g_ka_2, g_kidx_2, w_oa_2,
        cb_conv_w_2, cb_conv_b_2, cb_ln_g_2, cb_ln_b_2, w_ob_2, cc_conv_w_2, w_oc_2, w_od_2,
        w_merge_2, g_ffn_2, w_ffn_gate_2, w_ffn_up_2, ffn_conv_w_2, w_ffn_down_2,
    )


_drawn_inputs = setup_inputs


def setup_inputs(seed=0):
    import zlib

    import numpy as np

    out = dict(_drawn_inputs(seed))
    spreads = {}
    factors = {'b_q_gain': 6.836,
     'b_k_gain': 6.495,
     'b_sink': 8.0,
     'g_qa_2': 7.305,
     'g_ka_2': 6.951,
     'g_kidx_2': 3.006,
     'cb_conv_b_2': 2.858,
     'cb_ln_b_2': 5.791}
    for name, (base, spread) in spreads.items():
        noise = np.random.default_rng([zlib.crc32(name.encode()), seed]).standard_normal(out[name].shape)
        drawn = base * np.exp(spread * noise) if base else spread * noise
        out[name] = __import__('jax').numpy.asarray(drawn.astype(out[name].dtype))
    for name, factor in factors.items():
        out[name] = (out[name] * factor).astype(out[name].dtype)
    return out
```

```python
import math

import numpy as np

import concourse.bass as bass
from concourse import mybir
from concourse.alu_op_type import AluOpType as ALU

F32 = mybir.dt.float32
F32R = mybir.dt.float32r
I32 = mybir.dt.int32
ACT = mybir.ActivationFunctionType
AX = mybir.AxisListType.X

P = 128
D = 1024
KC = D // P
SEQ = 256
CTX = 256
BOTH = SEQ + CTX
DEPTH = 2
D_FF = 2816
FC = D_FF // P
HALF = FC // 2
N_MOD = 9
MODC = N_MOD * KC
EPS = 1e-6
GRID_W = 64
A_HEADS = 8
B_Q_HEADS = 16
B_KV_HEADS = 4
B_GROUP = B_Q_HEADS // B_KV_HEADS
HD = 64
WINDOW = 128
HEADS2 = 4
TOPK = min(256, SEQ // 4)
CB_TAPS = 31
CC_TAPS = 3
NEG = -1e30
LOWEST = -3e38
LAM_INIT = 0.8 - 0.6 * math.exp(-0.3 * 0)
RING = 3
SLOT = KC * 2 * P
OFF = {}
_at = 0
for _name, _w in (("aq", 512), ("ak", 512), ("av", 512), ("iq", 256), ("ik", 64), ("iw", 4), ("glu", 1024),
                  ("cc", 1536), ("sb", 1536), ("gate", 4096)):
    OFF[_name] = _at
    _at += _w
N_IN = _at

VEC = {}
_at = 0


def _vec(name, width):
    global _at
    VEC[name] = (_at, width)
    _at += width


_vec("cond", KC * 2)
for _l in range(DEPTH):
    _vec(f"ada_b{_l}", MODC * 2)
for _name in ("a_q_gain", "a_k_gain", "a_subln", "b_q_gain", "b_k_gain"):
    _vec(_name, 1)
_vec("lambda", 4 * HD)
_vec("sink", B_Q_HEADS)
for _l in range(DEPTH):
    for _name, _w in (("g_mix", KC), ("b_gate", 4 * KC), ("g_qa", 1), ("g_ka", 1), ("g_kidx", 1),
                      ("cb_w", 4 * CB_TAPS), ("cb_b", 4), ("ln_g", 4), ("ln_b", 4), ("cc_w", 4 * CC_TAPS),
                      ("g_ffn", KC), ("ffn_w", FC * CC_TAPS)):
        _vec(f"{_name}{_l}", _w)
N_VEC = _at

CON = {}
_at = 0
for _name, _w in (("ident", P), ("ones", P), ("blocks", P), ("rot_axial", P), ("rot_part128", P), ("rot_part64", P),
                  ("swap", P), ("suffix", P), ("cos_axial", SEQ), ("sin_axial", SEQ), ("band", 2 * SEQ),
                  ("freq128", 1), ("freq64", 1), ("eps", 1)):
    CON[_name] = (_at, _w)
    _at += _w
N_CON = _at


def shape_constants():
    c = np.zeros((P, N_CON), np.float32)

    def put(name, a):
        o, w = CON[name]
        c[:, o:o + w] = np.asarray(a, np.float32).reshape(P, w)

    lane = np.arange(P)
    put("ident", np.eye(P))
    put("ones", np.ones((P, P)))
    put("blocks", (lane[:, None] // HD) == (lane[None, :] // HD))

    def rotation(half, group):
        r = np.zeros((P, P), np.float32)
        for g in range(0, P, group[0]):
            for b in range(0, group[1], 2 * half):
                for f in range(half):
                    r[g + b + half + f, g + b + f] = -1.0
                    r[g + b + f, g + b + half + f] = 1.0
        return r

    put("rot_axial", rotation(HD // 4, (HD, HD)))
    put("rot_part128", rotation(P // 8, (P, P // 4)))
    put("rot_part64", rotation(HD // 8, (HD, HD // 4)))
    put("swap", np.roll(np.eye(P), HD, axis=0))
    put("suffix", lane[:, None] >= lane[None, :])
    nf = HD // 4
    inv = (np.float32(10000.0) ** (-np.arange(nf, dtype=np.float32) / np.float32(nf))).astype(np.float32)
    t = np.arange(SEQ)
    row, col = (t // GRID_W).astype(np.float32), (t % GRID_W).astype(np.float32)
    ang = np.zeros((HD, SEQ), np.float32)
    for d in range(HD):
        ang[d] = (row if d // (HD // 2) == 0 else col) * inv[d % nf]
    ang = np.concatenate([ang, ang])
    put("cos_axial", np.cos(ang))
    put("sin_axial", np.sin(ang))
    band = np.zeros((P, 2, SEQ), np.float32)
    for q in range(2):
        band[:, q, :] = np.where(np.abs(t[None, :] - (q * P + lane[:, None])) <= WINDOW, 0.0, NEG)
    put("band", band)
    for name, dim in (("freq128", P), ("freq64", HD)):
        rot = dim // 4
        half = rot // 2
        f = (np.float32(500000.0) ** (-(np.arange(half, dtype=np.float32) * np.float32(2.0)) / np.float32(rot)))
        v = np.zeros(P, np.float32)
        for g in range(0, P, dim):
            v[g:g + half] = f
            v[g + half:g + rot] = f
        put(name, v)
    put("eps", np.full(P, EPS))
    return c


class Run:

    def __init__(self, name, n, kc, cols, src, dmas=1):
        self.name, self.n, self.kc, self.cols, self.src, self.dmas = name, n, kc, cols, src, dmas


class Unit:

    def __init__(self, run, rep, j, t, turn=None):
        self.run, self.rep, self.j, self.t, self.turn = run, rep, j, t, turn
        self.slot = rep % RING
        self.j0 = rep - run.t0


def build(nc, x_t, vecs, consts, positions, ada_w, pre_wi, pre_wo, post_wi, post_wo, a_w_qkv, a_w_o, b_w_qkv, b_w_o,
          w_in, w_oa, w_ob, w_oc, w_od, w_merge, w_gate, w_up, w_down, out, stop=None):
    def cols_of(w, col0, width, k0=0, kc=KC):
        def src(j):
            return [(0, w[k0 * P:(k0 + kc) * P, :].rearrange("(k p) m -> p k m", p=P)
                     [:, :, bass.ds(col0 + j * width, width)])]
        return src

    def two_of(wa, ca, wb, cb):
        def src(j):
            return [(0, wa.rearrange("(k p) m -> p k m", p=P)[:, :, bass.ds(ca + j * P, P)]),
                    (P, wb.rearrange("(k p) m -> p k m", p=P)[:, :, bass.ds(cb + j * P, P)])]
        return src

    stages, runs, counts = [], [], {}
    bound = {}

    class Stage:
        def __init__(self, kind, run=None, N=SEQ, h=None, name=None, l=None, gate=None, gain=None, waits=(), ready=None,
                     x_at=None, mod=None, layer=None, halves=(), dim=None, dest=None, ch0=0, rot=None, cos=None, sin=None,
                     tiles=None, after=None, items=(), scale=None, v=None, out=None, per=None, swap=False, iw=None,
                     pair=None, i=None, gates=None, dk=None, dv=None):
            self.kind, self.run, self.N, self.h, self.name, self.l = kind, run, N, h, name, l
            self.gate, self.gain, self.waits, self.ready, self.x_at, self.mod = gate, gain, waits, ready, x_at, mod
            self.layer, self.halves, self.iw, self.pair, self.i, self.gates = layer, halves, iw, pair, i, gates
            self.dim, self.dest, self.ch0, self.rot, self.cos, self.sin = dim, dest, ch0, rot, cos, sin
            self.tiles, self.after, self.items, self.scale, self.v = tiles, after, items, scale, v
            self.out, self.per, self.swap, self.dk, self.dv = out, per, swap, dk, dv
            self.b = {}
            self.before = dict(counts)
            stages.append(self)

        def takes(self, **events):
            for name, n in events.items():
                self.b[name] = counts.get(name, 0)
                counts[name] = counts.get(name, 0) + n
            return self

    def add(run):
        run.t0 = sum(r.n for r in runs)
        runs.append(run)
        return run

    def norm(N, src, mod=None, gain=None):
        return Stage("norm", N=N, x_at=src, mod=mod, gain=gain).takes(squares_ready=KC, square_summed=KC, deviation_ready=1,
                                                       rstd_ready=1, scaled_ready=KC, h_full=KC, h_hi=KC, h_lo=KC)

    def ffn(N, wi, wo, gate):
        s = Stage("ffn", N=N, gate=gate, halves=[])
        for h in range(2):
            wi_run = add(Run("wi", HALF, KC, 2 * P, two_of(wi, h * HALF * P, wi, D_FF + h * HALF * P), 2))
            wo_run = add(Run("wo", KC, HALF, P, cols_of(wo, 0, P, h * HALF, HALF)))
            s.halves.append((wi_run, wo_run))
        s.takes(silu_ready=FC, act_full=FC, act_hi=FC, act_lo=FC, x_done=2 * KC)
        s.h = norms_done()
        return s

    def norms_done():
        return counts["h_lo"] - KC

    def head_units(name, run, N, norm_dim, dest, ch0, rot, cos, sin, gain):
        u = Stage("heads", name=name, run=add(run), N=N, dim=norm_dim, dest=dest, ch0=ch0, rot=rot, cos=cos, sin=sin,
                  gain=gain, h=norms_done())
        n = run.n
        u.takes(head_squares=n if norm_dim else 0, head_sums=n if norm_dim else 0, head_dev=n if norm_dim else 0,
                head_rstd=n if norm_dim else 0, head_normed=n, head_rotated=n, head_rope_a=n, head_done=n)
        return u

    def value_units(name, run, tiles, dest, after=None):
        add(run)
        return Stage("values", name=name, run=run, tiles=tiles, dest=dest, after=after, h=norms_done()).takes(v_done=run.n)

    def soft(items, scale, v, out, per, waits, swap=False):
        n = len(items)
        return Stage("soft", items=items, scale=scale, v=v, out=out, per=per, waits=waits, swap=swap).takes(
            s_scores=n, s_masked=n, s_max=n, s_neg=n, s_probs=n, s_sink=n, s_total=n, s_rcp=n, s_attn=n, s_turned=n,
            s_copied=n, s_chunk=n // per, s_hi=n // per, s_lo=n // per, s_swap=2 if swap else 0,
            s_swapped=2 if swap else 0)

    def plan_layer1():
        norm(BOTH, stages[-1].b["x_done"] + KC, mod=(1, 0))
        f = ffn(BOTH, pre_wi[1], pre_wo[1], (1, 2))
        norm(BOTH, f.b["x_done"] + KC, mod=(1, 1))
        head_units("gq", Run("gq", 4, KC, 2 * P, cols_of(b_w_qkv[0], 0, 2 * P)), SEQ, HD, "gq", 0, "rot_axial",
                   "cos_axial", "sin_axial", "b_q_gain")
        k = head_units("gk", Run("gk", 1, KC, 2 * P, cols_of(b_w_qkv[0], D, 2 * P)), BOTH, HD, "gk", 0, "rot_axial",
                       "cos_axial", "sin_axial", "b_k_gain")
        v = value_units("gv", Run("gv", 1, KC, 2 * P, cols_of(b_w_qkv[0], D + B_KV_HEADS * HD, 2 * P)), 4, "gv")
        items = []
        for h in range(B_Q_HEADS):
            kv, side = h // B_GROUP, h % 2
            half = slice(side * HD, (side + 1) * HD)
            kc = kv // 2 + (0 if kv % 2 == side else 2)
            for q in range(SEQ // P):
                items.append(dict(q=("gq", half, h // 2, q), k=("gk", half, kc, BOTH), mask=("band", q), sink=h,
                                  tiles=4, v=slice(kv * HD, (kv + 1) * HD), lanes=half))
        o = soft(items, HD ** -0.5, "gv", ("h", None), 4, [("head_done", k.b["head_done"] + 1), ("v_done", v.b["v_done"] + 1)],
                 swap=True)
        o = Stage("proj", run=add(Run("gwo", 4, KC, 2 * P, cols_of(b_w_o[0], 0, 2 * P))), N=SEQ, gate=(1, 5),
                  ready=("s_lo", o.b["s_lo"])).takes(x_done=KC)
        norm(SEQ, o.b["x_done"], mod=(1, 2))
        ffn(SEQ, post_wi[1], post_wo[1], (1, 8))

    def plan_second(l):
        w = w_in[l]
        prev = stages[-1]
        norm(SEQ, prev.b["x_done"] + (KC if prev.kind in ("ffn", "convffn") else 0), gain=f"g_mix{l}")
        head_units("aq", Run("aq", 2, KC, 2 * P, cols_of(w, OFF["aq"], 2 * P)), SEQ, P, "aq", 0, "rot_part128", "cos128",
                   "sin128", f"g_qa{l}")
        head_units("ak", Run("ak", 2, KC, 2 * P, cols_of(w, OFF["ak"], 2 * P)), SEQ, P, "ak", 0, "rot_part128", "cos128",
                   "sin128", f"g_ka{l}")
        v = value_units("av", Run("av", 2, KC, 2 * P, cols_of(w, OFF["av"], 2 * P)), 2, "av")
        head_units("iq", Run("iq", 1, KC, 2 * P, cols_of(w, OFF["iq"], 2 * P)), SEQ, None, "iq", 0, "rot_part64", "cos64",
                   "sin64", None)
        k = head_units("ik", Run("ik", 1, KC, P, lambda j: [
            (c, w.rearrange("(k p) m -> p k m", p=P)[:, :, OFF["ik"]:OFF["ik"] + HD]) for c in (0, HD)], 2), SEQ, HD, "ik", 0,
            "rot_part64", "cos64", "sin64", f"g_kidx{l}")
        iw = Stage("iw", run=add(Run("iw", 1, KC, HEADS2, cols_of(w, OFF["iw"], HEADS2))), h=norms_done()).takes(iw_done=1)
        sel = Stage("select", waits=[("head_done", k.b["head_done"] + 1), ("v_done", v.b["v_done"] + 2)], iw=iw)
        nt = SEQ // P
        sel.takes(idx_scores=nt * HEADS2, idx_relu=nt * HEADS2, idx_sum=nt * HEADS2, idx_causal=nt, top_steps=nt * 21,
                  sel_add=nt, sel_mask=nt)
        items = [dict(q=("aq", slice(0, P), h, q), k=("ak", slice(0, P), h, SEQ), mask=("sel", q), sink=None, tiles=2,
                      v=slice(h * P, (h + 1) * P), lanes=slice(0, P), needs=("sel_mask", sel.b["sel_mask"] + q + 1))
                 for h in range(HEADS2) for q in range(nt)]
        a = soft(items, P ** -0.5, "av", ("oa", None), nt, [("idx_relu", sel.b["idx_relu"] + nt * HEADS2)])
        done = {"oa": ("s_lo", a.b["s_lo"])}
        g = Stage("glu", run=add(Run("glu", 4, KC, 2 * P, two_of(w, OFF["glu"], w, OFF["glu"] + 512), 2)), l=l, h=norms_done())
        g.takes(glu_sig=4, glu_in=4, conv_pad=1, conv_steps=4 * CB_TAPS, ln_sum=1, ln_mean=1, ln_mid=4, ln_sq=4, ln_var=1,
                ln_dev=1, ln_rstd=1, ln_out=4, ln_act=4, ob_hi=4, ob_lo=4)
        done["ob"] = ("ob_lo", g.b["ob_lo"])
        c = Stage("cc", pair=add(Run("cc", 4, KC, 2 * P, two_of(w, OFF["cc"] + 512, w, OFF["cc"] + 1024), 2)),
                  run=add(Run("cb", 2, KC, 2 * P, cols_of(w, OFF["cc"], 2 * P))), l=l, h=norms_done())
        c.takes(cc_gate=4, cc_in=4, cc_pad=1, cc_steps=4 * CC_TAPS, cc_out=4, oc_hi=4, oc_lo=4)
        done["oc"] = ("oc_lo", c.b["oc_lo"])
        q = Stage("plain", run=add(Run("sq", 4, KC, 2 * P, cols_of(w, OFF["sb"], 2 * P))), h=norms_done()).takes(plain_done=4)
        v = value_units("sv", Run("sv", 2, KC, 2 * P, cols_of(w, OFF["sb"] + 1024, 2 * P)), 2, "sv",
                        after=("oc_lo", c.b["oc_lo"] + 4))
        t = Stage("stick", waits=[("plain_done", q.b["plain_done"] + 4), ("v_done", v.b["v_done"] + 2)])
        t.takes(**{n: HEADS2 for n in ("z_ready", "z_kept", "z_neg", "z_exp", "z_log", "z_soft", "z_soft_m", "z_sums", "z_arg",
                                       "z_arg_m", "z_attn", "z_out", "od_hi", "od_lo")})
        done["od"] = ("od_lo", t.b["od_lo"])
        for i, (name, wo) in enumerate((("oa", w_oa), ("ob", w_ob), ("oc", w_oc), ("od", w_od))):
            br = Stage("branch", i=i, l=l, name=name, gates=add(Run("gate", 4, KC, 2 * P, cols_of(
                w, OFF["gate"] + i * D, 2 * P))), run=add(Run("wo", 4, 4, 2 * P, cols_of(wo[l], 0, 2 * P, 0, 4))),
                ready=done[name], h=norms_done())
            br.takes(gate_done=4, gated=4, merged=4)
        m = Stage("merge").takes(m_hi=KC, m_lo=KC)
        o = Stage("proj", run=add(Run("merge", 4, KC, 2 * P, cols_of(w_merge[l], 0, 2 * P))), N=SEQ, gate=None,
                  ready=("m_lo", m.b["m_lo"])).takes(x_done=KC)
        norm(SEQ, o.b["x_done"], gain=f"g_ffn{l}")
        f = Stage("convffn", l=l, halves=[], h=norms_done())
        for hf in range(2):
            f.halves.append((add(Run("wi", HALF, KC, 2 * P, two_of(w_gate[l], hf * HALF * P, w_up[l], hf * HALF * P), 2)),
                             add(Run("wd", KC, HALF, P, cols_of(w_down[l], 0, P, hf * HALF, HALF)))))
        f.takes(cin_ready=FC, tap0=FC, tap1=FC, tap2=FC, silu_ready=FC, act_hi=FC, act_lo=FC, x_done=2 * KC, cin_pad=1)

    Stage("angles").takes(angle_step=4 * 8 + 3, angle_done=4)
    for layer in range(DEPTH):
        s = Stage("ada", layer=layer, run=add(Run("ada", MODC // 2, KC, 2 * P, cols_of(ada_w[layer], 0, 2 * P))))
        s.takes(mods_summed=MODC // 2, mods_ready=5)
    N = BOTH
    norm(N, None, mod=(0, 0))
    s = ffn(N, pre_wi[0], pre_wo[0], (0, 2))
    norm(N, s.b["x_done"] + KC, mod=(0, 1))

    head_units("dq", Run("dq", 4, KC, 2 * P, cols_of(a_w_qkv[0], 0, 2 * P)), N, HD, "qk", 0, "rot_axial",
               "cos_axial", "sin_axial", "a_q_gain")
    dk = head_units("dk", Run("dk", 4, KC, 2 * P, cols_of(a_w_qkv[0], D, 2 * P)), N, HD, "qk", KC, "rot_axial",
                    "cos_axial", "sin_axial", "a_k_gain")
    dv = value_units("dv", Run("dv", 4, KC, 2 * P, cols_of(a_w_qkv[0], 2 * D, 2 * P)), 4, "v")
    NI = A_HEADS * 4
    s = Stage("diff", dk=dk, dv=dv)
    s.takes(scores_ready=2 * NI, score_max=2 * NI, neg_max=NI, probs_ready=2 * NI, prob_sums=NI, prob_scales=NI,
            prob2_scaled=NI, attn_ready=NI, attn_turned=NI, turned_copied=NI, out_head=A_HEADS, out_kept=A_HEADS,
            lam_parts=3, out_squares=A_HEADS, out_sums=A_HEADS, out_dev=A_HEADS, out_rstd=A_HEADS, out_full=A_HEADS,
            out_hi=A_HEADS, out_lo=A_HEADS)
    o = Stage("proj", run=add(Run("dwo", 4, KC, 2 * P, cols_of(a_w_o[0], 0, 2 * P))), N=N, gate=(0, 5),
              ready=("out_lo", s.b["out_lo"])).takes(x_done=KC)
    norm(N, o.b["x_done"], mod=(0, 2))
    s = ffn(N, post_wi[0], post_wo[0], (0, 8))
    if stop != "layer0":
        plan_layer1()
    if stop not in ("layer0", "layer1"):
        for l in range(1 if stop == "second0" else DEPTH):
            plan_second(l)

    base = (nc.sbuf_base + 63) // 64 * 64
    at = [base]

    def place(name, cols, dt=F32, where=None):
        if where is None:
            where = at[0]
            at[0] += (cols * 4 + 63) // 64 * 64
        return nc.alloc_sbuf_tensor_at(name, [P, cols], dt, offset=where)

    raw = [place(f"raw{i}", SLOT) for i in range(RING)]
    w_hi = [place(f"w_hi{i}", SLOT, F32R) for i in range(RING)]
    w_lo = [place(f"w_lo{i}", SLOT, F32R) for i in range(RING)]
    xs = place("xs", KC * BOTH)[:, :].rearrange("p (c n) -> p c n", c=KC)
    h_hi = place("h_hi", KC * BOTH, F32R)[:, :].rearrange("p (c n) -> p c n", c=KC)
    h_lo = place("h_lo", KC * BOTH, F32R)[:, :].rearrange("p (c n) -> p c n", c=KC)
    vec_sb = place("vec_sb", N_VEC)
    con_sb = place("con_sb", N_CON)
    mod_sb = [place(f"mod_sb{i}", MODC * 2)[:, :].rearrange("p (c s) -> p c s", s=2) for i in range(DEPTH)]
    cond = place("cond", KC * 2)
    cond_hi = place("cond_hi", KC * 2, F32R)
    cond_lo = place("cond_lo", KC * 2, F32R)
    stats = place("stats", 64)
    angles = place("angles", 4 * SEQ)[:, :].rearrange("p (a n) -> p a n", a=4)
    arena = at[0]
    act_hi = place("act_hi", HALF * BOTH, F32R, arena)[:, :].rearrange("p (c n) -> p c n", c=HALF)
    act_lo = place("act_lo", HALF * BOTH, F32R, arena + HALF * BOTH * 4)[:, :].rearrange("p (c n) -> p c n", c=HALF)
    qk = place("qk", 2 * KC * BOTH, F32, arena)[:, :].rearrange("p (c n) -> p c n", c=2 * KC)
    v_lat = place("v_lat", 4 * D, F32, arena + 2 * KC * BOTH * 4)[:, :].rearrange("p (t c) -> p t c", t=4)
    at[0] += 2 * KC * BOTH * 4 + 4 * D * 4

    def over(name, at_kb, shape, dt=F32):
        n = 1
        for x in shape:
            n *= x
        t = place(name, n, dt, arena + int(at_kb * 1024))
        return t[:, :].rearrange("p (a n) -> p a n", a=shape[0]) if len(shape) == 2 else t

    gq, gk, gv = over("gq", 0, (KC, SEQ)), over("gk", 8, (4, BOTH)), over("gv", 16, (4, B_KV_HEADS * HD))
    aq, ak, av = over("aq", 0, (4, SEQ)), over("ak", 4, (4, SEQ)), over("av", 8, (2, 512))
    iq, ik, iw_sb = over("iq", 12, (2, SEQ)), over("ik", 14, (1, SEQ)), over("iw_sb", 15, (2, HEADS2))
    branch = {n: tuple(over(f"{n}_{half}", 16 + 8 * i + 4 * j, (4, SEQ), F32R) for j, half in enumerate(("hi", "lo")))
              for i, n in enumerate(("oa", "ob", "oc", "od"))}
    cb_in, cb_out = over("cb_in", 0, (4, SEQ + CB_TAPS - 1)), over("cb_out", 8, (4, SEQ))
    cc_in, cc_out = over("cc_in", 0, (4, SEQ + CC_TAPS - 1)), over("cc_out", 8, (4, SEQ))
    sqk, sv = over("sqk", 0, (8, SEQ)), over("sv", 8, (2, 512))
    gates, merged = over("gates", 0, (KC, SEQ)), over("merged", 8, (KC, SEQ))
    temp = at[0]
    TEMP = 20 * 1024
    sq = place("sq", 4 * BOTH, F32, temp)[:, :].rearrange("p (r n) -> p r n", r=4)
    scaled = place("scaled", 2 * BOTH, F32, temp + 8192)[:, :].rearrange("p (r n) -> p r n", r=2)
    full = place("full", 3 * BOTH, F32, temp + 12288)[:, :].rearrange("p (r n) -> p r n", r=3)
    rstd = place("rstd", BOTH, F32, temp + 18432)
    sil = place("sil", RING * BOTH, F32, temp)[:, :].rearrange("p (r n) -> p r n", r=RING)
    hr = place("hr", 4 * BOTH, F32, temp + 8192)[:, :].rearrange("p (r n) -> p r n", r=4)
    rope_t = place("rope_t", 2 * BOTH, F32, temp + 16384)[:, :].rearrange("p (r n) -> p r n", r=2)
    probs = place("probs", 4 * BOTH, F32, temp)[:, :].rearrange("p (r n) -> p r n", r=4)
    attn = place("attn", 2 * BOTH, F32, temp + 8192)[:, :].rearrange("p (r n) -> p r n", r=2)
    attn_t = place("attn_t", 2 * BOTH, F32, temp + 12288)[:, :].rearrange("p (r n) -> p r n", r=2)
    prob2 = place("prob2", BOTH, F32, temp + 16384)

    def tmp(name, at_kb, shape, dt=F32):
        n = 1
        for x in shape:
            n *= x
        t = place(name, n, dt, temp + int(at_kb * 1024))
        return t[:, :].rearrange("p (a n) -> p a n", a=shape[0])

    logits = tmp("logits", 16, (2, BOTH))
    rel = tmp("rel", 0, (HEADS2, SEQ))
    idx, idx_work, sel_gt = tmp("idx", 4, (2, SEQ)), tmp("idx_work", 6, (2, SEQ)), tmp("sel_gt", 8, (2, SEQ))
    sel_eq, sel_cum = tmp("sel_eq", 10, (2, SEQ)), tmp("sel_cum", 12, (2, SEQ))
    sel_mask = over("sel_mask", 24, (2, SEQ))
    ln_t = tmp("ln_t", 8, (4, SEQ))
    z_s, z_e, z_l, z_m, z_a = (tmp(f"z_{i}", 4 * i, (2, BOTH)) for i in range(5))
    tap_t = tmp("tap_t", 6, (RING, SEQ))
    cin = tmp("cin", 12, (RING, SEQ + CC_TAPS - 1))
    gated_t = tmp("gated_t", 0, (2, SEQ))
    ang = tmp("ang", 0, (8, SEQ))
    pos_i = tmp("pos_i", 8, (1, SEQ), I32)
    at[0] += TEMP
    assert at[0] <= nc.sbuf_usable_end, (at[0], nc.sbuf_usable_end)

    ps = [nc.alloc_psum_tensor(f"ps{i}", [P, 2, 512], F32) for i in range(RING)]
    pm = nc.alloc_psum_tensor("pm", [P, 2, 512], F32)
    bank = [ps[i // 2][:, i % 2, :] for i in range(6)]

    def vec(name, c=None):
        o, w = VEC[name]
        return vec_sb[:, o:o + w] if c is None else vec_sb[:, o + c:o + c + 1]

    ANGLES = ["cos128", "sin128", "cos64", "sin64"]

    def con(name):
        if name in ANGLES:
            return angles[:, ANGLES.index(name), :]
        o, w = CON[name]
        return con_sb[:, o:o + w]

    sems = {}

    def sem(name):
        if name not in sems:
            sems[name] = nc.alloc_semaphore(name)
        return sems[name]

    raw_landed = [sem(f"raw_landed{i}") for i in range(RING)]
    hi_ready, lo_ready = sem("hi_ready"), sem("lo_ready")
    unit_done, psum_free = sem("unit_done"), sem("psum_free")
    S = {name: sem(name) for name in counts}
    x_landed, vec_landed, out_stored = sem("x_landed"), sem("vec_landed"), sem("out_stored")
    cond_ready, cond_hi_ready, cond_lo_ready = sem("cond_ready"), sem("cond_hi_ready"), sem("cond_lo_ready")

    units = [r for r in runs for _ in range(r.n)]
    T = len(units)
    landed, per_slot = [], [0] * RING
    for t, r in enumerate(units):
        per_slot[t % RING] += 16 * r.dmas
        landed.append(per_slot[t % RING])

    def sweep(eng, run, body):
        head = RING
        turns = (run.n - head - 2) // RING
        if turns < 2:
            for j in range(run.n):
                body(Unit(run, run.t0 + j, j, run.t0 + j))
            return
        for j in range(head):
            body(Unit(run, run.t0 + j, j, run.t0 + j))
        with eng.Fori(0, turns) as turn:
            for r in range(RING):
                j = head + r
                body(Unit(run, run.t0 + j, turn * RING + j, turn * RING + (run.t0 + j), turn))
        for j in range(head + turns * RING, run.n):
            body(Unit(run, run.t0 + j, j, run.t0 + j))


    def weights(buf, run, k, m0, width):
        return buf[:, k * run.cols + m0:k * run.cols + m0 + width]

    def ahead(u, steps):
        rep = u.rep + steps
        if rep >= T:
            return None
        run = units[rep]
        assert u.turn is None or run is u.run
        return Unit(run, rep, u.j + steps, u.t + steps, u.turn)

    def dest_of(s, ch):
        return BUF[s.dest][:, s.ch0 + ch, :]

    BUF = dict(qk=qk, gq=gq, gk=gk, aq=aq, ak=ak, iq=iq, ik=ik)
    VALUES = dict(v=v_lat, gv=gv, av=av, sv=sv)

    def mask_of(item):
        kind, q = item["mask"]
        return sel_mask[:, q, :] if kind == "sel" else con("band")[:, q * SEQ:(q + 1) * SEQ]

    def out_of(s, chunk):
        hi, lo = (h_hi, h_lo) if s.out[0] == "h" else branch[s.out[0]]
        return hi[:, chunk, 0:SEQ], lo[:, chunk, 0:SEQ]

    def counts_before(stage, name):
        return stage.before[name]

    block = nc.Block()
    with block:
        @block.sync
        def _(sp):
            sp.dma_start(vec_sb[:, :], vecs[:, :]).then_inc(vec_landed, 16)
            sp.dma_start(con_sb[:, :], consts[:, :]).then_inc(vec_landed, 16)
            sp.dma_start(pos_i[:, 0, :], positions[:, :]).then_inc(vec_landed, 16)
            sp.dma_start(xs, x_t.rearrange("(c p) n -> p c n", p=P)).then_inc(x_landed, 16)

            def load(u):
                run = u.run
                if u.rep >= RING:
                    sp.wait_ge(lo_ready, u.t - (RING - 1))
                for c0, src in run.src(u.j):
                    dst = raw[u.slot][:, 0:run.kc * run.cols].rearrange("p (k m) -> p k m", k=run.kc)
                    dst = dst[:, :, c0:c0 + src.shape[2]]
                    sp.dma_start(dst, src).then_inc(raw_landed[u.slot], 16)

            for run in runs:
                sweep(sp, run, load)
            sp.wait_ge(S["x_done"], counts["x_done"])
            sp.dma_start(out.rearrange("(c p) n -> p c n", p=P), xs[:, :, 0:SEQ]).then_inc(out_stored, 16)
            sp.wait_ge(out_stored, 16)

        @block.tensor
        def _(pe):
            def open_unit(u):
                pe.wait_ge(lo_ready, u.t + 1)
                if u.rep >= RING:
                    pe.wait_ge(psum_free, u.t - (RING - 1))

            def dense(u, N, x_hi, x_lo, ready=None):
                run = u.run
                open_unit(u)
                for m in range(run.cols // P):
                    o = ps[u.slot][:, m, 0:N]
                    for k in range(run.kc):
                        if ready is not None and m == 0 and u.turn is None and u.j == 0:
                            pe.wait_ge(ready[0], ready[1] + k + 1)
                        hi = weights(w_hi[u.slot], run, k, m * P, P)
                        pe.matmul(o, hi, x_hi[:, k, 0:N], start=k == 0, stop=False)
                        pe.matmul(o, hi, x_lo[:, k, 0:N], start=False, stop=False)
                        last = pe.matmul(o, weights(w_lo[u.slot], run, k, m * P, P), x_hi[:, k, 0:N], start=False,
                                         stop=k == run.kc - 1)
                last.then_inc(unit_done, 1)

            def ada(s):
                pe.wait_ge(cond_lo_ready, 1)
                c_hi = cond_hi[:, :].rearrange("p (c s) -> p c s", s=2)
                c_lo = cond_lo[:, :].rearrange("p (c s) -> p c s", s=2)
                sweep(pe, s.run, lambda u: dense(u, 2, c_hi, c_lo))

            def norm(s):
                N, b = s.N, s.b
                pe.wait_ge(vec_landed, 48)
                for c in range(KC):
                    pe.wait_ge(S["squares_ready"], b["squares_ready"] + c + 1)
                    pe.matmul(pm[:, 0, 0:N], con("ones"), sq[:, c % 4, 0:N], start=c == 0,
                              stop=c == KC - 1).then_inc(S["square_summed"], 1)

            def ffn(s):
                for h, (wi, wo) in enumerate(s.halves):
                    sweep(pe, wi, lambda u: dense(u, s.N, h_hi, h_lo, (S["h_lo"], s.h)))
                    sweep(pe, wo, lambda u: dense(u, s.N, act_hi, act_lo, (S["act_lo"], s.b["act_lo"] + h * HALF)))

            def heads(s):
                run, N, b = s.run, s.N, s.b
                nm = run.cols // P
                for j in range(run.n + 2):
                    if j < run.n:
                        dense(Unit(run, run.t0 + j, j, run.t0 + j), N, h_hi, h_lo, (S["h_lo"], s.h))
                    if j >= 2:
                        i = j - 2
                        pe.wait_ge(S["head_normed"], b["head_normed"] + i + 1)
                        for m in range(nm):
                            last = pe.matmul(ps[(run.t0 + i) % RING][:, m, 0:SEQ], con(s.rot),
                                             dest_of(s, i * nm + m)[:, 0:SEQ], start=True, stop=True)
                        last.then_inc(S["head_rotated"], 1)
                    if s.dim and 1 <= j <= run.n:
                        i = j - 1
                        pe.wait_ge(S["head_squares"], b["head_squares"] + i + 1)
                        if i:
                            pe.wait_ge(S["head_dev"], b["head_dev"] + i)
                        ones = con("blocks" if s.dim == HD else "ones")
                        for m in range(nm):
                            last = pe.matmul(pm[:, m, 0:N], ones, sq[:, 2 * (i % 2) + m, 0:N], start=True, stop=True)
                        last.then_inc(S["head_sums"], 1)

            def values(s):
                run = s.run
                for j in range(run.n):
                    u = Unit(run, run.t0 + j, j, run.t0 + j)
                    open_unit(u)
                    for i in range(s.tiles):
                        o = ps[u.slot][:, i // 2, (i % 2) * run.cols:(i % 2 + 1) * run.cols]
                        tok = slice(i * P, (i + 1) * P)
                        for k in range(KC):
                            hi, lo = (weights(w[u.slot], run, k, 0, run.cols) for w in (w_hi, w_lo))
                            pe.matmul(o, h_hi[:, k, tok], hi, start=k == 0, stop=False)
                            pe.matmul(o, h_hi[:, k, tok], lo, start=False, stop=False)
                            last = pe.matmul(o, h_lo[:, k, tok], hi, start=False, stop=k == KC - 1)
                    last.then_inc(unit_done, 1)

            def diff(s):
                b = s.b
                pe.wait_ge(S["head_done"], s.dk.b["head_done"] + s.dk.run.n)
                pe.wait_ge(S["v_done"], s.dv.b["v_done"] + s.dv.run.n)

                def keys(qt):
                    return slice(0, BOTH) if qt < 2 else slice(SEQ, BOTH)

                def scores(i):
                    h, qt = divmod(i, 4)
                    if i >= 2:
                        pe.wait_ge(S["probs_ready"], b["probs_ready"] + 2 * (i - 1))
                    for c in range(2):
                        half = slice(c * HD, (c + 1) * HD)
                        n = keys(qt).stop - keys(qt).start
                        pe.matmul(bank[2 * (i % 2) + c][:, 0:n], qk[half, h, qt * P:(qt + 1) * P],
                                  qk[half, KC + h, keys(qt)], start=True, stop=True).then_inc(S["scores_ready"], 1)

                def turn(i):
                    n = 4 if i % 4 < 2 else 2
                    pe.wait_ge(S["attn_ready"], b["attn_ready"] + i + 1)
                    if i:
                        pe.wait_ge(S["turned_copied"], b["turned_copied"] + i)
                    for k in range(n):
                        last = pe.transpose(bank[4][:, k * P:(k + 1) * P], attn[:, i % 2, k * P:(k + 1) * P], con("ident"))
                    last.then_inc(S["attn_turned"], 1)

                def weigh(i):
                    h, qt = divmod(i, 4)
                    pe.wait_ge(S["turned_copied"], b["turned_copied"] + i + 1)
                    if qt == 0 and h >= 2:
                        pe.wait_ge(S["out_kept"], b["out_kept"] + h - 1)
                    tiles = range(4) if qt < 2 else range(2, 4)
                    for n, k in enumerate(tiles):
                        last = pe.matmul(pm[:, h % 2, qt * P:(qt + 1) * P], v_lat[:, k, h * P:(h + 1) * P],
                                         attn_t[:, i % 2, n * P:(n + 1) * P], start=n == 0, stop=n == len(tiles) - 1)
                    if qt == 3:
                        last.then_inc(S["out_head"], 1)

                scores(0)
                scores(1)
                for i in range(NI):
                    turn(i)
                    if i:
                        weigh(i - 1)
                    if i + 2 < NI:
                        scores(i + 2)
                weigh(NI - 1)
                for h in range(A_HEADS):
                    pe.wait_ge(S["out_squares"], b["out_squares"] + h + 1)
                    if h >= 2:
                        pe.wait_ge(S["out_dev"], b["out_dev"] + h - 1)
                    pe.matmul(bank[h % 2], con("ones"), sq[:, h % 4, :], start=True, stop=True).then_inc(S["out_sums"], 1)

            def proj(s):
                sweep(pe, s.run, lambda u: dense(u, s.N, h_hi, h_lo, (S[s.ready[0]], s.ready[1])))

            def soft(s):
                b, items = s.b, s.items
                n = len(items)
                for name, count in s.waits:
                    pe.wait_ge(S[name], count)
                if s.swap:
                    for c in range(2):
                        pe.matmul(bank[c], con("swap"), gk[:, c, :], start=True, stop=True).then_inc(S["s_swap"], 1)
                    pe.wait_ge(S["s_swapped"], b["s_swapped"] + 2)

                def scores(i):
                    it = items[i]
                    (qb, lanes, qc, q), (kb, _, kc, nk) = it["q"], it["k"]
                    if i >= 4:
                        pe.wait_ge(S["s_masked"], b["s_masked"] + i - 3)
                    pe.matmul(bank[i % 4][:, 0:nk], BUF[qb][lanes, qc, q * P:(q + 1) * P], BUF[kb][lanes, kc, 0:nk],
                              start=True, stop=True).then_inc(S["s_scores"], 1)

                def turn(i):
                    pe.wait_ge(S["s_attn"], b["s_attn"] + i + 1)
                    if i >= 2:
                        pe.wait_ge(S["s_copied"], b["s_copied"] + i - 1)
                    for k in range(items[i]["tiles"]):
                        last = pe.transpose(bank[4 + i % 2][:, k * P:(k + 1) * P], attn[:, i % 2, k * P:(k + 1) * P],
                                            con("ident"))
                    last.then_inc(S["s_turned"], 1)

                def weigh(i):
                    it = items[i]
                    q = it["q"][3]
                    chunk = i // s.per
                    pe.wait_ge(S["s_copied"], b["s_copied"] + i + 1)
                    if i % s.per == 0 and chunk >= 2:
                        pe.wait_ge(S["s_lo"], b["s_lo"] + chunk - 1)
                    for k in range(it["tiles"]):
                        last = pe.matmul(pm[it["lanes"], chunk % 2, q * P:(q + 1) * P], VALUES[s.v][:, k, it["v"]],
                                         attn_t[:, i % 2, k * P:(k + 1) * P], start=k == 0, stop=k == it["tiles"] - 1)
                    if i % s.per == s.per - 1:
                        last.then_inc(S["s_chunk"], 1)

                for i in range(min(3, n)):
                    scores(i)
                for i in range(n):
                    turn(i)
                    if i:
                        weigh(i - 1)
                    if i + 3 < n:
                        scores(i + 3)
                weigh(n - 1)

            def iw(s):
                u = Unit(s.run, s.run.t0, 0, s.run.t0)
                open_unit(u)
                for i in range(2):
                    o = ps[u.slot][:, 0, i * HEADS2:(i + 1) * HEADS2]
                    tok = slice(i * P, (i + 1) * P)
                    for k in range(KC):
                        hi, lo = (weights(w[u.slot], s.run, k, 0, HEADS2) for w in (w_hi, w_lo))
                        pe.matmul(o, h_hi[:, k, tok], hi, start=k == 0, stop=False)
                        pe.matmul(o, h_hi[:, k, tok], lo, start=False, stop=False)
                        last = pe.matmul(o, h_lo[:, k, tok], hi, start=False, stop=k == KC - 1)
                last.then_inc(unit_done, 1)

            def select(s):
                b = s.b
                for name, count in s.waits:
                    pe.wait_ge(S[name], count)
                pe.wait_ge(S["iw_done"], s.iw.b["iw_done"] + 1)
                for q in range(2):
                    for h in range(HEADS2):
                        half = slice(h % 2 * HD, (h % 2 + 1) * HD)
                        if q:
                            pe.wait_ge(S["idx_relu"], b["idx_relu"] + h + 1)
                        pe.matmul(bank[h][:, 0:SEQ], iq[half, h // 2, q * P:(q + 1) * P], ik[half, 0, :], start=True,
                                  stop=True).then_inc(S["idx_scores"], 1)

            def glu(s):
                b = s.b
                sweep(pe, s.run, lambda u: dense(u, SEQ, h_hi, h_lo))
                pe.wait_ge(S["conv_steps"], b["conv_steps"] + 4 * CB_TAPS)
                for c in range(4):
                    last = pe.matmul(pm[:, 0, 0:SEQ], con("ones"), cb_out[:, c, :], start=c == 0, stop=c == 3)
                last.then_inc(S["ln_sum"], 1)
                for c in range(4):
                    pe.wait_ge(S["ln_sq"], b["ln_sq"] + c + 1)
                    last = pe.matmul(pm[:, 1, 0:SEQ], con("ones"), ln_t[:, c, :], start=c == 0, stop=c == 3)
                last.then_inc(S["ln_var"], 1)

            def cc(s):
                sweep(pe, s.pair, lambda u: dense(u, SEQ, h_hi, h_lo))
                sweep(pe, s.run, lambda u: dense(u, SEQ, h_hi, h_lo))

            def plain(s):
                sweep(pe, s.run, lambda u: dense(u, SEQ, h_hi, h_lo))

            def stick(s):
                b = s.b
                for name, count in s.waits:
                    pe.wait_ge(S[name], count)

                def scores(h):
                    if h >= 2:
                        pe.wait_ge(S["z_kept"], b["z_kept"] + h - 1)
                    for k in range(2):
                        last = pe.matmul(bank[h % 2][:, k * SEQ:(k + 1) * SEQ], sqk[:, 4 + h, k * P:(k + 1) * P], sqk[:, h, :],
                                         start=True, stop=True)
                    last.then_inc(S["z_ready"], 1)

                def sums(h):
                    pe.wait_ge(S["z_soft_m"], b["z_soft_m"] + h + 1)
                    if h >= 2:
                        pe.wait_ge(S["z_arg"], b["z_arg"] + h - 1)
                    m = z_m[:, h % 2, :]
                    o = bank[2 + h % 2]
                    pe.matmul(o[:, 0:SEQ], con("suffix"), m[:, 0:SEQ], start=True, stop=False)
                    pe.matmul(o[:, 0:SEQ], con("ones"), m[:, SEQ:], start=False, stop=True)
                    pe.matmul(o[:, SEQ:], con("suffix"), m[:, SEQ:], start=True, stop=True).then_inc(S["z_sums"], 1)

                def weigh(h):
                    pe.wait_ge(S["z_attn"], b["z_attn"] + h + 1)
                    if h >= 2:
                        pe.wait_ge(S["od_lo"], b["od_lo"] + h - 1)
                    for k in range(2):
                        last = pe.matmul(pm[:, h % 2, 0:SEQ], sv[:, k, h * P:(h + 1) * P], z_a[:, h % 2, k * SEQ:(k + 1) * SEQ],
                                         start=k == 0, stop=k == 1)
                    last.then_inc(S["z_out"], 1)

                scores(0)
                for h in range(HEADS2):
                    if h + 1 < HEADS2:
                        scores(h + 1)
                    sums(h)
                    if h:
                        weigh(h - 1)
                weigh(HEADS2 - 1)

            def branches(s):
                sweep(pe, s.gates, lambda u: dense(u, SEQ, h_hi, h_lo))
                hi, lo = branch[s.name]
                pe.wait_ge(S[s.ready[0]], s.ready[1] + 4)
                sweep(pe, s.run, lambda u: dense(u, SEQ, hi, lo))

            def convffn(s):
                for h, (wi, wd) in enumerate(s.halves):
                    sweep(pe, wi, lambda u: dense(u, SEQ, h_hi, h_lo, (S["h_lo"], s.h)))
                    sweep(pe, wd, lambda u: dense(u, SEQ, act_hi, act_lo, (S["act_lo"], s.b["act_lo"] + h * HALF)))

            todo = dict(ada=ada, norm=norm, ffn=ffn, heads=heads, values=values, diff=diff, proj=proj, soft=soft, iw=iw,
                        select=select, glu=glu, cc=cc, plain=plain, stick=stick, branch=branches, convffn=convffn)
            for s in stages:
                if s.kind in todo:
                    todo[s.kind](s)

        @block.scalar
        def _(act):
            def split(u):
                if u is None:
                    return
                n = u.run.kc * u.run.cols
                at_landed = landed[u.rep]
                if u.turn is not None:
                    at_landed = u.turn * (16 * u.run.dmas) + at_landed
                act.wait_ge(raw_landed[u.slot], at_landed)
                if u.rep >= RING:
                    act.wait_ge(unit_done, u.t - (RING - 1))
                nc.scalar.copy(w_hi[u.slot][:, 0:n], raw[u.slot][:, 0:n]).then_inc(hi_ready, 1)

            def ada(s):
                if s.layer == 0:
                    act.wait_ge(vec_landed, 48)
                    nc.scalar.activation(cond[:, :], vec("cond"), ACT.Silu).then_inc(cond_ready, 1)
                    act.wait_ge(cond_ready, 1)
                    nc.scalar.copy(cond_hi[:, :], cond[:, :]).then_inc(cond_hi_ready, 1)
                    split(Unit(units[0], 0, 0, 0))
                    split(Unit(units[1], 1, 1, 1))
                sweep(act, s.run, lambda u: split(ahead(u, 2)))

            def norm(s):
                N, b = s.N, s.b
                if s.x_at is None:
                    act.wait_ge(x_landed, 16)
                for c in range(KC):
                    if s.x_at is not None:
                        act.wait_ge(S["x_done"], s.x_at + c + 1)
                    if c >= 4:
                        act.wait_ge(S["square_summed"], b["square_summed"] + c - 3)
                    nc.scalar.activation(sq[:, c % 4, 0:N], xs[:, c, 0:N], ACT.Square).then_inc(S["squares_ready"], 1)
                act.wait_ge(S["square_summed"], b["square_summed"] + KC)
                nc.scalar.activation(rstd[:, 0:N], pm[:, 0, 0:N], ACT.Sqrt, bias=con("eps"),
                                     scale=1.0 / D).then_inc(S["deviation_ready"], 1)
                for c in range(KC):
                    act.wait_ge(S["scaled_ready"], b["scaled_ready"] + c + 1)
                    if c >= 3:
                        act.wait_ge(S["h_lo"], b["h_lo"] + c - 2)
                    if s.gain is not None:
                        nc.scalar.activation(full[:, c % 3, 0:N], scaled[:, c % 2, 0:N], ACT.Copy,
                                             scale=vec(s.gain, c)).then_inc(S["h_full"], 1)
                        continue
                    layer, which = s.mod
                    act.wait_ge(S["mods_ready"], 5 * (layer + 1))
                    for st in range(N // SEQ):
                        tok = slice(st * SEQ, (st + 1) * SEQ)
                        last = nc.scalar.activation(
                            full[:, c % 3, tok], scaled[:, c % 2, tok], ACT.Identity,
                            bias=mod_sb[layer][:, 3 * which * KC + c, st:st + 1],
                            scale=mod_sb[layer][:, (3 * which + 1) * KC + c, st:st + 1])
                    last.then_inc(S["h_full"], 1)

            def ffn(s):
                N, b = s.N, s.b
                for h, (wi, wo) in enumerate(s.halves):
                    f0 = b["silu_ready"] + h * HALF

                    def gated(u):
                        split(ahead(u, 2))
                        act.wait_ge(unit_done, u.t + 1)
                        if u.j0 >= RING or u.turn is not None:
                            act.wait_ge(S["act_lo"], u.j + (b["act_lo"] + h * HALF - (RING - 1)))
                        nc.scalar.activation(sil[:, u.j0 % RING, 0:N], ps[u.slot][:, 0, 0:N],
                                             ACT.Silu).then_inc(S["silu_ready"], 1)

                    sweep(act, wi, gated)
                    sweep(act, wo, lambda u: split(ahead(u, 2)))

            def heads(s):
                run, N, b = s.run, s.N, s.b
                nm = run.cols // P
                for j in range(run.n + 1):
                    if j < run.n:
                        u = Unit(run, run.t0 + j, j, run.t0 + j)
                        split(ahead(u, 2))
                        if s.dim:
                            act.wait_ge(unit_done, u.t + 1)
                            if j >= 2:
                                act.wait_ge(S["head_sums"], b["head_sums"] + j - 1)
                            for m in range(nm):
                                last = nc.scalar.activation(sq[:, 2 * (j % 2) + m, 0:N], ps[u.slot][:, m, 0:N], ACT.Square)
                            last.then_inc(S["head_squares"], 1)
                    if s.dim and j:
                        i = j - 1
                        act.wait_ge(S["head_sums"], b["head_sums"] + i + 1)
                        if i >= 2:
                            act.wait_ge(S["head_normed"], b["head_normed"] + i - 1)
                        for m in range(nm):
                            last = nc.scalar.activation(hr[:, 2 * (i % 2) + m, 0:N], pm[:, m, 0:N], ACT.Sqrt,
                                                        bias=con("eps"), scale=1.0 / s.dim)
                        last.then_inc(S["head_dev"], 1)

            def values(s):
                run = s.run
                for j in range(run.n):
                    u = Unit(run, run.t0 + j, j, run.t0 + j)
                    split(ahead(u, 2))
                    if j == 0 and s.after is not None:
                        act.wait_ge(S[s.after[0]], s.after[1])
                    act.wait_ge(unit_done, u.t + 1)
                    for i in range(s.tiles // 2):
                        last = nc.scalar.copy(VALUES[s.dest][:, 2 * i:2 * i + 2, j * run.cols:(j + 1) * run.cols],
                                              ps[u.slot][:, i, :].rearrange("p (t c) -> p t c", t=2))
                    last.then_inc(S["v_done"], 1)

            def diff(s):
                b = s.b
                act.wait_ge(S["lam_parts"], b["lam_parts"] + 1)
                nc.scalar.activation(stats[:, 2:4], stats[:, 0:2], ACT.Exp).then_inc(S["lam_parts"], 1)
                for i in range(NI):
                    n = BOTH if i % 4 < 2 else CTX
                    act.wait_ge(S["neg_max"], b["neg_max"] + i + 1)
                    if i >= 2:
                        act.wait_ge(S["attn_ready"], b["attn_ready"] + i - 1)
                    for c in range(2):
                        r = 2 * (i % 2) + c
                        nc.scalar.activation(probs[:, r, 0:n], bank[r][:, 0:n], ACT.Exp, bias=stats[:, 16 + r:17 + r],
                                             scale=HD ** -0.5, accum_out=stats[:, 20 + r:21 + r]).then_inc(S["probs_ready"], 1)
                    if i:
                        turned(s, i - 1)
                turned(s, NI - 1)
                for step in range(A_HEADS + 2):
                    if step < A_HEADS:
                        h = step
                        if h >= 4:
                            act.wait_ge(S["out_sums"], b["out_sums"] + h - 3)
                        nc.scalar.activation(sq[:, h % 4, :], qk[:, h, :], ACT.Square).then_inc(S["out_squares"], 1)
                    if step >= 2:
                        h = step - 2
                        act.wait_ge(S["out_sums"], b["out_sums"] + h + 1)
                        if h >= 2:
                            act.wait_ge(S["out_full"], b["out_full"] + h - 1)
                        nc.scalar.activation(scaled[:, h % 2, :], bank[h % 2], ACT.Sqrt, bias=con("eps"),
                                             scale=1.0 / P).then_inc(S["out_dev"], 1)

            def turned(s, i):
                b = s.b
                n = BOTH if i % 4 < 2 else CTX
                act.wait_ge(S["attn_turned"], b["attn_turned"] + i + 1)
                nc.scalar.copy(attn_t[:, i % 2, 0:n], bank[4][:, 0:n]).then_inc(S["turned_copied"], 1)
                if i % 4 == 3:
                    pass
                if i % 4 == 0 and i >= 4:
                    kept(s, i // 4 - 1)
                if i == NI - 1:
                    kept(s, A_HEADS - 1)

            def kept(s, h):
                act.wait_ge(S["out_head"], s.b["out_head"] + h + 1)
                nc.scalar.copy(qk[:, h, :], pm[:, h % 2, :]).then_inc(S["out_kept"], 1)
                if h == A_HEADS - 1:
                    act.wait_ge(S["out_kept"], s.b["out_kept"] + A_HEADS)

            def proj(s):
                sweep(act, s.run, lambda u: split(ahead(u, 2)))

            def angles_(s):
                for i in range(4):
                    act.wait_ge(S["angle_step"], 3 + 8 * (i + 1))
                    nc.scalar.activation(angles[:, i, :], ang[:, 2 + i, :], ACT.Sin).then_inc(S["angle_done"], 1)

            def soft(s):
                b, n = s.b, len(s.items)
                for i in range(n):
                    it = s.items[i]
                    nk = it["k"][3]
                    act.wait_ge(S["s_neg"], b["s_neg"] + i + 1)
                    if i >= 2:
                        act.wait_ge(S["s_attn"], b["s_attn"] + i - 1)
                    nc.scalar.activation(probs[:, i % 2, 0:nk], logits[:, i % 2, 0:nk], ACT.Exp, bias=stats[:, 10 + i % 2:11 + i % 2],
                                         accum_out=stats[:, 12 + i % 2:13 + i % 2]).then_inc(S["s_probs"], 1)
                    if it["sink"] is not None:
                        nc.scalar.activation(stats[:, 14 + i % 2:15 + i % 2], vec("sink", it["sink"]), ACT.Exp,
                                             bias=stats[:, 10 + i % 2:11 + i % 2]).then_inc(S["s_sink"], 1)
                    if i:
                        copied(s, i - 1)
                copied(s, n - 1)

            def copied(s, i):
                b = s.b
                nk = s.items[i]["k"][3]
                act.wait_ge(S["s_turned"], b["s_turned"] + i + 1)
                if i >= 2:
                    pass
                nc.scalar.copy(attn_t[:, i % 2, 0:nk], bank[4 + i % 2][:, 0:nk]).then_inc(S["s_copied"], 1)

            def iw(s):
                u = Unit(s.run, s.run.t0, 0, s.run.t0)
                split(ahead(u, 2))
                act.wait_ge(unit_done, u.t + 1)
                nc.scalar.copy(iw_sb, ps[u.slot][:, 0, 0:2 * HEADS2].rearrange("p (t h) -> p t h", t=2)).then_inc(S["iw_done"], 1)

            def select(s):
                b = s.b
                for q in range(2):
                    for h in range(HEADS2):
                        i = q * HEADS2 + h
                        act.wait_ge(S["idx_scores"], b["idx_scores"] + i + 1)
                        if q:
                            act.wait_ge(S["idx_sum"], b["idx_sum"] + h + 1)
                        nc.scalar.activation(rel[:, h, :], bank[h][:, 0:SEQ], ACT.Relu,
                                             scale=(HD * HEADS2) ** -0.5).then_inc(S["idx_relu"], 1)

            def glu(s):
                b = s.b

                def gate(u):
                    split(ahead(u, 2))
                    act.wait_ge(unit_done, u.t + 1)
                    if u.j >= RING:
                        act.wait_ge(S["glu_in"], b["glu_in"] + u.j - RING + 1)
                    nc.scalar.activation(sil[:, u.j % RING, 0:SEQ], ps[u.slot][:, 1, 0:SEQ], ACT.Sigmoid).then_inc(S["glu_sig"], 1)

                sweep(act, s.run, gate)
                for c in range(4):
                    act.wait_ge(S["ln_mid"], b["ln_mid"] + c + 1)
                    nc.scalar.activation(ln_t[:, c, :], cb_out[:, c, :], ACT.Square).then_inc(S["ln_sq"], 1)
                act.wait_ge(S["ln_var"], b["ln_var"] + 1)
                nc.scalar.activation(rstd[:, 0:SEQ], pm[:, 1, 0:SEQ], ACT.Sqrt, bias=con("eps"),
                                     scale=1.0 / 512).then_inc(S["ln_dev"], 1)
                for c in range(4):
                    act.wait_ge(S["ln_out"], b["ln_out"] + c + 1)
                    nc.scalar.activation(ln_t[:, c, :], cb_out[:, c, :], ACT.Silu, bias=vec(f"ln_b{s.l}", c),
                                         scale=vec(f"ln_g{s.l}", c)).then_inc(S["ln_act"], 1)

            def cc(s):
                b = s.b

                def keep(u):
                    split(ahead(u, 2))
                    act.wait_ge(unit_done, u.t + 1)
                    if u.j >= RING:
                        act.wait_ge(S["cc_in"], b["cc_in"] + u.j - RING + 1)
                    nc.scalar.copy(sil[:, u.j % RING, 0:SEQ], ps[u.slot][:, 0, 0:SEQ]).then_inc(S["cc_gate"], 1)

                sweep(act, s.pair, keep)
                sweep(act, s.run, lambda u: split(ahead(u, 2)))

            def plain(s):
                def keep(u):
                    split(ahead(u, 2))
                    act.wait_ge(unit_done, u.t + 1)
                    nc.scalar.copy(sqk[:, 2 * u.j:2 * u.j + 2, :], ps[u.slot][:, :, 0:SEQ]).then_inc(S["plain_done"], 1)

                sweep(act, s.run, keep)

            def stick(s):
                b = s.b

                def softplus(h):
                    r = h % 2
                    act.wait_ge(S["z_ready"], b["z_ready"] + h + 1)
                    if h >= 2:
                        act.wait_ge(S["z_arg"], b["z_arg"] + h - 1)
                    nc.scalar.activation(z_s[:, r, :], bank[r], ACT.Copy, scale=P ** -0.5).then_inc(S["z_kept"], 1)
                    act.wait_ge(S["z_neg"], b["z_neg"] + h + 1)
                    nc.scalar.activation(z_e[:, r, :], z_e[:, r, :], ACT.Exp).then_inc(S["z_exp"], 1)
                    act.wait_ge(S["z_exp"], b["z_exp"] + h + 1)
                    if h >= 2:
                        act.wait_ge(S["z_soft"], b["z_soft"] + h - 1)
                    nc.scalar.activation(z_l[:, r, :], z_e[:, r, :], ACT.Ln, bias=1.0).then_inc(S["z_log"], 1)

                def weights_(h):
                    act.wait_ge(S["z_arg_m"], b["z_arg_m"] + h + 1)
                    if h >= 2:
                        act.wait_ge(S["z_out"], b["z_out"] + h - 1)
                    nc.scalar.activation(z_a[:, h % 2, :], z_e[:, h % 2, :], ACT.Exp).then_inc(S["z_attn"], 1)

                for h in range(HEADS2):
                    softplus(h)
                    if h:
                        weights_(h - 1)
                weights_(HEADS2 - 1)

            def branches(s):
                b = s.b

                def gate(u):
                    split(ahead(u, 2))
                    act.wait_ge(unit_done, u.t + 1)
                    if s.i:
                        act.wait_ge(S["gated"], b["gated"] - 4 + u.j + 1)
                    for m in range(2):
                        c = 2 * u.j + m
                        last = nc.scalar.activation(gates[:, c, :], ps[u.slot][:, m, 0:SEQ], ACT.Sigmoid,
                                                    bias=vec(f"b_gate{s.l}", s.i * KC + c))
                    last.then_inc(S["gate_done"], 1)

                sweep(act, s.gates, gate)
                sweep(act, s.run, lambda u: split(ahead(u, 2)))

            def convffn(s):
                b = s.b
                for h, (wi, wd) in enumerate(s.halves):
                    def keep(u):
                        split(ahead(u, 2))
                        act.wait_ge(unit_done, u.t + 1)
                        if u.j0 >= RING or u.turn is not None:
                            act.wait_ge(S["tap2"], u.j + (b["tap2"] + h * HALF - (RING - 1)))
                        r = u.j0 % RING
                        nc.scalar.copy(cin[:, r, CC_TAPS - 1:], ps[u.slot][:, 0, 0:SEQ]).then_inc(S["cin_ready"], 1)
                        act.wait_ge(S["tap2"], u.j + (b["tap2"] + h * HALF + 1))
                        if u.j0 >= RING or u.turn is not None:
                            act.wait_ge(S["act_lo"], u.j + (b["act_lo"] + h * HALF - (RING - 1)))
                        nc.scalar.activation(sil[:, r, 0:SEQ], tap_t[:, r, :], ACT.Silu).then_inc(S["silu_ready"], 1)

                    sweep(act, wi, keep)
                    sweep(act, wd, lambda u: split(ahead(u, 2)))

            todo = dict(ada=ada, norm=norm, ffn=ffn, heads=heads, values=values, diff=diff, proj=proj, angles=angles_, soft=soft,
                        iw=iw, select=select, glu=glu, cc=cc, plain=plain, stick=stick, branch=branches, convffn=convffn)
            for s in stages:
                if s.kind in todo:
                    todo[s.kind](s)

        @block.vector
        def _(dve):
            def split(u):
                if u is None:
                    return
                n = u.run.kc * u.run.cols
                dve.wait_ge(hi_ready, u.t + 1)
                nc.vector.tensor_tensor(w_lo[u.slot][:, 0:n], raw[u.slot][:, 0:n], w_hi[u.slot][:, 0:n].bitcast(F32),
                                        ALU.subtract).then_inc(lo_ready, 1)

            def ada(s):
                mod, bias = mod_sb[s.layer], vec(f"ada_b{s.layer}").rearrange("p (c s) -> p c s", s=2)
                if s.layer == 0:
                    dve.wait_ge(cond_hi_ready, 1)
                    nc.vector.tensor_tensor(cond_lo[:, :], cond[:, :], cond_hi[:, :].bitcast(F32),
                                            ALU.subtract).then_inc(cond_lo_ready, 1)
                    split(Unit(units[0], 0, 0, 0))
                    split(Unit(units[1], 1, 1, 1))

                def evict(u):
                    split(ahead(u, 2))
                    dve.wait_ge(unit_done, u.t + 1)
                    nc.vector.tensor_tensor(mod[:, bass.ds(u.j * 2, 2), :], ps[u.slot][:, :, 0:2],
                                            bias[:, bass.ds(u.j * 2, 2), :], ALU.add).then_inc(psum_free, 1)

                sweep(dve, s.run, evict)
                dve.wait_ge(psum_free, s.run.t0 + s.run.n)
                for which in (1, 4, 7):
                    part = mod[:, which * KC:(which + 1) * KC, :]
                    nc.vector.tensor_scalar(part, part, 1.0, None, ALU.add).then_inc(S["mods_ready"], 1)
                for which in (2, 8):
                    part = mod[:, which * KC:(which + 1) * KC, :]
                    nc.vector.tensor_scalar(part, part, 0.5, None, ALU.mult).then_inc(S["mods_ready"], 1)

            def norm(s):
                N, b = s.N, s.b
                dve.wait_ge(S["deviation_ready"], b["deviation_ready"] + 1)
                nc.vector.reciprocal(rstd[:, 0:N], rstd[:, 0:N]).then_inc(S["rstd_ready"], 1)
                dve.wait_ge(S["rstd_ready"], b["rstd_ready"] + 1)
                for c in range(KC + 1):
                    if c < KC:
                        if c >= 2:
                            dve.wait_ge(S["h_full"], b["h_full"] + c - 1)
                        nc.vector.tensor_tensor(scaled[:, c % 2, 0:N], xs[:, c, 0:N], rstd[:, 0:N],
                                                ALU.mult).then_inc(S["scaled_ready"], 1)
                    if c:
                        i = c - 1
                        dve.wait_ge(S["h_full"], b["h_full"] + i + 1)
                        nc.vector.tensor_copy(h_hi[:, i, 0:N], full[:, i % 3, 0:N]).then_inc(S["h_hi"], 1)

            def residual(u, s, gate, x0, m_of):
                split(ahead(u, 2))
                dve.wait_ge(unit_done, u.t + 1)
                for m in range(u.run.cols // P):
                    c = m_of(u, m)
                    if gate is None:
                        xc = xs[:, bass.ds(c, 1), 0:SEQ].rearrange("p c n -> p (c n)")
                        nc.vector.tensor_tensor(xc, ps[u.slot][:, m, 0:SEQ], xc, ALU.add).then_inc(S["x_done"], 1)
                        continue
                    layer, which = gate
                    for st in range(s.N // SEQ):
                        tok = slice(st * SEQ, (st + 1) * SEQ)
                        xc = xs[:, bass.ds(c, 1), tok].rearrange("p c n -> p (c n)")
                        g = mod_sb[layer][:, bass.ds(c + which * KC, 1), st:st + 1].rearrange("p c n -> p (c n)")
                        last = nc.vector.scalar_tensor_tensor(xc, ps[u.slot][:, m, tok], g, xc, ALU.mult, ALU.add)
                    last.then_inc(S["x_done"], 1)
                dve.wait_ge(S["x_done"], x0 + (u.j + 1) * (u.run.cols // P))
                dve.sem_inc(psum_free, 1)

            def ffn(s):
                N, b = s.N, s.b
                for h, (wi, wo) in enumerate(s.halves):
                    f0 = h * HALF

                    def gated(u):
                        split(ahead(u, 2))
                        r = u.j0 % RING
                        dve.wait_ge(S["silu_ready"], u.j + (b["silu_ready"] + f0 + 1))
                        nc.vector.tensor_tensor(sil[:, r, 0:N], sil[:, r, 0:N], ps[u.slot][:, 1, 0:N],
                                                ALU.mult).then_inc(psum_free, 1)
                        dve.wait_ge(psum_free, u.t + 1)
                        nc.vector.tensor_copy(act_hi[:, bass.ds(u.j, 1), 0:N].rearrange("p c n -> p (c n)"),
                                              sil[:, r, 0:N]).then_inc(S["act_hi"], 1)

                    sweep(dve, wi, gated)
                    sweep(dve, wo, lambda u: residual(u, s, s.gate, b["x_done"] + h * KC, lambda u, m: u.j))

            def heads(s):
                run, N, b = s.run, s.N, s.b
                nm = run.cols // P
                for j in range(run.n + 2):
                    if j < run.n:
                        split(ahead(Unit(run, run.t0 + j, j, run.t0 + j), 2))
                    if 1 <= j <= run.n:
                        i = j - 1
                        if not s.dim:
                            dve.wait_ge(unit_done, run.t0 + i + 1)
                        if s.dim:
                            dve.wait_ge(S["head_dev"], b["head_dev"] + i + 1)
                            r = hr[:, 2 * (i % 2):2 * (i % 2) + nm, 0:N]
                            nc.vector.reciprocal(r, r).then_inc(S["head_rstd"], 1)
                            dve.wait_ge(S["head_rstd"], b["head_rstd"] + i + 1)
                        for m in range(nm):
                            o = dest_of(s, i * nm + m)[:, 0:N]
                            src = ps[(run.t0 + i) % RING][:, m, 0:N]
                            if not s.dim:
                                last = nc.vector.tensor_copy(o, src)
                                continue
                            last = nc.vector.scalar_tensor_tensor(o, src, vec(s.gain), hr[:, 2 * (i % 2) + m, 0:N],
                                                                  ALU.mult, ALU.mult)
                        last.then_inc(S["head_normed"], 1)
                    if j >= 2:
                        i = j - 2
                        dve.wait_ge(S["head_rotated"], b["head_rotated"] + i + 1)
                        for m in range(nm):
                            nc.vector.tensor_tensor(rope_t[:, m, 0:SEQ], ps[(run.t0 + i) % RING][:, m, 0:SEQ], con(s.sin),
                                                    ALU.mult)
                            o = dest_of(s, i * nm + m)[:, 0:SEQ]
                            last = nc.vector.tensor_tensor(o, o, con(s.cos), ALU.mult)
                        last.then_inc(psum_free, 1)
                        dve.wait_ge(psum_free, run.t0 + i + 1)
                        for m in range(nm):
                            o = dest_of(s, i * nm + m)[:, 0:SEQ]
                            last = nc.vector.tensor_tensor(o, o, rope_t[:, m, 0:SEQ], ALU.add)
                        last.then_inc(S["head_done"], 1)
                        dve.wait_ge(S["head_done"], b["head_done"] + i + 1)

            def values(s):
                for j in range(s.run.n):
                    split(ahead(Unit(s.run, s.run.t0 + j, j, s.run.t0 + j), 2))
                    dve.wait_ge(S["v_done"], s.b["v_done"] + j + 1)
                    dve.sem_inc(psum_free, 1)

            def diff(s):
                b = s.b
                lam = vec("lambda").rearrange("p (a d) -> p a d", a=4)
                pairs = rope_t[:, 0, 0:2 * HD].rearrange("p (a d) -> p a d", a=2)
                nc.vector.tensor_tensor(pairs, lam[:, 0:4:2, :], lam[:, 1:4:2, :], ALU.mult).then_inc(S["head_rope_a"], 1)
                dve.wait_ge(S["head_rope_a"], 1)
                nc.vector.tensor_reduce(stats[:, 0:2], pairs, AX, ALU.add).then_inc(S["lam_parts"], 1)
                dve.wait_ge(S["lam_parts"], b["lam_parts"] + 2)
                nc.vector.scalar_tensor_tensor(stats[:, 4:5], stats[:, 2:3], LAM_INIT, stats[:, 3:4], ALU.add,
                                               ALU.subtract).then_inc(S["lam_parts"], 1)
                dve.wait_ge(S["lam_parts"], b["lam_parts"] + 3)

                def maxima(i):
                    n = BOTH if i % 4 < 2 else CTX
                    for c in range(2):
                        r = 2 * (i % 2) + c
                        dve.wait_ge(S["scores_ready"], b["scores_ready"] + 2 * i + c + 1)
                        nc.vector.tensor_reduce(stats[:, 8 + r:9 + r], bank[r][:, 0:n], AX, ALU.max).then_inc(S["score_max"], 1)
                    dve.wait_ge(S["score_max"], b["score_max"] + 2 * i + 2)
                    r = 2 * (i % 2)
                    nc.vector.tensor_scalar(stats[:, 16 + r:18 + r], stats[:, 8 + r:10 + r], -(HD ** -0.5), None,
                                            ALU.mult).then_inc(S["neg_max"], 1)

                def combine(i):
                    n = BOTH if i % 4 < 2 else CTX
                    r = 2 * (i % 2)
                    dve.wait_ge(S["probs_ready"], b["probs_ready"] + 2 * i + 2)
                    nc.vector.reciprocal(stats[:, 24 + r:26 + r], stats[:, 20 + r:22 + r]).then_inc(S["prob_sums"], 1)
                    dve.wait_ge(S["prob_sums"], b["prob_sums"] + i + 1)
                    nc.vector.tensor_scalar(stats[:, 28 + r:29 + r], stats[:, 25 + r:26 + r], stats[:, 4:5], None,
                                            ALU.mult).then_inc(S["prob_scales"], 1)
                    dve.wait_ge(S["prob_scales"], b["prob_scales"] + i + 1)
                    nc.vector.tensor_scalar(prob2[:, 0:n], probs[:, r + 1, 0:n], stats[:, 28 + r:29 + r], None,
                                            ALU.mult).then_inc(S["prob2_scaled"], 1)
                    dve.wait_ge(S["prob2_scaled"], b["prob2_scaled"] + i + 1)
                    if i >= 2:
                        dve.wait_ge(S["attn_turned"], b["attn_turned"] + i - 1)
                    nc.vector.scalar_tensor_tensor(attn[:, i % 2, 0:n], probs[:, r, 0:n], stats[:, 24 + r:25 + r],
                                                   prob2[:, 0:n], ALU.mult, ALU.subtract).then_inc(S["attn_ready"], 1)

                maxima(0)
                for i in range(NI):
                    if i + 1 < NI:
                        maxima(i + 1)
                    combine(i)
                nc.vector.tensor_scalar(stats[:, 5:6], vec("a_subln"), 1.0 - LAM_INIT, None,
                                        ALU.mult).then_inc(S["head_rope_a"], 1)
                dve.wait_ge(S["head_rope_a"], 2)
                for h in range(A_HEADS):
                    r = scaled[:, h % 2, :]
                    dve.wait_ge(S["out_dev"], b["out_dev"] + h + 1)
                    nc.vector.reciprocal(r, r).then_inc(S["out_rstd"], 1)
                    dve.wait_ge(S["out_rstd"], b["out_rstd"] + h + 1)
                    if h >= 3:
                        dve.wait_ge(S["out_lo"], b["out_lo"] + h - 2)
                    nc.vector.scalar_tensor_tensor(full[:, h % 3, :], qk[:, h, :], stats[:, 5:6], r, ALU.mult,
                                                   ALU.mult).then_inc(S["out_full"], 1)
                    dve.wait_ge(S["out_full"], b["out_full"] + h + 1)
                    nc.vector.tensor_copy(h_hi[:, h, :], full[:, h % 3, :]).then_inc(S["out_hi"], 1)

            def proj(s):
                sweep(dve, s.run, lambda u: residual(u, s, s.gate, s.b["x_done"], lambda u, m: u.j * 2 + m))

            def angles_(s):
                count = [0]

                def step(ins):
                    ins.then_inc(S["angle_step"], 1)
                    count[0] += 1
                    dve.wait_ge(S["angle_step"], count[0])

                turn = 2 * math.pi
                parts = [6.28125, 0.0019350051879882812]
                parts.append(turn - parts[0] - parts[1])
                magic = 1.5 * 2.0 ** 23
                dve.wait_ge(vec_landed, 48)
                step(nc.vector.tensor_copy(ang[:, 0, :], pos_i[:, 0, :]))
                step(nc.vector.tensor_scalar(ang[:, 6, :], ang[:, 0, :], con("freq128"), None, ALU.mult))
                step(nc.vector.tensor_scalar(ang[:, 7, :], ang[:, 0, :], con("freq64"), None, ALU.mult))
                for i in range(4):
                    a, r, k = ang[:, 6 + i // 2, :], ang[:, 2 + i, :], ang[:, 1, :]
                    quarter = 0.25 if i % 2 == 0 else 0.0
                    step(nc.vector.tensor_scalar(k, a, 1.0 / turn, quarter, ALU.mult, ALU.add))
                    step(nc.vector.tensor_scalar(k, k, magic, None, ALU.add))
                    step(nc.vector.tensor_scalar(k, k, magic, None, ALU.subtract))
                    step(nc.vector.scalar_tensor_tensor(r, k, -parts[0], a, ALU.mult, ALU.add))
                    step(nc.vector.scalar_tensor_tensor(r, k, -parts[1], r, ALU.mult, ALU.add))
                    step(nc.vector.scalar_tensor_tensor(r, k, -parts[2], r, ALU.mult, ALU.add))
                    step(nc.vector.tensor_scalar(r, r, quarter * turn, None, ALU.add))
                    step(nc.vector.tensor_scalar(r, r, 3.1415925, -3.1415925, ALU.min, ALU.max))
                dve.wait_ge(S["angle_done"], 4)

            def soft(s):
                b, n = s.b, len(s.items)
                if s.swap:
                    for c in range(2):
                        dve.wait_ge(S["s_swap"], b["s_swap"] + c + 1)
                        nc.vector.tensor_copy(gk[:, 2 + c, :], bank[c]).then_inc(S["s_swapped"], 1)

                def masked(i):
                    it = s.items[i]
                    nk, r = it["k"][3], i % 2
                    dve.wait_ge(S["s_scores"], b["s_scores"] + i + 1)
                    if i >= 2:
                        dve.wait_ge(S["s_probs"], b["s_probs"] + i - 1)
                    if "needs" in it:
                        dve.wait_ge(S[it["needs"][0]], it["needs"][1])
                    if nk > SEQ:
                        nc.vector.tensor_scalar(logits[:, r, SEQ:nk], bank[i % 4][:, SEQ:nk], s.scale, None, ALU.mult)
                    nc.vector.scalar_tensor_tensor(logits[:, r, 0:SEQ], bank[i % 4][:, 0:SEQ], s.scale, mask_of(it), ALU.mult,
                                                   ALU.add).then_inc(S["s_masked"], 1)
                    dve.wait_ge(S["s_masked"], b["s_masked"] + i + 1)
                    nc.vector.tensor_reduce(stats[:, 8 + r:9 + r], logits[:, r, 0:nk], AX, ALU.max).then_inc(S["s_max"], 1)
                    dve.wait_ge(S["s_max"], b["s_max"] + i + 1)
                    if it["sink"] is not None:
                        nc.vector.tensor_scalar(stats[:, 10 + r:11 + r], stats[:, 8 + r:9 + r], vec("sink", it["sink"]), -1.0,
                                                ALU.max, ALU.mult).then_inc(S["s_neg"], 1)
                    else:
                        nc.vector.tensor_scalar(stats[:, 10 + r:11 + r], stats[:, 8 + r:9 + r], -1.0, None,
                                                ALU.mult).then_inc(S["s_neg"], 1)

                def normed(i):
                    it = s.items[i]
                    nk, r = it["k"][3], i % 2
                    dve.wait_ge(S["s_probs"], b["s_probs"] + i + 1)
                    total = stats[:, 12 + r:13 + r]
                    if it["sink"] is not None:
                        dve.wait_ge(S["s_sink"], b["s_sink"] + i + 1)
                        nc.vector.tensor_tensor(stats[:, 16 + r:17 + r], total, stats[:, 14 + r:15 + r],
                                                ALU.add).then_inc(S["s_total"], 1)
                        dve.wait_ge(S["s_total"], b["s_total"] + i + 1)
                        total = stats[:, 16 + r:17 + r]
                    nc.vector.reciprocal(stats[:, 18 + r:19 + r], total).then_inc(S["s_rcp"], 1)
                    dve.wait_ge(S["s_rcp"], b["s_rcp"] + i + 1)
                    if i >= 2:
                        dve.wait_ge(S["s_turned"], b["s_turned"] + i - 1)
                    nc.vector.tensor_scalar(attn[:, r, 0:nk], probs[:, r, 0:nk], stats[:, 18 + r:19 + r], None,
                                            ALU.mult).then_inc(S["s_attn"], 1)

                def halves(chunk):
                    hi, lo = out_of(s, chunk)
                    dve.wait_ge(S["s_chunk"], b["s_chunk"] + chunk + 1)
                    nc.vector.tensor_copy(hi, pm[:, chunk % 2, 0:SEQ]).then_inc(S["s_hi"], 1)
                    dve.wait_ge(S["s_hi"], b["s_hi"] + chunk + 1)
                    nc.vector.tensor_tensor(lo, pm[:, chunk % 2, 0:SEQ], hi.bitcast(F32), ALU.subtract).then_inc(S["s_lo"], 1)

                masked(0)
                for i in range(n):
                    if i + 1 < n:
                        masked(i + 1)
                    normed(i)
                    if i >= 2 and (i - 2) % s.per == s.per - 1:
                        halves((i - 2) // s.per)
                for chunk in range((n - 2) // s.per, n // s.per):
                    halves(chunk)

            def iw(s):
                u = Unit(s.run, s.run.t0, 0, s.run.t0)
                split(ahead(u, 2))
                dve.wait_ge(S["iw_done"], s.b["iw_done"] + 1)
                dve.sem_inc(psum_free, 1)

            def select(s):
                b = s.b
                count = [b["top_steps"]]

                def step(ins):
                    ins.then_inc(S["top_steps"], 1)
                    count[0] += 1
                    dve.wait_ge(S["top_steps"], count[0])

                for q in range(2):
                    for h in range(HEADS2):
                        i = q * HEADS2 + h
                        dve.wait_ge(S["idx_relu"], b["idx_relu"] + i + 1)
                        wcol = iw_sb[:, q, h:h + 1]
                        if h == 0:
                            ins = nc.vector.tensor_scalar(idx[:, q, :], rel[:, h, :], wcol, None, ALU.mult)
                        else:
                            ins = nc.vector.scalar_tensor_tensor(idx[:, q, :], rel[:, h, :], wcol, idx[:, q, :], ALU.mult, ALU.add)
                        ins.then_inc(S["idx_sum"], 1)
                        dve.wait_ge(S["idx_sum"], b["idx_sum"] + i + 1)
                for q in range(2):
                    sc, work = idx[:, q, :], idx_work[:, q, :]
                    dve.wait_ge(S["idx_causal"], b["idx_causal"] + q + 1)
                    top = stats[:, 24 + 8 * q:32 + 8 * q]
                    cur = sc
                    for r in range(TOPK // 8):
                        step(nc.vector.max(top, cur))
                        if r < TOPK // 8 - 1:
                            step(nc.vector.match_replace(work, top, cur, LOWEST))
                            cur = work
                    least = top[:, 7:8]
                    above, need = stats[:, 40 + q:41 + q], stats[:, 42 + q:43 + q]
                    step(nc.vector.tensor_scalar(sel_gt[:, q, :], sc, least, None, ALU.is_gt, ALU.add, accum_out=above))
                    step(nc.vector.tensor_scalar(sel_eq[:, q, :], sc, least, None, ALU.is_equal))
                    step(nc.vector.tensor_tensor_scan(sel_cum[:, q, :], sel_eq[:, q, :], sel_eq[:, q, :], 0.0, ALU.add, ALU.max))
                    step(nc.vector.tensor_scalar(need, above, -1.0, float(TOPK), ALU.mult, ALU.add))
                    step(nc.vector.scalar_tensor_tensor(sel_eq[:, q, :], sel_cum[:, q, :], need, sel_eq[:, q, :], ALU.is_le, ALU.mult))
                    step(nc.vector.tensor_tensor(sel_gt[:, q, :], sel_gt[:, q, :], sel_eq[:, q, :], ALU.add))
                    nc.vector.tensor_scalar(sel_gt[:, q, :], sel_gt[:, q, :], -NEG, NEG, ALU.mult, ALU.add).then_inc(S["sel_add"], 1)

            def conv(src, dst, weights_of, bias_of, taps, signal, base):
                for w in range(taps):
                    for c in range(4):
                        if w:
                            dve.wait_ge(S[signal], base + 4 * (w - 1) + c + 1)
                        x = src[:, c, w:w + SEQ]
                        if w == 0 and bias_of is not None:
                            ins = nc.vector.tensor_scalar(dst[:, c, :], x, weights_of(c, w), bias_of(c), ALU.mult, ALU.add)
                        elif w == 0:
                            ins = nc.vector.tensor_scalar(dst[:, c, :], x, weights_of(c, w), None, ALU.mult)
                        else:
                            ins = nc.vector.scalar_tensor_tensor(dst[:, c, :], x, weights_of(c, w), dst[:, c, :], ALU.mult, ALU.add)
                        ins.then_inc(S[signal], 1)

            def glu(s):
                b, l = s.b, s.l
                nc.vector.memset(cb_in[:, :, 0:CB_TAPS - 1], 0.0).then_inc(S["conv_pad"], 1)

                def gated(u):
                    split(ahead(u, 2))
                    dve.wait_ge(S["glu_sig"], b["glu_sig"] + u.j + 1)
                    nc.vector.tensor_tensor(cb_in[:, u.j, CB_TAPS - 1:], sil[:, u.j % RING, 0:SEQ], ps[u.slot][:, 0, 0:SEQ],
                                            ALU.mult).then_inc(S["glu_in"], 1)
                    dve.wait_ge(S["glu_in"], b["glu_in"] + u.j + 1)
                    dve.sem_inc(psum_free, 1)

                sweep(dve, s.run, gated)
                dve.wait_ge(S["conv_pad"], b["conv_pad"] + 1)
                conv(cb_in, cb_out, lambda c, w: vec(f"cb_w{l}", c * CB_TAPS + w), lambda c: vec(f"cb_b{l}", c), CB_TAPS,
                     "conv_steps", b["conv_steps"])
                dve.wait_ge(S["ln_sum"], b["ln_sum"] + 1)
                nc.vector.tensor_scalar(rope_t[:, 0, 0:SEQ], pm[:, 0, 0:SEQ], 1.0 / 512, None, ALU.mult).then_inc(S["ln_mean"], 1)
                dve.wait_ge(S["ln_mean"], b["ln_mean"] + 1)
                for c in range(4):
                    nc.vector.tensor_tensor(cb_out[:, c, :], cb_out[:, c, :], rope_t[:, 0, 0:SEQ],
                                            ALU.subtract).then_inc(S["ln_mid"], 1)
                dve.wait_ge(S["ln_dev"], b["ln_dev"] + 1)
                nc.vector.reciprocal(rstd[:, 0:SEQ], rstd[:, 0:SEQ]).then_inc(S["ln_rstd"], 1)
                dve.wait_ge(S["ln_rstd"], b["ln_rstd"] + 1)
                for c in range(4):
                    nc.vector.tensor_tensor(cb_out[:, c, :], cb_out[:, c, :], rstd[:, 0:SEQ], ALU.mult).then_inc(S["ln_out"], 1)
                for c in range(4):
                    dve.wait_ge(S["ln_act"], b["ln_act"] + c + 1)
                    nc.vector.tensor_copy(branch["ob"][0][:, c, :], ln_t[:, c, :]).then_inc(S["ob_hi"], 1)

            def cc(s):
                b, l = s.b, s.l
                dve.wait_ge(S["ln_act"], counts_before(s, "ln_act"))
                nc.vector.memset(cc_in[:, :, 0:CC_TAPS - 1], 0.0).then_inc(S["cc_pad"], 1)

                def gated(u):
                    split(ahead(u, 2))
                    dve.wait_ge(S["cc_gate"], b["cc_gate"] + u.j + 1)
                    nc.vector.tensor_tensor(cc_in[:, u.j, CC_TAPS - 1:], sil[:, u.j % RING, 0:SEQ], ps[u.slot][:, 1, 0:SEQ],
                                            ALU.mult).then_inc(S["cc_in"], 1)
                    dve.wait_ge(S["cc_in"], b["cc_in"] + u.j + 1)
                    dve.sem_inc(psum_free, 1)

                sweep(dve, s.pair, gated)
                dve.wait_ge(S["cc_pad"], b["cc_pad"] + 1)
                conv(cc_in, cc_out, lambda c, w: vec(f"cc_w{l}", c * CC_TAPS + w), None, CC_TAPS, "cc_steps", b["cc_steps"])
                dve.wait_ge(S["cc_steps"], b["cc_steps"] + 4 * CC_TAPS)

                def product(u):
                    split(ahead(u, 2))
                    dve.wait_ge(unit_done, u.t + 1)
                    for m in range(2):
                        c = 2 * u.j + m
                        nc.vector.tensor_tensor(cc_out[:, c, :], cc_out[:, c, :], ps[u.slot][:, m, 0:SEQ],
                                                ALU.mult).then_inc(S["cc_out"], 1)
                        dve.wait_ge(S["cc_out"], b["cc_out"] + c + 1)
                        nc.vector.tensor_copy(branch["oc"][0][:, c, :], cc_out[:, c, :]).then_inc(S["oc_hi"], 1)
                    dve.sem_inc(psum_free, 1)

                sweep(dve, s.run, product)

            def plain(s):
                def free(u):
                    split(ahead(u, 2))
                    dve.wait_ge(S["plain_done"], s.b["plain_done"] + u.j + 1)
                    dve.sem_inc(psum_free, 1)

                sweep(dve, s.run, free)

            def stick(s):
                b = s.b

                def first(h):
                    r = h % 2
                    dve.wait_ge(S["z_kept"], b["z_kept"] + h + 1)
                    if h >= 2:
                        dve.wait_ge(S["z_attn"], b["z_attn"] + h - 1)
                    nc.vector.scalar_tensor_tensor(z_e[:, r, :], z_s[:, r, :], -1.0, z_s[:, r, :], ALU.mult,
                                                   ALU.min).then_inc(S["z_neg"], 1)
                    dve.wait_ge(S["z_log"], b["z_log"] + h + 1)
                    nc.vector.scalar_tensor_tensor(z_l[:, r, :], z_s[:, r, :], 0.0, z_l[:, r, :], ALU.max,
                                                   ALU.add).then_inc(S["z_soft"], 1)

                def second(h):
                    r = h % 2
                    dve.wait_ge(S["z_sums"], b["z_sums"] + h + 1)
                    nc.vector.tensor_tensor(z_e[:, r, :], z_s[:, r, :], bank[2 + r], ALU.subtract).then_inc(S["z_arg"], 1)

                def halves(h):
                    hi, lo = (t[:, h, :] for t in branch["od"])
                    dve.wait_ge(S["z_out"], b["z_out"] + h + 1)
                    nc.vector.tensor_copy(hi, pm[:, h % 2, 0:SEQ]).then_inc(S["od_hi"], 1)
                    dve.wait_ge(S["od_hi"], b["od_hi"] + h + 1)
                    nc.vector.tensor_tensor(lo, pm[:, h % 2, 0:SEQ], hi.bitcast(F32), ALU.subtract).then_inc(S["od_lo"], 1)

                for h in range(HEADS2):
                    first(h)
                    second(h)
                    if h:
                        halves(h - 1)
                halves(HEADS2 - 1)

            def branches(s):
                b = s.b

                def free(u):
                    split(ahead(u, 2))
                    dve.wait_ge(S["gate_done"], b["gate_done"] + u.j + 1)
                    dve.sem_inc(psum_free, 1)

                def weigh(u):
                    split(ahead(u, 2))
                    dve.wait_ge(unit_done, u.t + 1)
                    two = slice(2 * u.j, 2 * u.j + 2)
                    o = merged[:, two, :] if s.i == 0 else gated_t
                    nc.vector.tensor_tensor(o, gates[:, two, :], ps[u.slot][:, :, 0:SEQ], ALU.mult).then_inc(S["gated"], 1)
                    dve.wait_ge(S["gated"], b["gated"] + u.j + 1)
                    dve.sem_inc(psum_free, 1)
                    if s.i == 0:
                        dve.sem_inc(S["merged"], 1)
                    else:
                        nc.vector.tensor_tensor(merged[:, two, :], merged[:, two, :], gated_t, ALU.add).then_inc(S["merged"], 1)
                    dve.wait_ge(S["merged"], b["merged"] + u.j + 1)

                sweep(dve, s.gates, free)
                sweep(dve, s.run, weigh)

            def merge(s):
                for c in range(KC):
                    nc.vector.tensor_copy(h_hi[:, c, 0:SEQ], merged[:, c, :]).then_inc(S["m_hi"], 1)

            def convffn(s):
                b, l = s.b, s.l
                dve.wait_ge(S["h_lo"], s.h + KC)
                nc.vector.memset(cin[:, :, 0:CC_TAPS - 1], 0.0).then_inc(S["cin_pad"], 1)
                dve.wait_ge(S["cin_pad"], b["cin_pad"] + 1)
                o, _ = VEC[f"ffn_w{l}"]
                for h, (wi, wd) in enumerate(s.halves):
                    def taps(u):
                        split(ahead(u, 2))
                        r = u.j0 % RING
                        f0 = h * HALF
                        dve.wait_ge(S["cin_ready"], u.j + (b["cin_ready"] + f0 + 1))
                        for w in range(CC_TAPS):
                            wcol = vec_sb[:, bass.ds(u.j * CC_TAPS + (o + f0 * CC_TAPS + w), 1)]
                            x = cin[:, r, w:w + SEQ]
                            if w == 0:
                                ins = nc.vector.tensor_scalar(tap_t[:, r, :], x, wcol, None, ALU.mult)
                            else:
                                dve.wait_ge(S[f"tap{w - 1}"], u.j + (b[f"tap{w - 1}"] + f0 + 1))
                                ins = nc.vector.scalar_tensor_tensor(tap_t[:, r, :], x, wcol, tap_t[:, r, :], ALU.mult, ALU.add)
                            ins.then_inc(S[f"tap{w}"], 1)
                        dve.wait_ge(S["silu_ready"], u.j + (b["silu_ready"] + f0 + 1))
                        nc.vector.tensor_tensor(sil[:, r, 0:SEQ], sil[:, r, 0:SEQ], ps[u.slot][:, 1, 0:SEQ],
                                                ALU.mult).then_inc(psum_free, 1)
                        dve.wait_ge(psum_free, u.t + 1)
                        nc.vector.tensor_copy(act_hi[:, bass.ds(u.j, 1), 0:SEQ].rearrange("p c n -> p (c n)"),
                                              sil[:, r, 0:SEQ]).then_inc(S["act_hi"], 1)

                    sweep(dve, wi, taps)
                    sweep(dve, wd, lambda u: residual(u, s, None, b["x_done"] + h * KC, lambda u, m: u.j))

            todo = dict(ada=ada, norm=norm, ffn=ffn, heads=heads, values=values, diff=diff, proj=proj, angles=angles_, soft=soft,
                        iw=iw, select=select, glu=glu, cc=cc, plain=plain, stick=stick, branch=branches, merge=merge,
                        convffn=convffn)
            for s in stages:
                if s.kind in todo:
                    todo[s.kind](s)

        @block.gpsimd
        def _(pool):
            def rest(o, whole, hi, signal):
                nc.gpsimd.tensor_tensor(o, whole, hi.bitcast(F32), ALU.subtract).then_inc(signal, 1)

            def norm(s):
                N, b = s.N, s.b
                for c in range(KC):
                    pool.wait_ge(S["h_hi"], b["h_hi"] + c + 1)
                    rest(h_lo[:, c, 0:N], full[:, c % 3, 0:N], h_hi[:, c, 0:N], S["h_lo"])

            def ffn(s):
                N, b = s.N, s.b
                for h, (wi, wo) in enumerate(s.halves):
                    def lows(u):
                        pool.wait_ge(S["act_hi"], u.j + (b["act_hi"] + h * HALF + 1))
                        o = act_lo[:, bass.ds(u.j, 1), 0:N].rearrange("p c n -> p (c n)")
                        hi = act_hi[:, bass.ds(u.j, 1), 0:N].rearrange("p c n -> p (c n)")
                        rest(o, sil[:, u.j0 % RING, 0:N], hi, S["act_lo"])

                    sweep(pool, wi, lows)

            def diff(s):
                b = s.b
                for h in range(A_HEADS):
                    pool.wait_ge(S["out_hi"], b["out_hi"] + h + 1)
                    rest(h_lo[:, h, :], full[:, h % 3, :], h_hi[:, h, :], S["out_lo"])

            def select(s):
                b = s.b
                for src, signal, ready, fill, dst in ((idx, "idx_causal", "idx_sum", LOWEST, idx),
                                                      (sel_gt, "sel_mask", "sel_add", NEG, sel_mask)):
                    for q in range(2):
                        pool.wait_ge(S[ready], b[ready] + (HEADS2 * (q + 1) if ready == "idx_sum" else q + 1))
                        nc.gpsimd.affine_select(out=dst[:, q, :], in_=src[:, q, :], pattern=[[-1, SEQ]], compare_op=ALU.is_ge,
                                                fill=fill, base=q * P, channel_multiplier=1).then_inc(S[signal], 1)

            def glu(s):
                b = s.b
                for c in range(4):
                    pool.wait_ge(S["ob_hi"], b["ob_hi"] + c + 1)
                    rest(branch["ob"][1][:, c, :], ln_t[:, c, :], branch["ob"][0][:, c, :], S["ob_lo"])

            def cc(s):
                b = s.b
                for c in range(4):
                    pool.wait_ge(S["oc_hi"], b["oc_hi"] + c + 1)
                    rest(branch["oc"][1][:, c, :], cc_out[:, c, :], branch["oc"][0][:, c, :], S["oc_lo"])

            def stick(s):
                b = s.b

                def mask(dst, src, fill, signal):
                    nc.gpsimd.affine_select(out=dst.rearrange("p (k t) -> p k t", k=2), in_=src.rearrange("p (k t) -> p k t", k=2),
                                            pattern=[[-P, 2], [1, SEQ]], compare_op=ALU.is_gt, fill=fill, base=0,
                                            channel_multiplier=-1).then_inc(S[signal], 1)

                for h in range(HEADS2):
                    r = h % 2
                    pool.wait_ge(S["z_soft"], b["z_soft"] + h + 1)
                    mask(z_m[:, r, :], z_l[:, r, :], 0.0, "z_soft_m")
                    pool.wait_ge(S["z_arg"], b["z_arg"] + h + 1)
                    mask(z_e[:, r, :], z_e[:, r, :], NEG, "z_arg_m")

            def merge(s):
                b = s.b
                for c in range(KC):
                    pool.wait_ge(S["m_hi"], b["m_hi"] + c + 1)
                    rest(h_lo[:, c, 0:SEQ], merged[:, c, :], h_hi[:, c, 0:SEQ], S["m_lo"])

            def convffn(s):
                b = s.b
                for h, (wi, wd) in enumerate(s.halves):
                    def lows(u):
                        pool.wait_ge(S["act_hi"], u.j + (b["act_hi"] + h * HALF + 1))
                        o = act_lo[:, bass.ds(u.j, 1), 0:SEQ].rearrange("p c n -> p (c n)")
                        hi = act_hi[:, bass.ds(u.j, 1), 0:SEQ].rearrange("p c n -> p (c n)")
                        rest(o, sil[:, u.j0 % RING, 0:SEQ], hi, S["act_lo"])

                    sweep(pool, wi, lows)

            todo = dict(norm=norm, ffn=ffn, diff=diff, select=select, glu=glu, cc=cc, stick=stick, merge=merge, convffn=convffn)
            for s in stages:
                if s.kind in todo:
                    todo[s.kind](s)


INS = ["ada_w", "ffn_pre_wi", "ffn_pre_wo", "ffn_post_wi", "ffn_post_wo", "a_w_qkv", "a_w_o", "b_w_qkv", "b_w_o",
       "w_in_2", "w_oa_2", "w_ob_2", "w_oc_2", "w_od_2", "w_merge_2", "w_ffn_gate_2", "w_ffn_up_2", "w_ffn_down_2"]


def lay_out(inputs):
    arr = {k: np.asarray(v) for k, v in inputs.items()}
    x_t = np.concatenate([arr["x"][0].T, arr["ctx"][0].T], axis=1)
    vecs = np.zeros((P, N_VEC), np.float32)

    def put(name, a):
        o, w = VEC[name]
        vecs[:, o:o + w] = np.ascontiguousarray(a).reshape(P, w)

    def lanes(a):
        return a.reshape(-1, P).T

    put("cond", np.stack([lanes(arr["c"][0]), lanes(arr["c_ctx"])], axis=-1))
    for l in range(DEPTH):
        put(f"ada_b{l}", np.repeat(lanes(arr["ada_b"][l])[:, :, None], 2, axis=2))
    for name, key in (("a_q_gain", "a_q_gain"), ("a_k_gain", "a_k_gain"), ("b_q_gain", "b_q_gain"), ("b_k_gain", "b_k_gain")):
        put(name, np.tile(arr[key][0], 2))
    put("a_subln", arr["a_subln_gain"][0])
    put("lambda", np.broadcast_to(arr["a_lambda"][0].reshape(1, -1), (P, 4 * HD)))
    put("sink", np.broadcast_to(arr["b_sink"][0].reshape(1, -1), (P, B_Q_HEADS)))
    for l in range(DEPTH):
        put(f"g_mix{l}", lanes(arr["g_mix_2"][l]))
        put(f"b_gate{l}", lanes(arr["b_gate_2"][l]))
        put(f"g_qa{l}", arr["g_qa_2"][l])
        put(f"g_ka{l}", arr["g_ka_2"][l])
        put(f"g_kidx{l}", np.tile(arr["g_kidx_2"][l], 2))
        put(f"cb_w{l}", arr["cb_conv_w_2"][l].T.reshape(4, P, CB_TAPS).transpose(1, 0, 2))
        put(f"cb_b{l}", lanes(arr["cb_conv_b_2"][l]))
        put(f"ln_g{l}", lanes(arr["cb_ln_g_2"][l]))
        put(f"ln_b{l}", lanes(arr["cb_ln_b_2"][l]))
        put(f"cc_w{l}", arr["cc_conv_w_2"][l].T.reshape(4, P, CC_TAPS).transpose(1, 0, 2))
        put(f"g_ffn{l}", lanes(arr["g_ffn_2"][l]))
        put(f"ffn_w{l}", arr["ffn_conv_w_2"][l].T.reshape(FC, P, CC_TAPS).transpose(1, 0, 2))
    pos = np.ascontiguousarray(np.broadcast_to(arr["positions_2"].reshape(1, SEQ), (P, SEQ)))
    arrays = {"x_t": np.ascontiguousarray(x_t), "vecs": vecs, "consts": shape_constants(), "positions": pos}
    for name in INS:
        arrays[name] = np.ascontiguousarray(arr[name])
    return arrays


def kernel(**inputs):
    import concourse.bacc as bacc
    from concourse.bass_utils import run_bass_kernel_spmd

    arrays = lay_out(inputs)
    nc = bacc.Bacc("TRN2", target_bir_lowering=False, num_devices=1)
    args = [nc.dram_tensor(f"in_{n}", a.shape, mybir.dt.from_np(a.dtype), kind="ExternalInput").ap() for n, a in arrays.items()]
    out = nc.dram_tensor("out_t", (D, SEQ), F32, kind="ExternalOutput").ap()
    build(nc, *args, out)
    r = run_bass_kernel_spmd(nc, [{f"in_{n}": a for n, a in arrays.items()}], core_ids=[0])
    return np.ascontiguousarray(r.results[0]["out_t"].T).reshape(1, SEQ, D)
```

```python
import math
from collections import Counter

import numpy as np

import concourse.bass as bass
from concourse import mybir
from concourse.alu_op_type import AluOpType as ALU

F32 = mybir.dt.float32
F32R = mybir.dt.float32r
I32 = mybir.dt.int32
ACT = mybir.ActivationFunctionType
AX = mybir.AxisListType.X

P = 128
D = 1024
KC = D // P
SEQ = 256
CTX = 256
BOTH = SEQ + CTX
DEPTH = 2
D_FF = 2816
FC = D_FF // P
HALF = FC // 2
N_MOD = 9
MODC = N_MOD * KC
EPS = 1e-6
GRID_W = 64
A_HEADS = 8
B_Q_HEADS = 16
B_KV_HEADS = 4
B_GROUP = B_Q_HEADS // B_KV_HEADS
HD = 64
WINDOW = 128
HEADS2 = 4
TOPK = min(256, SEQ // 4)
CB_TAPS = 31
CC_TAPS = 3
NEG = -1e30
LOWEST = -3e38
LAM_INIT = 0.8 - 0.6 * math.exp(-0.3 * 0)
RING = 3
SLOT = KC * 2 * P
PER_MOD = KC // 2
NI = A_HEADS * 4
OFF = {}
_at = 0
for _name, _w in (("aq", 512), ("ak", 512), ("av", 512), ("iq", 256), ("ik", 64), ("iw", 4), ("glu", 1024),
                  ("cc", 1536), ("sb", 1536), ("gate", 4096)):
    OFF[_name] = _at
    _at += _w
N_IN = _at

VEC = {}
_at = 0


def _vec(name, width):
    global _at
    VEC[name] = (_at, width)
    _at += width


_vec("cond", KC * 2)
for _l in range(DEPTH):
    _vec(f"ada_b{_l}", MODC * 2)
for _name in ("a_q_gain", "a_k_gain", "a_subln", "b_q_gain", "b_k_gain"):
    _vec(_name, 1)
_vec("lambda", 4 * HD)
_vec("sink", B_Q_HEADS)
for _l in range(DEPTH):
    for _name, _w in (("g_mix", KC), ("b_gate", 4 * KC), ("g_qa", 1), ("g_ka", 1), ("g_kidx", 1),
                      ("cb_w", 4 * CB_TAPS), ("cb_b", 4), ("ln_g", 4), ("ln_b", 4), ("cc_w", 4 * CC_TAPS),
                      ("g_ffn", KC), ("ffn_w", FC * CC_TAPS)):
        _vec(f"{_name}{_l}", _w)
N_VEC = _at

CON = {}
_at = 0
for _name, _w in (("ident", P), ("ones", P), ("blocks", P), ("rot_axial", P), ("rot_part128", P), ("rot_part64", P),
                  ("swap", P), ("suffix", P), ("cos_axial", SEQ), ("sin_axial", SEQ), ("band", 2 * SEQ),
                  ("causal", 2 * SEQ), ("fold", 2), ("freq128", 1), ("freq64", 1), ("eps", 1)):
    CON[_name] = (_at, _w)
    _at += _w
N_CON = _at


def shape_constants():
    c = np.zeros((P, N_CON), np.float32)

    def put(name, a):
        o, w = CON[name]
        c[:, o:o + w] = np.asarray(a, np.float32).reshape(P, w)

    lane = np.arange(P)
    put("ident", np.eye(P))
    put("ones", np.ones((P, P)))
    put("blocks", (lane[:, None] // HD) == (lane[None, :] // HD))

    def rotation(half, group):
        r = np.zeros((P, P), np.float32)
        for g in range(0, P, group[0]):
            for b in range(0, group[1], 2 * half):
                for f in range(half):
                    r[g + b + half + f, g + b + f] = -1.0
                    r[g + b + f, g + b + half + f] = 1.0
        return r

    put("rot_axial", rotation(HD // 4, (HD, HD)))
    put("rot_part128", rotation(P // 8, (P, P // 4)))
    put("rot_part64", rotation(HD // 8, (HD, HD // 4)))
    put("swap", np.roll(np.eye(P), HD, axis=0))
    put("suffix", lane[:, None] >= lane[None, :])
    nf = HD // 4
    inv = (np.float32(10000.0) ** (-np.arange(nf, dtype=np.float32) / np.float32(nf))).astype(np.float32)
    t = np.arange(SEQ)
    row, col = (t // GRID_W).astype(np.float32), (t % GRID_W).astype(np.float32)
    ang = np.zeros((HD, SEQ), np.float32)
    for d in range(HD):
        ang[d] = (row if d // (HD // 2) == 0 else col) * inv[d % nf]
    ang = np.concatenate([ang, ang])
    put("cos_axial", np.cos(ang))
    put("sin_axial", np.sin(ang))
    band = np.zeros((P, 2, SEQ), np.float32)
    for q in range(2):
        band[:, q, :] = np.where(np.abs(t[None, :] - (q * P + lane[:, None])) <= WINDOW, 0.0, NEG)
    put("band", band)
    causal = np.zeros((P, 2, SEQ), np.float32)
    for q in range(2):
        causal[:, q, :] = np.where(t[None, :] <= q * P + lane[:, None], 0.0, LOWEST)
    put("causal", causal)
    put("fold", (lane[:, None] % 2 == np.arange(2)[None, :]) & (lane[:, None] < 4))
    for name, dim in (("freq128", P), ("freq64", HD)):
        rot = dim // 4
        half = rot // 2
        f = (np.float32(500000.0) ** (-(np.arange(half, dtype=np.float32) * np.float32(2.0)) / np.float32(rot)))
        v = np.zeros(P, np.float32)
        for g in range(0, P, dim):
            v[g:g + half] = f
            v[g + half:g + rot] = f
        put(name, v)
    put("eps", np.full(P, EPS))
    return c


class Run:

    def __init__(self, name, n, kc, cols, src, by, dmas=1):
        self.name, self.n, self.kc, self.cols, self.src, self.by = name, n, kc, cols, src, by
        self.dmas = dmas


class Unit:

    def __init__(self, run, j0, turn=None):
        self.run, self.j0, self.turn = run, j0, turn
        at = (lambda n: n) if turn is None else (lambda n: turn * RING + n)
        self.t0 = run.t0 + j0
        self.j = at(j0)
        self.slot = self.t0 % RING
        self.count = at(self.t0 + 1)
        self.out = at(run.f0 + j0 + 1)


def build(nc, x_t, vecs, consts, positions, ada_w, pre_wi, pre_wo, post_wi, post_wo, a_w_qkv, a_w_o, b_w_qkv, b_w_o,
          w_in, w_oa, w_ob, w_oc, w_od, w_merge, w_gate, w_up, w_down, out, stop=None):
    def cols_of(w, col0, width, k0=0, kc=KC):
        def src(j):
            return [(0, w[k0 * P:(k0 + kc) * P, :].rearrange("(k p) m -> p k m", p=P)
                     [:, :, bass.ds(col0 + j * width, width)])]
        return src

    def two_of(wa, ca, wb, cb):
        def src(j):
            return [(0, wa.rearrange("(k p) m -> p k m", p=P)[:, :, bass.ds(ca + j * P, P)]),
                    (P, wb.rearrange("(k p) m -> p k m", p=P)[:, :, bass.ds(cb + j * P, P)])]
        return src

    unit_done, hi_ready, lo_ready = (nc.alloc_semaphore(n) for n in ("unit_done", "hi_ready", "lo_ready"))
    stages, runs, counts = [], [], {}
    units, psum_users = [], []

    class Stage:

        def __init__(self, kind, run=None, N=SEQ, h=None, name=None, l=None, gate=None, gain=None, waits=(), x=None, ready=None,
                     after=None, mod=None, layer=None, which=None, wi=None, wo=None, dim=None, dest=None, ch0=0, rot=None, cos=None,
                     sin=None, tiles=None, items=(), scale=None, v=None, out=None, per=None, swap=False, iw=None,
                     pair=None, i=None, filler=None, steps=(), conv=None, next=None, early=0, runs=()):
            self.kind, self.run, self.N, self.h, self.name, self.l, self.x = kind, run, N, h, name, l, x
            self.gate, self.gain, self.waits, self.ready, self.after, self.mod = gate, gain, waits, ready, after, mod
            self.layer, self.which, self.wi, self.wo, self.iw, self.pair = layer, which, wi, wo, iw, pair
            self.dim, self.dest, self.ch0, self.rot, self.cos, self.sin = dim, dest, ch0, rot, cos, sin
            self.tiles, self.items, self.scale, self.v, self.i = tiles, items, scale, v, i
            self.out, self.per, self.swap, self.filler, self.runs, self.steps, self.conv, self.next, self.early = out, per, swap, filler, runs, steps, conv, next, early
            self.b = Counter(counts)
            stages.append(self)

        def takes(self, **events):
            for name, n in events.items():
                counts[name] = counts.get(name, 0) + n
            return self

    def add(run):
        run.t0 = len(units)
        units.extend((run, j) for j in range(run.n))
        if run.by is None:
            run.free, run.f0 = None, 0
            psum_users.extend([None] * run.n)
        else:
            run.free = "psum_read_" + run.by
            run.f0 = counts.get(run.free, 0)
            psum_users.extend((run.free, run.f0 + j + 1) for j in range(run.n))
            counts[run.free] = run.f0 + run.n
        runs.append(run)
        return run

    def ada(layer, which, filler=False):
        run = Run("ada", len(which) * PER_MOD, KC, 2 * P, cols_of(ada_w[layer], which[0] * D, 2 * P), None)
        s = Stage("ada", layer=layer, which=which, run=add(run), filler=filler)
        s.steps = []
        for i, w in enumerate(which):
            for j in range(PER_MOD):
                s.steps.append(("row", i * PER_MOD + j, ("ada_rows", counts.get("ada_rows", 0) + i * PER_MOD + j + 1)))
            s.steps.append(("turn", w, ("mods_summed", counts.get("mods_summed", 0) + i + 1)))
        return s.takes(ada_rows=run.n, ada_turned=len(which), mods_summed=len(which),
                       mods_ready=sum(w in (1, 2, 4, 7, 8) for w in which))

    def share(s, i, n):
        todo = [(a, k) for a in s.filler or () for k in range(len(a.steps))]
        return todo[i * len(todo) // n:(i + 1) * len(todo) // n]

    def statistics(N, after):
        s = Stage("statistics", N=N, after=after)
        s.early = 0
        if after is not None and stages[-2].kind == "proj":
            s.early = KC - stages[-2].run.cols // P
            stages[-2].next = s
        return s.takes(squares_ready=KC, square_added=KC, square_summed=1,
                                                                     log_ready=1, rstd_ready=1)

    def norm(N, after, mod=None, gain=None, before="ffn_in"):
        if after is not None:
            statistics(N, after)
        s = Stage("norm", N=N, after=after, mod=mod, gain=gain, next=before)
        s.takes(h_lo=KC)
        s.takes(**(dict(h_scaled=KC, h_hi_act=KC) if mod is None else dict(scaled_ready=KC, h_modulated=KC, h_hi_dve=KC)))
        s.h = ("h_lo", s.b["h_lo"])
        norms.append(s.h)
        return s

    norms = []

    def residual_of(run, per):
        return lambda c: (run.free, run.f0 + c // per + 1)

    def ffn(N, wi, wo, gate, between=None):
        for half in range(2):
            wi_run = add(Run("wi", HALF, KC, 2 * P, two_of(wi, half * HALF * P, wi, D_FF + half * HALF * P), "dve", 2))
            first = Stage("ffn_in", N=N, run=wi_run, h=norms[-1]).takes(silu_ready=HALF, act_hi=HALF, act_lo=HALF)
            if between is not None and half == 0:
                between()
            wo_run = add(Run("wo", KC, HALF, P, cols_of(wo, 0, P, half * HALF, HALF), "dve"))
            Stage("proj", run=wo_run, N=N, gate=gate, x="act", ready=("act_lo", first.b["act_lo"]))
        return residual_of(wo_run, 1)

    def head_units(run, N, dim, dest, ch0, rot, cos, sin, gain, name=None):
        u = Stage("heads", run=add(run), name=name, N=N, dim=dim, dest=dest, ch0=ch0, rot=rot, cos=cos, sin=sin, gain=gain, h=norms[-1])
        n = run.n
        u.takes(head_tables=1 if gain else 0, head_kept=n, head_squares=n if dim else 0, head_sums=n if dim else 0,
                head_log=n if dim else 0, head_rstd=n if dim else 0, head_rotated=n, head_cos=n, head_summed=n, head_done=n)
        return u

    def value_units(run, tiles, dest):
        return Stage("values", run=add(run), tiles=tiles, dest=dest, h=norms[-1])

    def soft(items, scale, v, out, per, waits, swap=False, filler=None):
        n = len(items)
        return Stage("soft", items=items, scale=scale, v=v, out=out, per=per, waits=waits, swap=swap, filler=filler).takes(
            s_scores=n, s_masked=n, s_max=n, s_neg=n, s_probs=n, s_sink=n if items[0]["sink"] is not None else 0,
            s_total=n if items[0]["sink"] is not None else 0, s_rcp=n, s_attn=n, s_turned=n,
            s_copied=n, s_chunk=n // per, s_hi=n // per, s_out=n // per, s_swap=2 if swap else 0, s_swapped=2 if swap else 0)

    def plan_layer0():
        statistics(BOTH, None)
        ada(0, range(0, 2))
        norm(BOTH, None, mod=(0, 0))
        x = ffn(BOTH, pre_wi[0], pre_wo[0], (0, 2), between=lambda: ada(0, range(2, 5)))
        norm(BOTH, x, mod=(0, 1), before="heads")
        head_units(Run("dq", 4, KC, 2 * P, cols_of(a_w_qkv[0], 0, 2 * P), "dve"), BOTH, HD, "qk", 0, "rot_axial",
                   "cos_axial", "sin_axial", "a_q_gain")
        dk = head_units(Run("dk", 4, KC, 2 * P, cols_of(a_w_qkv[0], D, 2 * P), "dve"), BOTH, HD, "qk", KC, "rot_axial",
                        "cos_axial", "sin_axial", "a_k_gain")
        dv = value_units(Run("dv", 4, KC, 2 * P, cols_of(a_w_qkv[0], 2 * D, 2 * P), "act"), 4, "v")
        fill = [ada(0, range(5, 9), True), ada(1, range(0, 5), True)]
        s = Stage("diff", waits=[("head_done", dk.b["head_done"] + 4), ("psum_read_act", dv.run.f0 + 4)], filler=fill)
        s.takes(scores_ready=2 * NI, score_max=2 * NI, neg_max=NI, probs_ready=2 * NI, prob_sums=NI, prob_scales=NI,
                prob2_scaled=NI, attn_ready=NI, attn_turned=NI, turned_copied=NI, out_head=A_HEADS, out_kept=A_HEADS,
                lam_step=4, lam_exp=1, out_squares=A_HEADS, out_sums=A_HEADS, out_log=A_HEADS, out_rstd=A_HEADS, out_full=A_HEADS, out_hi=A_HEADS, out_ready=A_HEADS)
        run = add(Run("dwo", 4, KC, 2 * P, cols_of(a_w_o[0], 0, 2 * P), "dve"))
        Stage("proj", run=run, N=BOTH, gate=(0, 5), x="h", ready=("out_ready", s.b["out_ready"]))
        norm(BOTH, residual_of(run, 2), mod=(0, 2))
        return ffn(BOTH, post_wi[0], post_wo[0], (0, 8))

    def plan_layer1(x):
        norm(BOTH, x, mod=(1, 0))
        x = ffn(BOTH, pre_wi[1], pre_wo[1], (1, 2))
        norm(BOTH, x, mod=(1, 1), before="heads")
        head_units(Run("gq", 4, KC, 2 * P, cols_of(b_w_qkv[0], 0, 2 * P), "dve"), SEQ, HD, "gq", 0, "rot_axial",
                   "cos_axial", "sin_axial", "b_q_gain")
        k = head_units(Run("gk", 1, KC, 2 * P, cols_of(b_w_qkv[0], D, 2 * P), "dve"), BOTH, HD, "gk", 0, "rot_axial",
                       "cos_axial", "sin_axial", "b_k_gain")
        v = value_units(Run("gv", 1, KC, 2 * P, cols_of(b_w_qkv[0], D + B_KV_HEADS * HD, 2 * P), "act"), 4, "gv")
        fill = [ada(1, range(5, 9), True)]
        items = []
        for h in range(B_Q_HEADS):
            kv, side = h // B_GROUP, h % 2
            half = slice(side * HD, (side + 1) * HD)
            kc = kv // 2 + (0 if kv % 2 == side else 2)
            for q in range(SEQ // P):
                items.append(dict(q=("gq", half, h // 2, q), k=("gk", half, kc, BOTH), mask=("band", q), sink=h,
                                  tiles=4, v=slice(kv * HD, (kv + 1) * HD), lanes=half))
        s = soft(items, HD ** -0.5, "gv", "h", 4, [("head_done", k.b["head_done"] + 1), ("psum_read_act", v.run.f0 + 1)],
                 swap=True, filler=fill)
        run = add(Run("gwo", 4, KC, 2 * P, cols_of(b_w_o[0], 0, 2 * P), "dve"))
        Stage("proj", run=run, N=SEQ, gate=(1, 5), x="h", ready=("s_out", s.b["s_out"]))
        norm(SEQ, residual_of(run, 2), mod=(1, 2))
        Stage("angles").takes(angle_step=4 * 8 + 3, angle_done=4)
        return ffn(SEQ, post_wi[1], post_wo[1], (1, 8))

    def plan_second(l, x):
        w = w_in[l]
        nt = SEQ // P
        norm(SEQ, x, gain=f"g_mix{l}", before="glu")
        h = norms[-1]
        g = Stage("glu", run=add(Run("glu", 4, KC, 2 * P, two_of(w, OFF["glu"], w, OFF["glu"] + 512), "dve", 2)), l=l, h=h)
        g.takes(glu_sig=4, conv_pad=1, conv_first=2 * CB_TAPS, conv_steps=CB_TAPS, conv_steps_product=CB_TAPS - 1)
        c = Stage("cc", pair=add(Run("cc", 4, KC, 2 * P, two_of(w, OFF["cc"] + 512, w, OFF["cc"] + 1024), "dve", 2)),
                  run=add(Run("cb", 2, KC, 2 * P, cols_of(w, OFF["cc"], 2 * P), "act")), l=l, h=h)
        c.conv = g
        c.takes(cc_gate=4, cc_pad=1, cc_steps=CC_TAPS, cc_steps_product=CC_TAPS - 1, cc_full=4, cc_hi=4, cc_out=4)
        head_units(Run("aq", 2, KC, 2 * P, cols_of(w, OFF["aq"], 2 * P), "dve"), SEQ, P, "aq", 0, "rot_part128", "cos128",
                   "sin128", f"g_qa{l}", "first")
        head_units(Run("ak", 2, KC, 2 * P, cols_of(w, OFF["ak"], 2 * P), "dve"), SEQ, P, "ak", 0, "rot_part128", "cos128",
                   "sin128", f"g_ka{l}")
        head_units(Run("iq", 1, KC, 2 * P, cols_of(w, OFF["iq"], 2 * P), "dve"), SEQ, None, "iq", 0, "rot_part64", "cos64",
                   "sin64", None)
        k = head_units(Run("ik", 1, KC, P, lambda j: [
            (col, w.rearrange("(k p) m -> p k m", p=P)[:, :, OFF["ik"]:OFF["ik"] + HD]) for col in (0, HD)], "dve", 2), SEQ, HD,
            "ik", 0, "rot_part64", "cos64", "sin64", f"g_kidx{l}")
        iw = Stage("iw", run=add(Run("iw", 1, KC, HEADS2, cols_of(w, OFF["iw"], HEADS2), "act")), h=h)
        v = value_units(Run("av", 2, KC, 2 * P, cols_of(w, OFF["av"], 2 * P), "act"), 2, "av")
        sel = Stage("select", waits=[("head_done", k.b["head_done"] + 1), ("psum_read_act", v.run.f0 + 2)], iw=iw)
        sel.takes(idx_scores=nt * HEADS2, idx_relu=nt * HEADS2, idx_sum=nt * HEADS2, top_steps=nt * 22, sel_mask=nt)
        branch_read = []
        q = Stage("plain", run=add(Run("sq", 4, KC, 2 * P, cols_of(w, OFF["sb"], 2 * P), "act")), h=h,
                  waits=[("idx_relu", sel.b["idx_relu"] + nt * HEADS2)])
        v2 = value_units(Run("sv", 2, KC, 2 * P, cols_of(w, OFF["sb"] + 1024, 2 * P), "act"), 2, "sv")
        gates = Stage("gates", runs=[add(Run("gate", 4, KC, 2 * P, cols_of(w, OFF["gate"] + i * D, 2 * P), "act"))
                                     for i in range(2)], i=0, l=l, h=h)
        sel.runs = [q.run, v2.run] + gates.runs
        q.filler = v2.filler = gates.filler = sel
        items = [dict(q=("aq", slice(0, P), hd, q_), k=("ak", slice(0, P), hd, SEQ), mask=("sel", q_), sink=None, tiles=2,
                      v=slice(hd * P, (hd + 1) * P), lanes=slice(0, P), needs=("sel_mask", sel.b["sel_mask"] + q_ + 1))
                 for hd in range(HEADS2) for q_ in range(nt)]
        gate_last = gates.runs[-1]
        a = soft(items, P ** -0.5, "av", "oa", nt, [(gate_last.free, gate_last.f0 + 4)])
        t = Stage("stick", waits=[("s_out", a.b["s_out"] + HEADS2)])
        t.takes(**{n: HEADS2 for n in ("z_ready", "z_kept", "z_neg", "z_exp", "z_log", "z_soft", "z_soft_m", "z_sums", "z_arg",
                                       "z_arg_m", "z_attn", "z_out", "od_hi", "od_out")})
        n = Stage("layernorm", l=l, waits=[("od_out", t.b["od_out"] + HEADS2), ("conv_steps", g.b["conv_steps"] + CB_TAPS),
                                              ("conv_first", g.b["conv_first"] + 2 * CB_TAPS)])
        n.takes(ln_sum=1, ln_mean=1, ln_mid=4, ln_sq=4, ln_var=1, ln_log=1, ln_rstd=1, ln_out=4, ln_act=4, ln_hi=4, ob_out=4)
        done = dict(oa=("s_out", a.b["s_out"] + 4), ob=("ob_out", n.b["ob_out"] + 4), oc=("cc_out", c.b["cc_out"] + 4),
                    od=("od_out", t.b["od_out"] + 4))
        for i, (name, wo) in enumerate((("oa", w_oa), ("ob", w_ob), ("oc", w_oc), ("od", w_od))):
            if i >= 2:
                Stage("gates", runs=[add(Run("gate", 4, KC, 2 * P, cols_of(w, OFF["gate"] + i * D, 2 * P), "act"))], i=i, l=l,
                      waits=branch_read[i - 2], h=h)
            br = Stage("branch", i=i, l=l, x=name, run=add(Run("wo", 4, 4, 2 * P, cols_of(wo[l], 0, 2 * P, 0, 4), "dve")),
                       waits=[done[name]])
            br.takes(merged=4)
            branch_read.append([(br.run.free, br.run.f0 + 4)])
        m = Stage("merge", ready=("merged", br.b["merged"])).takes(m_hi=KC, m_lo=KC)
        run = add(Run("merge", 4, KC, 2 * P, cols_of(w_merge[l], 0, 2 * P), "dve"))
        Stage("proj", run=run, N=SEQ, x="h", ready=("m_lo", m.b["m_lo"]))
        norm(SEQ, residual_of(run, 2), gain=f"g_ffn{l}", before="conv_in")
        for half in range(2):
            wi_run = add(Run("wi", HALF, KC, 2 * P, two_of(w_gate[l], half * HALF * P, w_up[l], half * HALF * P), "dve", 2))
            f = Stage("conv_in", run=wi_run, l=l, i=half, h=norms[-1])
            f.takes(cin_pad=1, cin_ready=HALF, tap0=HALF, tap1=HALF, tap2=HALF, silu_ready=HALF, act_hi=HALF, act_lo=HALF)
            wo_run = add(Run("wd", KC, HALF, P, cols_of(w_down[l], 0, P, half * HALF, HALF), "dve"))
            Stage("proj", run=wo_run, N=SEQ, x="act", ready=("act_lo", f.b["act_lo"]))
        return residual_of(wo_run, 1)

    x_at = plan_layer0()
    if stop != "layer0":
        x_at = plan_layer1(x_at)
    if stop not in ("layer0", "layer1"):
        for l in range(1 if stop == "second0" else DEPTH):
            x_at = plan_second(l, x_at)

    base = (nc.sbuf_base + 63) // 64 * 64
    at = [base]

    def place(name, shape, where=None, dt=F32):
        n = 1
        for d in shape:
            n *= d
        if where is None:
            where = at[0]
            at[0] += (n * 4 + 63) // 64 * 64
        t = nc.alloc_sbuf_tensor_at(name, [P, n], dt, offset=where)
        return t[:, :] if len(shape) == 1 else t[:, :].rearrange("p (a n) -> p a n", a=shape[0])

    raw = [place(f"raw{i}", (SLOT,)) for i in range(RING)]
    w_hi = [place(f"w_hi{i}", (SLOT,), dt=F32R) for i in range(RING)]
    w_lo = [place(f"w_lo{i}", (SLOT,), dt=F32R) for i in range(RING)]
    xs = place("xs", (KC, BOTH))
    h_at = at[0]
    h_hi, h_lo = place("h_hi", (KC, BOTH), dt=F32R), place("h_lo", (KC, BOTH), dt=F32R)
    vec_sb, con_sb = place("vec_sb", (N_VEC,)), place("con_sb", (N_CON,))
    mod_sb = [place(f"mod_sb{i}", (MODC, 2)) for i in range(DEPTH)]
    cond, cond_halves = place("cond", (KC, 2)), place("cond_halves", (KC, 4), dt=F32R)
    stats = place("stats", (64,))
    pos_i = place("pos_i", (1, SEQ), dt=I32)
    arena = at[0]
    ARENA = 48 * 1024

    def over(name, at_kb, shape, dt=F32):
        return place(name, shape, arena + int(at_kb * 1024), dt)

    act_hi, act_lo = over("act_hi", 0, (HALF, BOTH), F32R), over("act_lo", 22, (HALF, BOTH), F32R)
    qk, v_lat = over("qk", 0, (2 * KC, BOTH)), over("v_lat", 32, (4, D))
    gq, gk, gv = over("gq", 0, (KC, SEQ)), over("gk", 8, (4, BOTH)), over("gv", 16, (4, B_KV_HEADS * HD))
    gates_sb = over("gates_sb", 0, (2 * KC, SEQ))
    branch = {n: tuple(over(f"{n}_{half}", 16 + 8 * i + 4 * k, (4, SEQ), F32R) for k, half in enumerate(("hi", "lo")))
              for i, n in enumerate(("oa", "ob", "oc", "od"))}
    cb_in, cb_sum = over("cb_in", 16, (4, SEQ + CB_TAPS - 1)), over("cb_sum", 28, (4, SEQ))
    cc_b, cc_sum = over("cc_b", 32, (4, SEQ)), over("cc_sum", 36, (4, SEQ))
    cb_product, cc_product = over("cb_product", 36, (4, SEQ)), over("cc_product", 16, (4, SEQ))
    cc_in = over("cc_in", 40, (4, SEQ + CC_TAPS - 1))
    iq, ik, iw_sb = over("iq", 44.25, (2, SEQ)), over("ik", 46.25, (1, SEQ)), over("iw_sb", 47.25, (2, HEADS2))
    spare = [place(f"spare{i}", (KC, BOTH), h_at + i * KC * BOTH * 4)[:, :, SEQ:BOTH] for i in range(2)]
    sqk, aq, ak = spare[0], spare[1][:, 0:4, :], spare[1][:, 4:8, :]
    merged = sqk
    at[0] += ARENA
    temp = at[0]
    TEMP = 23040

    def tmp(name, at_kb, shape, dt=F32):
        return place(name, shape, temp + int(at_kb * 1024), dt)

    sq, rstd, scaled = tmp("sq", 0, (4, BOTH)), tmp("rstd", 8, (BOTH,)), tmp("scaled", 10, (2, BOTH))
    sil = tmp("sil", 0, (RING, BOTH))
    square_sum = scaled[:, 0, :]
    kept, hr, rope_t = tmp("kept", 8, (4, BOTH)), tmp("hr", 16, (2, BOTH)), tmp("rope_t", 20, (2, SEQ))
    rot_g, rows = tmp("rot_g", 22, (P,)), tmp("rows", 18, (D,))
    full = tmp("full", 14, (RING, BOTH))
    probs, attn, attn_t = tmp("probs", 0, (4, BOTH)), tmp("attn", 8, (2, BOTH)), tmp("attn_t", 12, (2, BOTH))
    prob2, logits = tmp("prob2", 16, (BOTH,)), tmp("logits", 4, (2, BOTH))
    lam_t = tmp("lam_t", 12, (2, HD))
    rel, idx, idx_work = tmp("rel", 0, (HEADS2, SEQ)), tmp("idx", 4, (2, SEQ)), tmp("idx_work", 6, (2, SEQ))
    sel_gt, sel_eq, sel_cum = tmp("sel_gt", 8, (2, SEQ)), tmp("sel_eq", 10, (2, SEQ)), tmp("sel_cum", 12, (2, SEQ))
    sel_mask = tmp("sel_mask", 16, (2, SEQ))
    z_s, z_e, z_l, z_m, z_a = (tmp(f"z_{i}", 4 * i, (2, BOTH)) for i in range(5))
    ln_t, ln_stat = tmp("ln_t", 0, (4, SEQ)), tmp("ln_stat", 4, (2, SEQ))
    tap_t, cin = tmp("tap_t", 6, (RING, SEQ)), tmp("cin", 16, (RING, SEQ + CC_TAPS - 1))
    gated_t = tmp("gated_t", 16, (2, SEQ))
    ang = tmp("ang", 14, (8, SEQ))
    at[0] += TEMP
    assert at[0] <= nc.sbuf_usable_end, (at[0], nc.sbuf_usable_end)

    ps = [nc.alloc_psum_tensor(f"ps{i}", [P, 2, 512], F32) for i in range(RING)]
    pm = nc.alloc_psum_tensor("pm", [P, 2, 512], F32)
    bank = [ps[i // 2][:, i % 2, :] for i in range(6)]
    ADA_BANKS, ADA_FILL_BANK = [pm[:, 1, :], pm[:, 0, :]], [bank[5]]

    def vec(name, c=None):
        o, w = VEC[name]
        return vec_sb[:, o:o + w] if c is None else vec_sb[:, o + c:o + c + 1]

    ANGLES = ["cos128", "sin128", "cos64", "sin64"]
    o = CON["cos_axial"][0]
    angles = con_sb[:, o:o + 4 * SEQ].rearrange("p (a n) -> p a n", a=4)

    def con(name):
        if name in ANGLES:
            return angles[:, ANGLES.index(name), :]
        o, w = CON[name]
        return con_sb[:, o:o + w]

    landed_sem = [nc.alloc_semaphore(f"raw_landed{i}") for i in range(RING)]
    S = {name: nc.alloc_semaphore(name) for name in counts}
    x_landed, vec_landed, con_landed, out_stored, cond_ready, cond_hi_ready, cond_lo_ready = (nc.alloc_semaphore(n) for n in (
        "x_landed", "vec_landed", "con_landed", "out_stored", "cond_ready", "cond_hi_ready", "cond_lo_ready"))

    landed, per_slot = [], [0] * RING
    for t, r in enumerate(r for r in runs for _ in range(r.n)):
        per_slot[t % RING] += 16 * r.dmas
        landed.append(per_slot[t % RING])

    def sweep(eng, run, body):
        turns = (run.n - RING - 2) // RING
        if turns < 2:
            for j in range(run.n):
                body(Unit(run, j))
            return
        for j in range(RING):
            body(Unit(run, j))
        with eng.Fori(0, turns) as turn:
            for r in range(RING):
                body(Unit(run, RING + r, turn))
        for j in range(RING + turns * RING, run.n):
            body(Unit(run, j))

    def landed_at(u):
        count = landed[u.t0]
        return count if u.turn is None else u.turn * (16 * u.run.dmas) + count

    def next_split(u):
        if u.t0 + 2 >= len(units):
            return None
        run, j = units[u.t0 + 2]
        assert u.turn is None or run is u.run
        return Unit(run, j, u.turn)

    BUF = dict(qk=qk, gq=gq, gk=gk, aq=aq, ak=ak, iq=iq, ik=ik)
    VALUES = dict(v=v_lat, gv=gv)
    XS_VALUES = dict(av=0, sv=4)

    def values_of(name, k, cols):
        if name in VALUES:
            return VALUES[name][:, k, cols]
        at_col = SEQ + cols.start % SEQ
        return xs[:, XS_VALUES[name] + 2 * k + cols.start // SEQ, at_col:at_col + cols.stop - cols.start]

    def x_of(s):
        return dict(h=(h_hi, h_lo), act=(act_hi, act_lo), **branch)[s.x or "h"]

    def dest_of(s, ch):
        return BUF[s.dest][:, s.ch0 + ch, :]

    def mask_of(item):
        kind, q = item["mask"]
        return sel_mask[:, q, :] if kind == "sel" else con("band")[:, q * SEQ:(q + 1) * SEQ]

    def out_of(s, chunk):
        return tuple(t[:, chunk, 0:SEQ] for t in ((h_hi, h_lo) if s.out == "h" else branch[s.out]))

    def waits_of(eng, s):
        for name, count in s.waits:
            eng.wait_ge(S[name], count)

    block = nc.Block()
    with block:
        @block.sync
        def _(sp):
            sp.dma_start(vec_sb, vecs[:, :]).then_inc(vec_landed, 16)

            def load(u):
                run = u.run
                if u.t0 >= RING:
                    sp.wait_ge(lo_ready, u.count - RING)
                dst = raw[u.slot][:, 0:run.kc * run.cols].rearrange("p (k m) -> p k m", k=run.kc)
                for c0, src in run.src(u.j):
                    sp.dma_start(dst[:, :, c0:c0 + src.shape[2]], src).then_inc(landed_sem[u.slot], 16)
                if u.turn is None and u.t0 == RING - 1:
                    sp.dma_start(xs, x_t.rearrange("(c p) n -> p c n", p=P)).then_inc(x_landed, 16)
                    sp.dma_start(con_sb, consts[:, :]).then_inc(con_landed, 16)
                    sp.dma_start(pos_i[:, 0, :], positions[:, :]).then_inc(con_landed, 16)

            for run in runs:
                sweep(sp, run, load)
            sp.wait_ge(S["psum_read_dve"], counts["psum_read_dve"])
            sp.dma_start(out.rearrange("(c p) n -> p c n", p=P), xs[:, :, 0:SEQ]).then_inc(out_stored, 16)
            sp.wait_ge(out_stored, 16)

        @block.tensor
        def _(pe):
            def open_unit(u):
                pe.wait_ge(lo_ready, u.count)
                if u.run.by is None or u.t0 < RING or psum_users[u.t0 - RING] is None:
                    return
                free, count = psum_users[u.t0 - RING]
                if u.turn is None:
                    pe.wait_ge(S[free], count)
                else:
                    pe.wait_ge(S[u.run.free], u.out - RING)

            def weights(buf, u, k, m0, width):
                at_k = k * u.run.cols + m0
                return buf[:, at_k:at_k + width]

            def dense(u, N, x, ready=None):
                run = u.run
                x_hi, x_lo = x
                open_unit(u)
                first = ready is not None and u.turn is None and u.j0 == 0
                blocks = range(run.cols // P)
                for k, m in [(k, m) for k in range(run.kc) for m in blocks] if first else [(k, m) for m in blocks for k in range(run.kc)]:
                    if first and m == 0:
                        pe.wait_ge(S[ready[0]], ready[1] + k + 1)
                    o = ps[u.slot][:, m, 0:N]
                    hi = weights(w_hi[u.slot], u, k, m * P, P)
                    pe.matmul(o, hi, x_hi[:, k, 0:N], start=k == 0, stop=False)
                    pe.matmul(o, hi, x_lo[:, k, 0:N], start=False, stop=False)
                    last = pe.matmul(o, weights(w_lo[u.slot], u, k, m * P, P), x_hi[:, k, 0:N], start=False, stop=k == run.kc - 1)
                last.then_inc(unit_done, 1)

            def ada_step(s, k, banks):
                kind, j, _ = s.steps[k]
                o = banks[k % len(banks)]
                if k >= len(banks):
                    name, count = s.steps[k - len(banks)][2]
                    pe.wait_ge(S[name], count)
                elif s.b["mods_summed"]:
                    pe.wait_ge(S["mods_summed"], s.b["mods_summed"])
                if kind == "row":
                    u = Unit(s.run, j)
                    open_unit(u)
                    for c in range(KC):
                        hi, lo = (weights(w[u.slot], u, c, 0, 2 * P) for w in (w_hi, w_lo))
                        if c:
                            pe.matmul(o[0:2, 0:2 * P], cond_halves[:, c - 1, 0:2], lo_before, start=False, stop=False)
                        if c == KC - 1:
                            pe.matmul(o[0:2, 0:2 * P], cond_halves[:, c, 0:2], lo, start=False, stop=False)
                        last = pe.matmul(o[0:4, 0:2 * P], cond_halves[:, c, :], hi, start=c == 0, stop=c == KC - 1)
                        lo_before = lo
                    last.then_inc(unit_done, 1)
                    return
                name, count = s.steps[k - 1][2]
                pe.wait_ge(S[name], count)
                for c in range(KC):
                    last = pe.matmul(o[:, 2 * c:2 * c + 2], rows[0:4, c * P:(c + 1) * P], con("fold")[0:4, :], start=True, stop=True)
                last.then_inc(S["ada_turned"], 1)

            def ada(s):
                if not s.filler:
                    pe.wait_ge(cond_lo_ready, 1)
                    pe.wait_ge(con_landed, 32)
                    if s.b["log_ready"]:
                        pe.wait_ge(S["log_ready"], s.b["log_ready"])
                    for k in range(len(s.steps)):
                        ada_step(s, k, ADA_BANKS)

            def fill(s, i, n):
                for a, k in share(s, i, n):
                    ada_step(a, k, ADA_FILL_BANK)

            def statistics(s):
                N, b = s.N, s.b
                pe.wait_ge(con_landed, 32)
                if b["mods_summed"]:
                    pe.wait_ge(S["mods_summed"], b["mods_summed"])
                pe.wait_ge(S["square_added"], b["square_added"] + KC)
                pe.matmul(pm[:, 0, 0:N], con("ones"), square_sum[:, 0:N], start=True, stop=True).then_inc(S["square_summed"], 1)

            def dense_run(s):
                ready = s.h if s.ready is None else s.ready
                waits_of(pe, s)
                sweep(pe, s.run, lambda u: dense(u, s.N, x_of(s), ready))

            def heads(s):
                run, N, b = s.run, s.N, s.b
                nm = run.cols // P
                for j in range(run.n + 1):
                    if j < run.n:
                        dense(Unit(run, j), N, (h_hi, h_lo), s.h)
                    if not j:
                        continue
                    i = j - 1
                    if s.dim:
                        pe.wait_ge(S["head_squares"], b["head_squares"] + j)
                        if b["head_log"] + i:
                            pe.wait_ge(S["head_log"], b["head_log"] + i)
                        ones = con("blocks" if s.dim == HD else "ones")
                        for m in range(nm):
                            last = pe.matmul(pm[:, m, 0:N], ones, sq[:, 2 * ((b["head_done"] + i) % 2) + m, 0:N], start=True, stop=True)
                        last.then_inc(S["head_sums"], 1)
                    if s.gain and not i:
                        pe.wait_ge(S["head_tables"], b["head_tables"] + 1)
                    pe.wait_ge(S["head_kept"], b["head_kept"] + j)
                    for m in range(nm):
                        last = pe.matmul(ps[Unit(run, i).slot][:, 0, m * SEQ:(m + 1) * SEQ], rot_g if s.gain else con(s.rot),
                                         kept[:, 2 * ((b["head_done"] + i) % 2) + m, 0:SEQ], start=True, stop=True)
                    last.then_inc(S["head_rotated"], 1)

            def values(s):
                run = s.run
                for j in range(run.n):
                    u = Unit(run, j)
                    open_unit(u)
                    for i in range(s.tiles):
                        o = ps[u.slot][:, i // 2, (i % 2) * run.cols:(i % 2 + 1) * run.cols]
                        tok = slice(i * P, (i + 1) * P)
                        for k in range(KC):
                            hi, lo = (weights(w[u.slot], u, k, 0, run.cols) for w in (w_hi, w_lo))
                            pe.matmul(o, h_hi[:, k, tok], hi, start=k == 0, stop=False)
                            pe.matmul(o, h_hi[:, k, tok], lo, start=False, stop=False)
                            last = pe.matmul(o, h_lo[:, k, tok], hi, start=False, stop=k == KC - 1)
                    last.then_inc(unit_done, 1)

            def diff(s):
                b = s.b
                waits_of(pe, s)

                def keys(qt):
                    return slice(0, BOTH) if qt < 2 else slice(SEQ, BOTH)

                def scores(i):
                    h, qt = divmod(i, 4)
                    if i >= 2:
                        pe.wait_ge(S["probs_ready"], b["probs_ready"] + 2 * (i - 1))
                    for c in range(2):
                        half = slice(c * HD, (c + 1) * HD)
                        n = keys(qt).stop - keys(qt).start
                        pe.matmul(bank[2 * (i % 2) + c][:, 0:n], qk[half, h, qt * P:(qt + 1) * P],
                                  qk[half, KC + h, keys(qt)], start=True, stop=True).then_inc(S["scores_ready"], 1)

                def turn(i):
                    n = 4 if i % 4 < 2 else 2
                    pe.wait_ge(S["attn_ready"], b["attn_ready"] + i + 1)
                    if i:
                        pe.wait_ge(S["turned_copied"], b["turned_copied"] + i)
                    for k in range(n):
                        last = pe.transpose(bank[4][:, k * P:(k + 1) * P], attn[:, i % 2, k * P:(k + 1) * P], con("ident"))
                    last.then_inc(S["attn_turned"], 1)

                def weigh(i):
                    h, qt = divmod(i, 4)
                    pe.wait_ge(S["turned_copied"], b["turned_copied"] + i + 1)
                    if qt == 0 and h >= 2:
                        pe.wait_ge(S["out_kept"], b["out_kept"] + h - 1)
                    tiles = range(4) if qt < 2 else range(2, 4)
                    for n, k in enumerate(tiles):
                        last = pe.matmul(pm[:, h % 2, qt * P:(qt + 1) * P], v_lat[:, k, h * P:(h + 1) * P],
                                         attn_t[:, i % 2, n * P:(n + 1) * P], start=n == 0, stop=n == len(tiles) - 1)
                    if qt == 3:
                        last.then_inc(S["out_head"], 1)

                scores(0)
                scores(1)
                for i in range(NI):
                    fill(s, i, NI)
                    turn(i)
                    if i:
                        weigh(i - 1)
                    if i + 2 < NI:
                        scores(i + 2)
                weigh(NI - 1)
                for h in range(A_HEADS):
                    pe.wait_ge(S["out_squares"], b["out_squares"] + h + 1)
                    if h >= 2:
                        pe.wait_ge(S["out_log"], b["out_log"] + h - 1)
                    pe.matmul(pm[:, h % 2, :], con("ones"), sq[:, h % 4, :], start=True, stop=True).then_inc(S["out_sums"], 1)

            def soft(s):
                b, items = s.b, s.items
                n = len(items)
                waits_of(pe, s)
                if s.swap:
                    for c in range(2):
                        pe.matmul(bank[c], con("swap"), gk[:, c, :], start=True, stop=True).then_inc(S["s_swap"], 1)
                    pe.wait_ge(S["s_swapped"], b["s_swapped"] + 2)

                def scores(i):
                    it = items[i]
                    (qb, lanes, qc, q), (kb, _, kc, nk) = it["q"], it["k"]
                    if i >= 3:
                        pe.wait_ge(S["s_masked"], b["s_masked"] + i - 2)
                    pe.matmul(bank[i % 3][:, 0:nk], BUF[qb][lanes, qc, q * P:(q + 1) * P], BUF[kb][lanes, kc, 0:nk],
                              start=True, stop=True).then_inc(S["s_scores"], 1)

                def turn(i):
                    pe.wait_ge(S["s_attn"], b["s_attn"] + i + 1)
                    if i >= 2:
                        pe.wait_ge(S["s_copied"], b["s_copied"] + i - 1)
                    for k in range(items[i]["tiles"]):
                        last = pe.transpose(bank[3 + i % 2][:, k * P:(k + 1) * P], attn[:, i % 2, k * P:(k + 1) * P],
                                            con("ident"))
                    last.then_inc(S["s_turned"], 1)

                def weigh(i):
                    it = items[i]
                    q = it["q"][3]
                    chunk = i // s.per
                    pe.wait_ge(S["s_copied"], b["s_copied"] + i + 1)
                    if i % s.per == 0 and chunk >= 2:
                        pe.wait_ge(S["s_out"], b["s_out"] + chunk - 1)
                    for k in range(it["tiles"]):
                        last = pe.matmul(pm[it["lanes"], chunk % 2, q * P:(q + 1) * P], values_of(s.v, k, it["v"]),
                                         attn_t[:, i % 2, k * P:(k + 1) * P], start=k == 0, stop=k == it["tiles"] - 1)
                    if i % s.per == s.per - 1:
                        last.then_inc(S["s_chunk"], 1)

                for i in range(min(2, n)):
                    scores(i)
                for i in range(n):
                    if i + 2 < n:
                        scores(i + 2)
                    fill(s, i, n)
                    turn(i)
                    if i:
                        weigh(i - 1)
                weigh(n - 1)

            def iw(s):
                u = Unit(s.run, 0)
                open_unit(u)
                for i in range(2):
                    o = ps[u.slot][:, 0, i * HEADS2:(i + 1) * HEADS2]
                    tok = slice(i * P, (i + 1) * P)
                    for k in range(KC):
                        hi, lo = (weights(w[u.slot], u, k, 0, HEADS2) for w in (w_hi, w_lo))
                        pe.matmul(o, h_hi[:, k, tok], hi, start=k == 0, stop=False)
                        pe.matmul(o, h_hi[:, k, tok], lo, start=False, stop=False)
                        last = pe.matmul(o, h_lo[:, k, tok], hi, start=False, stop=k == KC - 1)
                last.then_inc(unit_done, 1)

            def select(s):
                b = s.b
                waits_of(pe, s)
                for q in range(2):
                    for h in range(HEADS2):
                        half = slice(h % 2 * HD, (h % 2 + 1) * HD)
                        if q:
                            pe.wait_ge(S["idx_relu"], b["idx_relu"] + h + 1)
                        pe.matmul(bank[h][:, 0:SEQ], iq[half, h // 2, q * P:(q + 1) * P], ik[half, 0, :], start=True,
                                  stop=True).then_inc(S["idx_scores"], 1)

            def cc(s):
                sweep(pe, s.pair, lambda u: dense(u, SEQ, (h_hi, h_lo)))
                sweep(pe, s.run, lambda u: dense(u, SEQ, (h_hi, h_lo)))

            def gates(s):
                for run in s.runs:
                    sweep(pe, run, lambda u: dense(u, SEQ, (h_hi, h_lo)))

            def stick(s):
                b = s.b
                waits_of(pe, s)

                def scores(h):
                    if h >= 2:
                        pe.wait_ge(S["z_kept"], b["z_kept"] + h - 1)
                    for k in range(2):
                        last = pe.matmul(bank[h % 2][:, k * SEQ:(k + 1) * SEQ], sqk[:, 4 + h, k * P:(k + 1) * P], sqk[:, h, :],
                                         start=True, stop=True)
                    last.then_inc(S["z_ready"], 1)

                def sums(h):
                    pe.wait_ge(S["z_soft_m"], b["z_soft_m"] + h + 1)
                    if h >= 2:
                        pe.wait_ge(S["z_arg"], b["z_arg"] + h - 1)
                    m = z_m[:, h % 2, :]
                    o = bank[2 + h % 2]
                    pe.matmul(o[:, 0:SEQ], con("suffix"), m[:, 0:SEQ], start=True, stop=False)
                    pe.matmul(o[:, 0:SEQ], con("ones"), m[:, SEQ:], start=False, stop=True)
                    pe.matmul(o[:, SEQ:], con("suffix"), m[:, SEQ:], start=True, stop=True).then_inc(S["z_sums"], 1)

                def weigh(h):
                    pe.wait_ge(S["z_attn"], b["z_attn"] + h + 1)
                    if h >= 2:
                        pe.wait_ge(S["od_out"], b["od_out"] + h - 1)
                    for k in range(2):
                        last = pe.matmul(pm[:, h % 2, 0:SEQ], values_of("sv", k, slice(h * P, (h + 1) * P)),
                                         z_a[:, h % 2, k * SEQ:(k + 1) * SEQ], start=k == 0, stop=k == 1)
                    last.then_inc(S["z_out"], 1)

                scores(0)
                for h in range(HEADS2):
                    if h + 1 < HEADS2:
                        scores(h + 1)
                    sums(h)
                    if h:
                        weigh(h - 1)
                weigh(HEADS2 - 1)

            def layernorm(s):
                b = s.b
                waits_of(pe, s)
                for c in range(4):
                    last = pe.matmul(pm[:, 0, 0:SEQ], con("ones"), cb_sum[:, c, :], start=c == 0, stop=c == 3)
                last.then_inc(S["ln_sum"], 1)
                for c in range(4):
                    pe.wait_ge(S["ln_sq"], b["ln_sq"] + c + 1)
                    last = pe.matmul(pm[:, 1, 0:SEQ], con("ones"), ln_t[:, c, :], start=c == 0, stop=c == 3)
                last.then_inc(S["ln_var"], 1)

            def branch_out(s):
                waits_of(pe, s)
                sweep(pe, s.run, lambda u: dense(u, SEQ, x_of(s)))

            todo = dict(ada=ada, statistics=statistics, ffn_in=dense_run, proj=dense_run, heads=heads, values=values, diff=diff, soft=soft,
                        iw=iw, select=select, glu=dense_run, cc=cc, plain=dense_run, gates=gates, stick=stick,
                        layernorm=layernorm, branch=branch_out, conv_in=dense_run)
            for s in stages:
                if s.kind in todo:
                    todo[s.kind](s)

        @block.scalar
        def _(act):
            LOG_EXP = "natural_log_exp_and_others"

            def rsqrt(o, mean_square, log_signal, log_count, signal):
                nc.scalar.activation(o, mean_square, ACT.Ln, bias=con("eps")).then_inc(S[log_signal], 1)
                act.wait_ge(S[log_signal], log_count)
                nc.scalar.activation(o, o, ACT.Exp, scale=-0.5).then_inc(S[signal], 1)

            def split(u):
                if u is None:
                    return
                n = u.run.kc * u.run.cols
                act.wait_ge(landed_sem[u.slot], landed_at(u))
                if u.t0 >= RING:
                    act.wait_ge(unit_done, u.count - RING)
                nc.scalar.copy(w_hi[u.slot][:, 0:n], raw[u.slot][:, 0:n]).then_inc(hi_ready, 1)

            def split_ahead(u):
                split(next_split(u))

            def splits_only(s):
                sweep(act, s.run, split_ahead)

            def ada_row(s, k, banks):
                kind, j, _ = s.steps[k]
                if kind == "row":
                    split_ahead(Unit(s.run, j))
                    act.wait_ge(unit_done, Unit(s.run, j).count)
                    i = j % PER_MOD
                    if i == 0 and s.b["ada_turned"] + j // PER_MOD:
                        act.wait_ge(S["ada_turned"], s.b["ada_turned"] + j // PER_MOD)
                    nc.scalar.copy(rows[0:4, i * 2 * P:(i + 1) * 2 * P], banks[k % len(banks)][0:4, 0:2 * P]).then_inc(S["ada_rows"], 1)

            def ada(s):
                if not s.filler:
                    for k in range(len(s.steps)):
                        ada_row(s, k, ADA_BANKS)

            def fill(s, i, n):
                for a, k in share(s, i, n):
                    ada_row(a, k, ADA_FILL_BANK)

            def statistics(s):
                N, b = s.N, s.b
                nc.scalar.preload_act_table_set(LOG_EXP)
                if s.after is None:
                    act.wait_ge(x_landed, 16)
                for c in range(KC):
                    if s.after is not None:
                        name, count = s.after(c)
                        act.wait_ge(S[name], count)
                    if c >= 4:
                        act.wait_ge(S["square_added"], b["square_added"] + c - 3)
                    nc.scalar.activation(sq[:, c % 4, 0:N], xs[:, c, 0:N], ACT.Square,
                                         scale=D ** -0.5).then_inc(S["squares_ready"], 1)
                act.wait_ge(S["square_summed"], b["square_summed"] + 1)
                rsqrt(rstd[:, 0:N], pm[:, 0, 0:N], "log_ready", b["log_ready"] + 1, "rstd_ready")

            def norm(s):
                N, b = s.N, s.b
                if s.next in ("ffn_in", "conv_in"):
                    nc.scalar.preload_act_table(ACT.Silu)
                elif s.next == "glu":
                    nc.scalar.preload_act_table(ACT.Sigmoid)
                if s.gain is not None:
                    for c in range(KC):
                        act.wait_ge(S["h_scaled"], b["h_scaled"] + c + 1)
                        nc.scalar.copy(h_hi[:, c, 0:N], full[:, c % RING, 0:N]).then_inc(S["h_hi_act"], 1)
                    return
                layer, which = s.mod
                act.wait_ge(S["mods_summed"], b["mods_summed"])
                act.wait_ge(S["mods_ready"], b["mods_ready"])
                for c in range(KC):
                    act.wait_ge(S["scaled_ready"], b["scaled_ready"] + c + 1)
                    if c >= RING:
                        act.wait_ge(S["h_lo"], b["h_lo"] + c - RING + 1)
                    for st in range(N // SEQ):
                        tok = slice(st * SEQ, (st + 1) * SEQ)
                        last = nc.scalar.activation(
                            full[:, c % RING, tok], scaled[:, c % 2, tok], ACT.Identity,
                            bias=mod_sb[layer][:, 3 * which * KC + c, st:st + 1],
                            scale=mod_sb[layer][:, (3 * which + 1) * KC + c, st:st + 1])
                    last.then_inc(S["h_modulated"], 1)

            def ffn_in(s):
                N, b, run = s.N, s.b, s.run

                def silu(u):
                    split_ahead(u)
                    act.wait_ge(unit_done, u.count)
                    if u.j0 >= RING:
                        act.wait_ge(S["act_lo"], u.j + (b["act_lo"] + 1 - RING))
                    nc.scalar.activation(sil[:, u.j0 % RING, 0:N], ps[u.slot][:, 0, 0:N],
                                         ACT.Silu).then_inc(S["silu_ready"], 1)

                sweep(act, run, silu)

            def heads(s):
                run, N, b = s.run, s.N, s.b
                nm = run.cols // P

                def deviation(i):
                    act.wait_ge(S["head_sums"], b["head_sums"] + i + 1)
                    if b["head_done"] + i:
                        act.wait_ge(S["head_done"], b["head_done"] + i)
                    rsqrt(hr[:, 0:nm, 0:N], pm[:, 0:nm, 0:N], "head_log", b["head_log"] + i + 1, "head_rstd")

                if s.name == "first":
                    nc.scalar.preload_act_table_set(LOG_EXP)
                for j in range(run.n):
                    u = Unit(run, j)
                    split_ahead(u)
                    act.wait_ge(unit_done, u.count)
                    g = b["head_done"] + j
                    if g >= 2:
                        act.wait_ge(S["head_done"], g - 1)
                    two = slice(2 * (g % 2), 2 * (g % 2) + nm)
                    nc.scalar.copy(kept[:, two, 0:N], ps[u.slot][:, 0:nm, 0:N]).then_inc(S["head_kept"], 1)
                    if s.dim:
                        act.wait_ge(S["head_kept"], b["head_kept"] + j + 1)
                        nc.scalar.activation(sq[:, two, 0:N], kept[:, two, 0:N], ACT.Square,
                                             scale=s.dim ** -0.5).then_inc(S["head_squares"], 1)
                    if s.dim and j:
                        deviation(j - 1)
                if s.dim:
                    deviation(run.n - 1)

            def values(s):
                run = s.run
                for j in range(run.n):
                    u = Unit(run, j)
                    split_ahead(u)
                    act.wait_ge(unit_done, u.count)
                    for i in range(s.tiles // 2):
                        src = ps[u.slot][:, i, :].rearrange("p (t c) -> p t c", t=2)
                        if s.dest in XS_VALUES:
                            dst = xs[:, XS_VALUES[s.dest] + j:XS_VALUES[s.dest] + 4:2, SEQ:BOTH]
                        else:
                            dst = VALUES[s.dest][:, 2 * i:2 * i + 2, j * run.cols:(j + 1) * run.cols]
                        last = nc.scalar.copy(dst, src)
                    last.then_inc(S[run.free], 1)

            def diff(s):
                b = s.b
                act.wait_ge(S["lam_step"], b["lam_step"] + 2)
                nc.scalar.activation(stats[:, 2:4], stats[:, 0:2], ACT.Exp).then_inc(S["lam_exp"], 1)

                def turned(i):
                    n = BOTH if i % 4 < 2 else CTX
                    act.wait_ge(S["attn_turned"], b["attn_turned"] + i + 1)
                    nc.scalar.copy(attn_t[:, i % 2, 0:n], bank[4][:, 0:n]).then_inc(S["turned_copied"], 1)
                    if i % 4 == 0 and i >= 4:
                        keep(i // 4 - 1)

                def keep(h):
                    act.wait_ge(S["out_head"], b["out_head"] + h + 1)
                    nc.scalar.copy(qk[:, h, :], pm[:, h % 2, :]).then_inc(S["out_kept"], 1)

                for i in range(NI):
                    n = BOTH if i % 4 < 2 else CTX
                    act.wait_ge(S["neg_max"], b["neg_max"] + i + 1)
                    if i >= 2:
                        act.wait_ge(S["attn_ready"], b["attn_ready"] + i - 1)
                    for c in range(2):
                        r = 2 * (i % 2) + c
                        nc.scalar.activation(probs[:, r, 0:n], bank[r][:, 0:n], ACT.Exp, bias=stats[:, 16 + r:17 + r],
                                             scale=HD ** -0.5, accum_out=stats[:, 20 + r:21 + r]).then_inc(S["probs_ready"], 1)
                    fill(s, i, NI)
                    if i:
                        turned(i - 1)
                turned(NI - 1)
                keep(A_HEADS - 1)
                act.wait_ge(S["out_kept"], b["out_kept"] + A_HEADS)
                for step in range(A_HEADS + 2):
                    h = step
                    if h < A_HEADS:
                        if h >= 4:
                            act.wait_ge(S["out_sums"], b["out_sums"] + h - 3)
                        nc.scalar.activation(sq[:, h % 4, :], qk[:, h, :], ACT.Square, scale=P ** -0.5).then_inc(S["out_squares"], 1)
                    h = step - 2
                    if h >= 0:
                        act.wait_ge(S["out_sums"], b["out_sums"] + h + 1)
                        if h >= 2:
                            act.wait_ge(S["out_ready"], b["out_ready"] + h - 1)
                        rsqrt(scaled[:, h % 2, :], pm[:, h % 2, :], "out_log", b["out_log"] + h + 1, "out_rstd")

            def angles_(s):
                for i in range(4):
                    act.wait_ge(S["angle_step"], 3 + 8 * (i + 1))
                    nc.scalar.activation(angles[:, i, :], ang[:, 2 + i, :], ACT.Sin).then_inc(S["angle_done"], 1)

            def soft(s):
                b, n = s.b, len(s.items)
                if s.out == "oa":
                    nc.scalar.preload_act_table_set(LOG_EXP)

                def copied(i):
                    nk = s.items[i]["k"][3]
                    act.wait_ge(S["s_turned"], b["s_turned"] + i + 1)
                    nc.scalar.copy(attn_t[:, i % 2, 0:nk], bank[3 + i % 2][:, 0:nk]).then_inc(S["s_copied"], 1)

                for i in range(n):
                    it = s.items[i]
                    nk = it["k"][3]
                    act.wait_ge(S["s_neg"], b["s_neg"] + i + 1)
                    if i >= 2:
                        act.wait_ge(S["s_attn"], b["s_attn"] + i - 1)
                    nc.scalar.activation(probs[:, i % 2, 0:nk], logits[:, i % 2, 0:nk], ACT.Exp, bias=stats[:, 10 + i % 2:11 + i % 2],
                                         accum_out=stats[:, 12 + i % 2:13 + i % 2]).then_inc(S["s_probs"], 1)
                    if it["sink"] is not None:
                        nc.scalar.activation(stats[:, 14 + i % 2:15 + i % 2], vec("sink", it["sink"]), ACT.Exp,
                                             bias=stats[:, 10 + i % 2:11 + i % 2]).then_inc(S["s_sink"], 1)
                    fill(s, i, n)
                    if i:
                        copied(i - 1)
                copied(n - 1)

            def iw(s):
                u = Unit(s.run, 0)
                split_ahead(u)
                act.wait_ge(unit_done, u.count)
                nc.scalar.copy(iw_sb, ps[u.slot][:, 0, 0:2 * HEADS2].rearrange("p (t h) -> p t h", t=2)).then_inc(S[s.run.free], 1)

            def select(s):
                b = s.b
                for q in range(2):
                    for h in range(HEADS2):
                        i = q * HEADS2 + h
                        act.wait_ge(S["idx_scores"], b["idx_scores"] + i + 1)
                        if q:
                            act.wait_ge(S["idx_sum"], b["idx_sum"] + h + 1)
                        nc.scalar.activation(rel[:, h, :], bank[h][:, 0:SEQ], ACT.Relu,
                                             scale=(HD * HEADS2) ** -0.5).then_inc(S["idx_relu"], 1)

            def glu(s):
                b = s.b

                def gate(u):
                    split_ahead(u)
                    act.wait_ge(unit_done, u.count)
                    if u.j >= RING:
                        act.wait_ge(S[s.run.free], u.out - RING)
                    nc.scalar.activation(sil[:, u.j % RING, 0:SEQ], ps[u.slot][:, 1, 0:SEQ], ACT.Sigmoid).then_inc(S["glu_sig"], 1)

                sweep(act, s.run, gate)

            def cc(s):
                b = s.b

                def first(u):
                    split_ahead(u)
                    act.wait_ge(unit_done, u.count)
                    if u.j < RING:
                        name, count = s.pair.free, s.pair.f0
                    else:
                        name, count = s.pair.free, u.out - RING
                    act.wait_ge(S[name], count)
                    nc.scalar.copy(sil[:, u.j % RING, 0:SEQ], ps[u.slot][:, 0, 0:SEQ]).then_inc(S["cc_gate"], 1)

                def outer(u):
                    split_ahead(u)
                    act.wait_ge(unit_done, u.count)
                    nc.scalar.copy(cc_b[:, 2 * u.j:2 * u.j + 2, :], ps[u.slot][:, :, 0:SEQ]).then_inc(S[s.run.free], 1)

                sweep(act, s.pair, first)
                sweep(act, s.run, outer)

            def plain(s):
                def keep(u):
                    split_ahead(u)
                    act.wait_ge(unit_done, u.count)
                    nc.scalar.copy(sqk[:, 2 * u.j:2 * u.j + 2, :], ps[u.slot][:, :, 0:SEQ]).then_inc(S[s.run.free], 1)

                sweep(act, s.run, keep)

            def stick(s):
                b = s.b

                def softplus(h):
                    r = h % 2
                    act.wait_ge(S["z_ready"], b["z_ready"] + h + 1)
                    if h >= 2:
                        act.wait_ge(S["z_arg"], b["z_arg"] + h - 1)
                    nc.scalar.activation(z_s[:, r, :], bank[r], ACT.Copy, scale=P ** -0.5).then_inc(S["z_kept"], 1)
                    act.wait_ge(S["z_neg"], b["z_neg"] + h + 1)
                    nc.scalar.activation(z_e[:, r, :], z_e[:, r, :], ACT.Exp).then_inc(S["z_exp"], 1)
                    act.wait_ge(S["z_exp"], b["z_exp"] + h + 1)
                    if h >= 2:
                        act.wait_ge(S["z_soft_m"], b["z_soft_m"] + h - 1)
                    nc.scalar.activation(z_l[:, r, :], z_e[:, r, :], ACT.Ln, bias=1.0).then_inc(S["z_log"], 1)

                def weights_(h):
                    act.wait_ge(S["z_arg_m"], b["z_arg_m"] + h + 1)
                    if h >= 2:
                        act.wait_ge(S["z_out"], b["z_out"] + h - 1)
                    nc.scalar.activation(z_a[:, h % 2, :], z_e[:, h % 2, :], ACT.Exp).then_inc(S["z_attn"], 1)

                for h in range(HEADS2):
                    softplus(h)
                    if h:
                        weights_(h - 1)
                weights_(HEADS2 - 1)

            def layernorm(s):
                b = s.b
                for c in range(4):
                    act.wait_ge(S["ln_mid"], b["ln_mid"] + c + 1)
                    nc.scalar.activation(ln_t[:, c, :], cb_sum[:, c, :], ACT.Square,
                                         scale=512 ** -0.5).then_inc(S["ln_sq"], 1)
                act.wait_ge(S["ln_var"], b["ln_var"] + 1)
                rsqrt(ln_stat[:, 1, :], pm[:, 1, 0:SEQ], "ln_log", b["ln_log"] + 1, "ln_rstd")
                for c in range(4):
                    act.wait_ge(S["ln_out"], b["ln_out"] + c + 1)
                    nc.scalar.activation(cb_sum[:, c, :], cb_sum[:, c, :], ACT.Silu, bias=vec(f"ln_b{s.l}", c),
                                         scale=vec(f"ln_g{s.l}", c)).then_inc(S["ln_act"], 1)

            def gates(s):
                waits_of(act, s)
                for i, run in enumerate(s.runs, s.i):
                    def gate(u):
                        split_ahead(u)
                        act.wait_ge(unit_done, u.count)
                        for m in range(2):
                            c = 2 * u.j + m
                            last = nc.scalar.activation(gates_sb[:, i % 2 * KC + c, :], ps[u.slot][:, m, 0:SEQ], ACT.Sigmoid,
                                                        bias=vec(f"b_gate{s.l}", i * KC + c))
                        last.then_inc(S[run.free], 1)

                    sweep(act, run, gate)

            def conv_in(s):
                b, run = s.b, s.run

                def keep(u):
                    split_ahead(u)
                    act.wait_ge(unit_done, u.count)
                    if u.j0 >= RING:
                        act.wait_ge(S["act_lo"], u.j + (b["act_lo"] + 1 - RING))
                    r = u.j0 % RING
                    nc.scalar.copy(cin[:, r, CC_TAPS - 1:], ps[u.slot][:, 0, 0:SEQ]).then_inc(S["cin_ready"], 1)
                    act.wait_ge(S["tap2"], u.j + (b["tap2"] + 1))
                    nc.scalar.activation(sil[:, r, 0:SEQ], tap_t[:, r, :], ACT.Silu).then_inc(S["silu_ready"], 1)

                sweep(act, run, keep)

            todo = dict(ada=ada, statistics=statistics, norm=norm, ffn_in=ffn_in, heads=heads, values=values, diff=diff, angles=angles_, soft=soft,
                        iw=iw, select=select, glu=glu, cc=cc, plain=plain, stick=stick, layernorm=layernorm, gates=gates,
                        conv_in=conv_in, proj=splits_only, branch=splits_only)
            act.wait_ge(vec_landed, 16)
            nc.scalar.activation(cond, vec("cond").rearrange("p (c s) -> p c s", s=2), ACT.Silu).then_inc(cond_ready, 1)
            act.wait_ge(cond_ready, 1)
            nc.scalar.copy(cond_halves[:, :, 0:2], cond).then_inc(cond_hi_ready, 1)
            split(Unit(*units[0]))
            split(Unit(*units[1]))
            for s in stages:
                if s.kind in todo:
                    todo[s.kind](s)

        @block.vector
        def _(dve):
            def split(u):
                if u is None:
                    return
                n = u.run.kc * u.run.cols
                dve.wait_ge(hi_ready, u.count)
                nc.vector.tensor_tensor(w_lo[u.slot][:, 0:n], raw[u.slot][:, 0:n], w_hi[u.slot][:, 0:n].bitcast(F32),
                                        ALU.subtract).then_inc(lo_ready, 1)

            def split_ahead(u):
                split(next_split(u))

            def splits_only(s):
                for run in s.runs or (s.run,):
                    if s.filler is None:
                        sweep(dve, run, split_ahead)

            def halves(o, src, hi_signal, lo_signal, count):
                hi, lo = o
                nc.vector.tensor_copy(hi, src).then_inc(S[hi_signal], 1)
                dve.wait_ge(S[hi_signal], count)
                nc.vector.tensor_tensor(lo, src, hi.bitcast(F32), ALU.subtract).then_inc(S[lo_signal], 1)

            def ada_mods(s, k, banks):
                kind, which, done = s.steps[k]
                if kind == "row":
                    split_ahead(Unit(s.run, which))
                    return
                at_w = s.which.index(which)
                bias = vec(f"ada_b{s.layer}").rearrange("p (c s) -> p c s", s=2)
                part = slice(which * KC, (which + 1) * KC)
                one = mod_sb[s.layer][:, part, :]
                dve.wait_ge(S["ada_turned"], s.b["ada_turned"] + at_w + 1)
                nc.vector.tensor_tensor(one, banks[k % len(banks)][:, 0:2 * KC].rearrange("p (c s) -> p c s", s=2),
                                        bias[:, part, :], ALU.add).then_inc(S["mods_summed"], 1)
                if which in (1, 2, 4, 7, 8):
                    dve.wait_ge(S["mods_summed"], done[1])
                if which % 3 == 1:
                    nc.vector.tensor_scalar(one, one, 1.0, None, ALU.add).then_inc(S["mods_ready"], 1)
                elif which in (2, 8):
                    nc.vector.tensor_scalar(one, one, 0.5, None, ALU.mult).then_inc(S["mods_ready"], 1)

            def ada(s):
                if not s.filler:
                    dve.wait_ge(vec_landed, 16)
                    for k in range(len(s.steps)):
                        ada_mods(s, k, ADA_BANKS)

            def fill(s, i, n):
                for a, k in share(s, i, n):
                    ada_mods(a, k, ADA_FILL_BANK)

            def add_squares(s, chunks):
                N, b = s.N, s.b
                for c in chunks:
                    dve.wait_ge(S["squares_ready"], b["squares_ready"] + c + 1)
                    if c:
                        dve.wait_ge(S["square_added"], b["square_added"] + c)
                        ins = nc.vector.tensor_tensor(square_sum[:, 0:N], square_sum[:, 0:N], sq[:, c % 4, 0:N], ALU.add)
                    else:
                        ins = nc.vector.tensor_copy(square_sum[:, 0:N], sq[:, 0, 0:N])
                    ins.then_inc(S["square_added"], 1)

            def statistics(s):
                add_squares(s, range(s.early, KC))

            def norm(s):
                N, b = s.N, s.b
                if s.after is None:
                    dve.wait_ge(x_landed, 16)
                else:
                    name, count = s.after(KC - 1)
                    dve.wait_ge(S[name], count)
                dve.wait_ge(S["rstd_ready"], b["rstd_ready"])
                for c in range(KC + (s.gain is None)):
                    if s.gain is not None:
                        if c >= RING:
                            dve.wait_ge(S["h_lo"], b["h_lo"] + c - RING + 1)
                        nc.vector.scalar_tensor_tensor(full[:, c % RING, 0:N], xs[:, c, 0:N], vec(s.gain, c), rstd[:, 0:N],
                                                       ALU.mult, ALU.mult).then_inc(S["h_scaled"], 1)
                        continue
                    if c < KC:
                        if c >= 2:
                            dve.wait_ge(S["h_modulated"], b["h_modulated"] + c - 1)
                        nc.vector.tensor_tensor(scaled[:, c % 2, 0:N], xs[:, c, 0:N], rstd[:, 0:N],
                                                ALU.mult).then_inc(S["scaled_ready"], 1)
                    if c:
                        dve.wait_ge(S["h_modulated"], b["h_modulated"] + c)
                        nc.vector.tensor_copy(h_hi[:, c - 1, 0:N], full[:, (c - 1) % RING, 0:N]).then_inc(S["h_hi_dve"], 1)

            def proj(s):
                run = s.run
                if s.gate is not None:
                    dve.wait_ge(S["mods_summed"], s.b["mods_summed"])
                    dve.wait_ge(S["mods_ready"], s.b["mods_ready"])

                def add_on(u):
                    split_ahead(u)
                    per = run.cols // P
                    if s.next is not None and u.j0 == run.n - 1:
                        add_squares(s.next, range(s.next.early))
                    dve.wait_ge(unit_done, u.count)
                    if s.gate is None:
                        xc = xs[:, bass.ds(u.j * per, per), 0:SEQ]
                        nc.vector.tensor_tensor(xc, ps[u.slot][:, 0:per, 0:SEQ], xc, ALU.add).then_inc(S[run.free], 1)
                        return
                    layer, which = s.gate
                    for m in range(per):
                        c = u.j * per + m
                        for st in range(s.N // SEQ):
                            tok = slice(st * SEQ, (st + 1) * SEQ)
                            xc = xs[:, bass.ds(c, 1), tok].rearrange("p c n -> p (c n)")
                            g = mod_sb[layer][:, bass.ds(c + which * KC, 1), st:st + 1].rearrange("p c n -> p (c n)")
                            last = nc.vector.scalar_tensor_tensor(xc, ps[u.slot][:, m, tok], g, xc, ALU.mult, ALU.add)
                    last.then_inc(S[run.free], 1)

                sweep(dve, run, add_on)

            def ffn_in(s):
                N, b, run = s.N, s.b, s.run

                def gated(u):
                    split_ahead(u)
                    r = u.j0 % RING
                    dve.wait_ge(S["silu_ready"], u.j + (b["silu_ready"] + 1))
                    nc.vector.tensor_tensor(sil[:, r, 0:N], sil[:, r, 0:N], ps[u.slot][:, 1, 0:N], ALU.mult).then_inc(S[run.free], 1)
                    dve.wait_ge(S[run.free], u.out)
                    nc.vector.tensor_copy(act_hi[:, bass.ds(u.j, 1), 0:N].rearrange("p c n -> p (c n)"),
                                          sil[:, r, 0:N]).then_inc(S["act_hi"], 1)

                sweep(dve, run, gated)

            def heads(s):
                run, N, b = s.run, s.N, s.b
                nm = run.cols // P
                if s.cos in ANGLES:
                    dve.wait_ge(S["angle_done"], 4)
                if s.gain:
                    nc.vector.tensor_scalar(rot_g, con(s.rot), vec(s.gain), None, ALU.mult).then_inc(S["head_tables"], 1)
                for i in range(run.n):
                    u = Unit(run, i)
                    split_ahead(u)
                    two = 2 * ((b["head_done"] + i) % 2)
                    dve.wait_ge(S["head_kept"], b["head_kept"] + i + 1)
                    for m in range(nm):
                        o, x = dest_of(s, i * nm + m)[:, 0:SEQ], kept[:, two + m, 0:SEQ]
                        if s.gain:
                            last = nc.vector.scalar_tensor_tensor(o, x, vec(s.gain), con(s.cos), ALU.mult, ALU.mult)
                        else:
                            last = nc.vector.tensor_tensor(o, x, con(s.cos), ALU.mult)
                    last.then_inc(S["head_cos"], 1)
                    if s.dim:
                        dve.wait_ge(S["head_rstd"], b["head_rstd"] + i + 1)
                    dve.wait_ge(S["head_rotated"], b["head_rotated"] + i + 1)
                    for m in range(nm):
                        last = nc.vector.tensor_tensor(rope_t[:, m, :], ps[u.slot][:, 0, m * SEQ:(m + 1) * SEQ], con(s.sin),
                                                       ALU.mult)
                    last.then_inc(S[run.free], 1)
                    dve.wait_ge(S[run.free], u.out)
                    ch = s.ch0 + i * nm
                    o = BUF[s.dest][:, ch:ch + nm, 0:SEQ]
                    ins = nc.vector.tensor_tensor(o, o, rope_t[:, 0:nm, :], ALU.add)
                    if not s.dim:
                        ins.then_inc(S["head_summed"], 1)
                        dve.wait_ge(S["head_summed"], b["head_summed"] + i + 1)
                        dve.sem_inc(S["head_done"], 1)
                        continue
                    ins.then_inc(S["head_summed"], 1)
                    for m in range(nm if N > SEQ else 0):
                        nc.vector.scalar_tensor_tensor(dest_of(s, i * nm + m)[:, SEQ:N], kept[:, two + m, SEQ:N], vec(s.gain),
                                                       hr[:, m, SEQ:N], ALU.mult, ALU.mult)
                    dve.wait_ge(S["head_summed"], b["head_summed"] + i + 1)
                    nc.vector.tensor_tensor(o, o, hr[:, 0:nm, 0:SEQ], ALU.mult).then_inc(S["head_done"], 1)

            def diff(s):
                b = s.b
                lam = vec("lambda").rearrange("p (a d) -> p a d", a=4)
                steps = [b["lam_step"]]

                def step(ins):
                    steps[0] += 1
                    ins.then_inc(S["lam_step"], 1)
                    dve.wait_ge(S["lam_step"], steps[0])

                waits_of(dve, s)
                step(nc.vector.tensor_tensor(lam_t, lam[:, 0:4:2, :], lam[:, 1:4:2, :], ALU.mult))
                step(nc.vector.tensor_reduce(stats[:, 0:2], lam_t, AX, ALU.add))
                dve.wait_ge(S["lam_exp"], b["lam_exp"] + 1)
                step(nc.vector.scalar_tensor_tensor(stats[:, 4:5], stats[:, 2:3], LAM_INIT, stats[:, 3:4], ALU.add, ALU.subtract))
                step(nc.vector.tensor_scalar(stats[:, 5:6], vec("a_subln"), 1.0 - LAM_INIT, None, ALU.mult))

                def maxima(i):
                    n = BOTH if i % 4 < 2 else CTX
                    for c in range(2):
                        r = 2 * (i % 2) + c
                        dve.wait_ge(S["scores_ready"], b["scores_ready"] + 2 * i + c + 1)
                        nc.vector.tensor_reduce(stats[:, 8 + r:9 + r], bank[r][:, 0:n], AX, ALU.max).then_inc(S["score_max"], 1)
                    dve.wait_ge(S["score_max"], b["score_max"] + 2 * i + 2)
                    r = 2 * (i % 2)
                    nc.vector.tensor_scalar(stats[:, 16 + r:18 + r], stats[:, 8 + r:10 + r], -(HD ** -0.5), None,
                                            ALU.mult).then_inc(S["neg_max"], 1)

                def combine(i):
                    n = BOTH if i % 4 < 2 else CTX
                    r = 2 * (i % 2)
                    dve.wait_ge(S["probs_ready"], b["probs_ready"] + 2 * i + 2)
                    nc.vector.reciprocal(stats[:, 24 + r:26 + r], stats[:, 20 + r:22 + r]).then_inc(S["prob_sums"], 1)
                    dve.wait_ge(S["prob_sums"], b["prob_sums"] + i + 1)
                    nc.vector.tensor_scalar(stats[:, 28 + r:29 + r], stats[:, 25 + r:26 + r], stats[:, 4:5], None,
                                            ALU.mult).then_inc(S["prob_scales"], 1)
                    dve.wait_ge(S["prob_scales"], b["prob_scales"] + i + 1)
                    nc.vector.tensor_scalar(prob2[:, 0:n], probs[:, r + 1, 0:n], stats[:, 28 + r:29 + r], None,
                                            ALU.mult).then_inc(S["prob2_scaled"], 1)
                    dve.wait_ge(S["prob2_scaled"], b["prob2_scaled"] + i + 1)
                    if i >= 2:
                        dve.wait_ge(S["attn_turned"], b["attn_turned"] + i - 1)
                    nc.vector.scalar_tensor_tensor(attn[:, i % 2, 0:n], probs[:, r, 0:n], stats[:, 24 + r:25 + r],
                                                   prob2[:, 0:n], ALU.mult, ALU.subtract).then_inc(S["attn_ready"], 1)

                maxima(0)
                for i in range(NI):
                    if i + 1 < NI:
                        maxima(i + 1)
                    combine(i)
                    fill(s, i, NI)
                for h in range(A_HEADS):
                    r = scaled[:, h % 2, :]
                    dve.wait_ge(S["out_rstd"], b["out_rstd"] + h + 1)
                    if h >= RING:
                        dve.wait_ge(S["out_ready"], b["out_ready"] + h - RING + 1)
                    nc.vector.scalar_tensor_tensor(full[:, h % RING, :], qk[:, h, :], stats[:, 5:6], r, ALU.mult,
                                                   ALU.mult).then_inc(S["out_full"], 1)
                    dve.wait_ge(S["out_full"], b["out_full"] + h + 1)
                    nc.vector.tensor_copy(h_hi[:, h, :], full[:, h % RING, :]).then_inc(S["out_hi"], 1)

            def merge(s):
                for c in range(KC):
                    dve.wait_ge(S["merged"], s.ready[1] + c // 2 + 1)
                    nc.vector.tensor_copy(h_hi[:, c, 0:SEQ], merged[:, c, :]).then_inc(S["m_hi"], 1)

            def angles_(s):
                count = [0]

                def step(ins):
                    ins.then_inc(S["angle_step"], 1)
                    count[0] += 1
                    dve.wait_ge(S["angle_step"], count[0])

                turn = 2 * math.pi
                parts = [6.28125, 0.0019350051879882812]
                parts.append(turn - parts[0] - parts[1])
                magic = 1.5 * 2.0 ** 23
                dve.wait_ge(S["h_lo"], s.b["h_lo"])
                step(nc.vector.tensor_copy(ang[:, 0, :], pos_i[:, 0, :]))
                step(nc.vector.tensor_scalar(ang[:, 6, :], ang[:, 0, :], con("freq128"), None, ALU.mult))
                step(nc.vector.tensor_scalar(ang[:, 7, :], ang[:, 0, :], con("freq64"), None, ALU.mult))
                for i in range(4):
                    a, r, k = ang[:, 6 + i // 2, :], ang[:, 2 + i, :], ang[:, 1, :]
                    quarter = 0.25 if i % 2 == 0 else 0.0
                    step(nc.vector.tensor_scalar(k, a, 1.0 / turn, quarter, ALU.mult, ALU.add))
                    step(nc.vector.tensor_scalar(k, k, magic, None, ALU.add))
                    step(nc.vector.tensor_scalar(k, k, magic, None, ALU.subtract))
                    step(nc.vector.scalar_tensor_tensor(r, k, -parts[0], a, ALU.mult, ALU.add))
                    step(nc.vector.scalar_tensor_tensor(r, k, -parts[1], r, ALU.mult, ALU.add))
                    step(nc.vector.scalar_tensor_tensor(r, k, -parts[2], r, ALU.mult, ALU.add))
                    step(nc.vector.tensor_scalar(r, r, quarter * turn, None, ALU.add))
                    step(nc.vector.tensor_scalar(r, r, 3.1415925, -3.1415925, ALU.min, ALU.max))

            def soft(s):
                b, n = s.b, len(s.items)
                if s.swap:
                    for c in range(2):
                        dve.wait_ge(S["s_swap"], b["s_swap"] + c + 1)
                        nc.vector.tensor_copy(gk[:, 2 + c, :], bank[c]).then_inc(S["s_swapped"], 1)

                def masked(i):
                    it = s.items[i]
                    nk, r = it["k"][3], i % 2
                    dve.wait_ge(S["s_scores"], b["s_scores"] + i + 1)
                    if i >= 2:
                        dve.wait_ge(S["s_probs"], b["s_probs"] + i - 1)
                    if "needs" in it:
                        dve.wait_ge(S[it["needs"][0]], it["needs"][1])
                    if nk > SEQ:
                        nc.vector.tensor_scalar(logits[:, r, SEQ:nk], bank[i % 3][:, SEQ:nk], s.scale, None, ALU.mult)
                    nc.vector.scalar_tensor_tensor(logits[:, r, 0:SEQ], bank[i % 3][:, 0:SEQ], s.scale, mask_of(it), ALU.mult,
                                                   ALU.add).then_inc(S["s_masked"], 1)
                    dve.wait_ge(S["s_masked"], b["s_masked"] + i + 1)
                    nc.vector.tensor_reduce(stats[:, 8 + r:9 + r], logits[:, r, 0:nk], AX, ALU.max).then_inc(S["s_max"], 1)
                    dve.wait_ge(S["s_max"], b["s_max"] + i + 1)
                    if it["sink"] is not None:
                        nc.vector.tensor_scalar(stats[:, 10 + r:11 + r], stats[:, 8 + r:9 + r], vec("sink", it["sink"]), -1.0,
                                                ALU.max, ALU.mult).then_inc(S["s_neg"], 1)
                    else:
                        nc.vector.tensor_scalar(stats[:, 10 + r:11 + r], stats[:, 8 + r:9 + r], -1.0, None,
                                                ALU.mult).then_inc(S["s_neg"], 1)

                def normed(i):
                    it = s.items[i]
                    nk, r = it["k"][3], i % 2
                    dve.wait_ge(S["s_probs"], b["s_probs"] + i + 1)
                    total = stats[:, 12 + r:13 + r]
                    if it["sink"] is not None:
                        dve.wait_ge(S["s_sink"], b["s_sink"] + i + 1)
                        nc.vector.tensor_tensor(stats[:, 16 + r:17 + r], total, stats[:, 14 + r:15 + r],
                                                ALU.add).then_inc(S["s_total"], 1)
                        dve.wait_ge(S["s_total"], b["s_total"] + i + 1)
                        total = stats[:, 16 + r:17 + r]
                    nc.vector.reciprocal(stats[:, 18 + r:19 + r], total).then_inc(S["s_rcp"], 1)
                    dve.wait_ge(S["s_rcp"], b["s_rcp"] + i + 1)
                    if i >= 2:
                        dve.wait_ge(S["s_turned"], b["s_turned"] + i - 1)
                    nc.vector.tensor_scalar(attn[:, r, 0:nk], probs[:, r, 0:nk], stats[:, 18 + r:19 + r], None,
                                            ALU.mult).then_inc(S["s_attn"], 1)

                def chunk_out(chunk):
                    dve.wait_ge(S["s_chunk"], b["s_chunk"] + chunk + 1)
                    halves(out_of(s, chunk), pm[:, chunk % 2, 0:SEQ], "s_hi", "s_out", b["s_hi"] + chunk + 1)

                if s.out == "oa":
                    dve.wait_ge(S["cc_out"], b["cc_out"])
                masked(0)
                for i in range(n):
                    if i + 1 < n:
                        masked(i + 1)
                    normed(i)
                    fill(s, i, n)
                    if i >= 2 and (i - 2) % s.per == s.per - 1:
                        chunk_out((i - 2) // s.per)
                for chunk in range((n - 2) // s.per, n // s.per):
                    chunk_out(chunk)

            def iw(s):
                split_ahead(Unit(s.run, 0))

            def select(s):
                b = s.b
                dve.wait_ge(S[s.iw.run.free], s.iw.run.f0 + 1)
                for q in range(2):
                    for h in range(HEADS2):
                        i = q * HEADS2 + h
                        dve.wait_ge(S["idx_relu"], b["idx_relu"] + i + 1)
                        before = con("causal")[:, q * SEQ:(q + 1) * SEQ] if h == 0 else idx[:, q, :]
                        nc.vector.scalar_tensor_tensor(idx[:, q, :], rel[:, h, :], iw_sb[:, q, h:h + 1], before, ALU.mult,
                                                       ALU.add).then_inc(S["idx_sum"], 1)
                        dve.wait_ge(S["idx_sum"], b["idx_sum"] + i + 1)
                count = [b["top_steps"]]
                last = [0, 0]

                def step(q, ins):
                    count[0] += 1
                    last[q] = count[0]
                    ins.then_inc(S["top_steps"], 1)

                def wait_last(q):
                    if last[q]:
                        dve.wait_ge(S["top_steps"], last[q])

                behind = [Unit(run, j) for run in s.runs for j in range(run.n)]
                turns = [0]

                def each(body):
                    for q in range(2):
                        wait_last(q)
                        step(q, body(q))
                    if turns[0] < len(behind):
                        split_ahead(behind[turns[0]])
                    turns[0] += 1

                top = [stats[:, 24 + 8 * q:32 + 8 * q] for q in range(2)]
                cur = [idx[:, q, :] for q in range(2)]
                work = [idx_work[:, q, :] for q in range(2)]
                for r in range(TOPK // 8):
                    each(lambda q: nc.vector.max(top[q], cur[q]))
                    if r < TOPK // 8 - 1:
                        each(lambda q: nc.vector.match_replace(work[q], top[q], cur[q], LOWEST))
                        cur = work
                least = [top[q][:, 7:8] for q in range(2)]
                above = [stats[:, 40 + q:41 + q] for q in range(2)]
                need = [stats[:, 42 + q:43 + q] for q in range(2)]
                gt, eq, cum = ([t[:, q, :] for q in range(2)] for t in (sel_gt, sel_eq, sel_cum))
                each(lambda q: nc.vector.tensor_scalar(gt[q], idx[:, q, :], least[q], None, ALU.is_gt, ALU.add, accum_out=above[q]))
                each(lambda q: nc.vector.tensor_scalar(eq[q], idx[:, q, :], least[q], None, ALU.is_equal))
                each(lambda q: nc.vector.tensor_tensor_scan(cum[q], eq[q], eq[q], 0.0, ALU.add, ALU.max))
                each(lambda q: nc.vector.tensor_scalar(need[q], above[q], -1.0, float(TOPK), ALU.mult, ALU.add))
                each(lambda q: nc.vector.scalar_tensor_tensor(eq[q], cum[q], need[q], eq[q], ALU.is_le, ALU.mult))
                each(lambda q: nc.vector.tensor_tensor(gt[q], gt[q], eq[q], ALU.add))
                each(lambda q: nc.vector.tensor_scalar(gt[q], gt[q], -NEG, NEG, ALU.mult, ALU.add))
                for u in behind[turns[0]:]:
                    split_ahead(u)
                for q in range(2):
                    wait_last(q)
                    nc.vector.tensor_tensor(sel_mask[:, q, :], gt[q], con("causal")[:, q * SEQ:(q + 1) * SEQ],
                                            ALU.add).then_inc(S["sel_mask"], 1)

            def glu(s):
                def gated(u):
                    split_ahead(u)
                    dve.wait_ge(S["glu_sig"], s.b["glu_sig"] + u.j + 1)
                    nc.vector.tensor_tensor(cb_in[:, u.j, CB_TAPS - 1:], sil[:, u.j % RING, 0:SEQ], ps[u.slot][:, 0, 0:SEQ],
                                            ALU.mult).then_inc(S[s.run.free], 1)

                sweep(dve, s.run, gated)

            def cc(s):
                units = s.pair.n + s.run.n
                share = -(-CB_TAPS // units)

                def conv_taps(i):
                    l, base = s.l, s.conv.b["conv_first"]
                    for w in range(i * share, min((i + 1) * share, CB_TAPS)):
                        for c in range(2):
                            x, wcol = cb_in[:, c, w:w + SEQ], vec(f"cb_w{l}", c * CB_TAPS + w)
                            if w == 0:
                                ins = nc.vector.tensor_scalar(cb_sum[:, c, :], x, wcol, vec(f"cb_b{l}", c), ALU.mult, ALU.add)
                            else:
                                dve.wait_ge(S["conv_first"], base + 2 * (w - 1) + c + 1)
                                ins = nc.vector.scalar_tensor_tensor(cb_sum[:, c, :], x, wcol, cb_sum[:, c, :], ALU.mult, ALU.add)
                            ins.then_inc(S["conv_first"], 1)

                def gated(u):
                    split_ahead(u)
                    dve.wait_ge(S["cc_gate"], s.b["cc_gate"] + u.j + 1)
                    nc.vector.tensor_tensor(cc_in[:, u.j, CC_TAPS - 1:], sil[:, u.j % RING, 0:SEQ], ps[u.slot][:, 1, 0:SEQ],
                                            ALU.mult).then_inc(S[s.pair.free], 1)
                    conv_taps(u.j)

                def outer(u):
                    split_ahead(u)
                    conv_taps(s.pair.n + u.j)

                conv = s.conv
                dve.wait_ge(S["conv_pad"], conv.b["conv_pad"] + 1)
                dve.wait_ge(S[conv.run.free], conv.run.f0 + conv.run.n)
                sweep(dve, s.pair, gated)
                sweep(dve, s.run, outer)

            def stick(s):
                b = s.b

                def first(h):
                    r = h % 2
                    dve.wait_ge(S["z_kept"], b["z_kept"] + h + 1)
                    if h >= 2:
                        dve.wait_ge(S["z_attn"], b["z_attn"] + h - 1)
                    nc.vector.scalar_tensor_tensor(z_e[:, r, :], z_s[:, r, :], -1.0, z_s[:, r, :], ALU.mult,
                                                   ALU.min).then_inc(S["z_neg"], 1)
                    dve.wait_ge(S["z_log"], b["z_log"] + h + 1)
                    nc.vector.scalar_tensor_tensor(z_l[:, r, :], z_s[:, r, :], 0.0, z_l[:, r, :], ALU.max,
                                                   ALU.add).then_inc(S["z_soft"], 1)

                def second(h):
                    r = h % 2
                    dve.wait_ge(S["z_sums"], b["z_sums"] + h + 1)
                    nc.vector.tensor_tensor(z_e[:, r, :], z_s[:, r, :], bank[2 + r], ALU.subtract).then_inc(S["z_arg"], 1)

                def keep(h):
                    dve.wait_ge(S["z_out"], b["z_out"] + h + 1)
                    halves(tuple(t[:, h, :] for t in branch["od"]), pm[:, h % 2, 0:SEQ], "od_hi", "od_out", b["od_hi"] + h + 1)

                dve.wait_ge(S["cc_out"], s.b["cc_out"])
                for h in range(HEADS2):
                    first(h)
                    second(h)
                    if h:
                        keep(h - 1)
                keep(HEADS2 - 1)

            def layernorm(s):
                b = s.b
                ob = cb_sum
                mean, dev = ln_stat[:, 0, :], ln_stat[:, 1, :]
                dve.wait_ge(S["ln_sum"], b["ln_sum"] + 1)
                nc.vector.tensor_scalar(mean, pm[:, 0, 0:SEQ], 1.0 / 512, None, ALU.mult).then_inc(S["ln_mean"], 1)
                dve.wait_ge(S["ln_mean"], b["ln_mean"] + 1)
                for c in range(4):
                    nc.vector.tensor_tensor(ob[:, c, :], ob[:, c, :], mean, ALU.subtract).then_inc(S["ln_mid"], 1)
                dve.wait_ge(S["ln_rstd"], b["ln_rstd"] + 1)
                for c in range(4):
                    nc.vector.tensor_tensor(ob[:, c, :], ob[:, c, :], dev, ALU.mult).then_inc(S["ln_out"], 1)
                for c in range(4):
                    dve.wait_ge(S["ln_act"], b["ln_act"] + c + 1)
                    hi, lo = (t[:, c, :] for t in branch["ob"])
                    halves((hi, lo), ob[:, c, :], "ln_hi", "ob_out", b["ln_hi"] + c + 1)

            def branch_out(s):
                b, run = s.b, s.run

                def weigh(u):
                    split_ahead(u)
                    dve.wait_ge(unit_done, u.count)
                    two = slice(2 * u.j, 2 * u.j + 2)
                    o = merged[:, two, :] if s.i == 0 else gated_t
                    gate = gates_sb[:, s.i % 2 * KC + 2 * u.j:s.i % 2 * KC + 2 * u.j + 2, :]
                    nc.vector.tensor_tensor(o, gate, ps[u.slot][:, :, 0:SEQ], ALU.mult).then_inc(S[run.free], 1)
                    dve.wait_ge(S[run.free], u.out)
                    if s.i == 0:
                        dve.sem_inc(S["merged"], 1)
                    else:
                        nc.vector.tensor_tensor(merged[:, two, :], merged[:, two, :], gated_t, ALU.add).then_inc(S["merged"], 1)
                        dve.wait_ge(S["merged"], b["merged"] + u.j + 1)

                sweep(dve, run, weigh)

            def conv_in(s):
                b, l, run = s.b, s.l, s.run
                dve.wait_ge(S["h_lo"], s.h[1] + KC)
                nc.vector.memset(cin[:, :, 0:CC_TAPS - 1], 0.0).then_inc(S["cin_pad"], 1)
                dve.wait_ge(S["cin_pad"], b["cin_pad"] + 1)
                o = VEC[f"ffn_w{l}"][0] + s.i * HALF * CC_TAPS

                def taps(u):
                    split_ahead(u)
                    r = u.j0 % RING
                    dve.wait_ge(S["cin_ready"], u.j + (b["cin_ready"] + 1))
                    for w in range(CC_TAPS):
                        wcol = vec_sb[:, bass.ds(u.j * CC_TAPS + (o + w), 1)]
                        x = cin[:, r, w:w + SEQ]
                        if w == 0:
                            ins = nc.vector.tensor_scalar(tap_t[:, r, :], x, wcol, None, ALU.mult)
                        else:
                            dve.wait_ge(S[f"tap{w - 1}"], u.j + (b[f"tap{w - 1}"] + 1))
                            ins = nc.vector.scalar_tensor_tensor(tap_t[:, r, :], x, wcol, tap_t[:, r, :], ALU.mult, ALU.add)
                        ins.then_inc(S[f"tap{w}"], 1)
                    dve.wait_ge(S["silu_ready"], u.j + (b["silu_ready"] + 1))
                    nc.vector.tensor_tensor(sil[:, r, 0:SEQ], sil[:, r, 0:SEQ], ps[u.slot][:, 1, 0:SEQ],
                                            ALU.mult).then_inc(S[run.free], 1)
                    dve.wait_ge(S[run.free], u.out)
                    nc.vector.tensor_copy(act_hi[:, bass.ds(u.j, 1), 0:SEQ].rearrange("p c n -> p (c n)"),
                                          sil[:, r, 0:SEQ]).then_inc(S["act_hi"], 1)

                sweep(dve, run, taps)

            todo = dict(ada=ada, statistics=statistics, norm=norm, ffn_in=ffn_in, proj=proj, heads=heads, diff=diff, angles=angles_, soft=soft,
                        select=select, glu=glu, cc=cc, stick=stick, layernorm=layernorm, branch=branch_out, conv_in=conv_in, values=splits_only,
                        iw=iw, plain=splits_only, gates=splits_only, merge=merge)
            dve.wait_ge(cond_hi_ready, 1)
            nc.vector.tensor_tensor(cond_halves[:, :, 2:4], cond, cond_halves[:, :, 0:2].bitcast(F32),
                                    ALU.subtract).then_inc(cond_lo_ready, 1)
            split(Unit(*units[0]))
            split(Unit(*units[1]))
            for s in stages:
                if s.kind in todo:
                    todo[s.kind](s)

        @block.gpsimd
        def _(pool):
            def rest(o, whole, hi, signal):
                nc.gpsimd.tensor_tensor(o, whole, hi.bitcast(F32), ALU.subtract).then_inc(S[signal], 1)

            def norm(s):
                N, b = s.N, s.b
                hi = "h_hi_act" if s.mod is None else "h_hi_dve"
                for c in range(KC):
                    pool.wait_ge(S[hi], b[hi] + c + 1)
                    rest(h_lo[:, c, 0:N], full[:, c % RING, 0:N], h_hi[:, c, 0:N], "h_lo")

            def act_lows(s):
                N, b = s.N, s.b

                def lows(u):
                    pool.wait_ge(S["act_hi"], u.j + (b["act_hi"] + 1))
                    o, hi = (t[:, bass.ds(u.j, 1), 0:N].rearrange("p c n -> p (c n)") for t in (act_lo, act_hi))
                    rest(o, sil[:, u.j0 % RING, 0:N], hi, "act_lo")

                sweep(pool, s.run, lows)

            def diff(s):
                for h in range(A_HEADS):
                    pool.wait_ge(S["out_hi"], s.b["out_hi"] + h + 1)
                    rest(h_lo[:, h, :], full[:, h % RING, :], h_hi[:, h, :], "out_ready")

            def merge(s):
                for c in range(KC):
                    pool.wait_ge(S["m_hi"], s.b["m_hi"] + c + 1)
                    rest(h_lo[:, c, 0:SEQ], merged[:, c, :], h_hi[:, c, 0:SEQ], "m_lo")

            def conv(src, dst, product, chunks, weights_of, bias_of, taps, signal, base):
                for w in range(taps):
                    if w:
                        pool.wait_ge(S[signal], base + w)
                    for c in range(chunks.start, chunks.stop):
                        x = src[:, c, w:w + SEQ]
                        if w == 0 and bias_of is not None:
                            ins = nc.gpsimd.tensor_scalar(dst[:, c, :], x, weights_of(c, w), bias_of(c), ALU.mult, ALU.add)
                        else:
                            ins = nc.gpsimd.tensor_scalar((product if w else dst)[:, c, :], x, weights_of(c, w), None, ALU.mult)
                    if not w:
                        ins.then_inc(S[signal], 1)
                        continue
                    ins.then_inc(S[signal + "_product"], 1)
                    pool.wait_ge(S[signal + "_product"], base // taps * (taps - 1) + w)
                    nc.gpsimd.tensor_tensor(dst[:, chunks, :], dst[:, chunks, :], product[:, chunks, :],
                                            ALU.add).then_inc(S[signal], 1)

            def glu(s):
                b, l = s.b, s.l
                pool.wait_ge(S[s.run.free], s.run.f0 + 1)
                nc.gpsimd.memset(cb_in[:, :, 0:CB_TAPS - 1], 0.0).then_inc(S["conv_pad"], 1)
                pool.wait_ge(S["conv_pad"], b["conv_pad"] + 1)
                pool.wait_ge(S[s.run.free], s.run.f0 + 4)
                conv(cb_in, cb_sum, cb_product, slice(2, 4), lambda c, w: vec(f"cb_w{l}", c * CB_TAPS + w), lambda c: vec(f"cb_b{l}", c), CB_TAPS,
                     "conv_steps", b["conv_steps"])

            def cc(s):
                b, l = s.b, s.l
                nc.gpsimd.memset(cc_in[:, :, 0:CC_TAPS - 1], 0.0).then_inc(S["cc_pad"], 1)
                pool.wait_ge(S["cc_pad"], b["cc_pad"] + 1)
                pool.wait_ge(S[s.pair.free], s.pair.f0 + 4)
                pool.wait_ge(S["conv_first"], s.conv.b["conv_first"] + 2 * CB_TAPS)
                conv(cc_in, cc_sum, cc_product, slice(0, 4), lambda c, w: vec(f"cc_w{l}", c * CC_TAPS + w), None, CC_TAPS, "cc_steps", b["cc_steps"])
                pool.wait_ge(S[s.run.free], s.run.f0 + 2)
                for c in range(4):
                    pool.wait_ge(S["cc_steps"], b["cc_steps"] + CC_TAPS)
                    hi, lo = (t[:, c, :] for t in branch["oc"])
                    nc.gpsimd.tensor_tensor(cc_sum[:, c, :], cc_sum[:, c, :], cc_b[:, c, :], ALU.mult).then_inc(S["cc_full"], 1)
                    pool.wait_ge(S["cc_full"], b["cc_full"] + c + 1)
                    nc.gpsimd.tensor_copy(hi, cc_sum[:, c, :]).then_inc(S["cc_hi"], 1)
                    pool.wait_ge(S["cc_hi"], b["cc_hi"] + c + 1)
                    rest(lo, cc_sum[:, c, :], hi, "cc_out")

            def stick(s):
                b = s.b

                def mask(dst, src, fill, signal):
                    nc.gpsimd.affine_select(out=dst.rearrange("p (k t) -> p k t", k=2), in_=src.rearrange("p (k t) -> p k t", k=2),
                                            pattern=[[-P, 2], [1, SEQ]], compare_op=ALU.is_gt, fill=fill, base=0,
                                            channel_multiplier=-1).then_inc(S[signal], 1)

                for h in range(HEADS2):
                    r = h % 2
                    pool.wait_ge(S["z_soft"], b["z_soft"] + h + 1)
                    mask(z_m[:, r, :], z_l[:, r, :], 0.0, "z_soft_m")
                    pool.wait_ge(S["z_arg"], b["z_arg"] + h + 1)
                    mask(z_e[:, r, :], z_e[:, r, :], NEG, "z_arg_m")

            todo = dict(norm=norm, ffn_in=act_lows, conv_in=act_lows, diff=diff, merge=merge, glu=glu, cc=cc, stick=stick)
            for s in stages:
                if s.kind in todo:
                    todo[s.kind](s)


INS = ["ada_w", "ffn_pre_wi", "ffn_pre_wo", "ffn_post_wi", "ffn_post_wo", "a_w_qkv", "a_w_o", "b_w_qkv", "b_w_o",
       "w_in_2", "w_oa_2", "w_ob_2", "w_oc_2", "w_od_2", "w_merge_2", "w_ffn_gate_2", "w_ffn_up_2", "w_ffn_down_2"]


def lay_out(inputs):
    arr = {k: np.asarray(v) for k, v in inputs.items()}
    x_t = np.concatenate([arr["x"][0].T, arr["ctx"][0].T], axis=1)
    vecs = np.zeros((P, N_VEC), np.float32)

    def put(name, a):
        o, w = VEC[name]
        vecs[:, o:o + w] = np.ascontiguousarray(a).reshape(P, w)

    def lanes(a):
        return a.reshape(-1, P).T

    put("cond", np.stack([lanes(arr["c"][0]), lanes(arr["c_ctx"])], axis=-1))
    for l in range(DEPTH):
        put(f"ada_b{l}", np.repeat(lanes(arr["ada_b"][l])[:, :, None], 2, axis=2))
    for name, key in (("a_q_gain", "a_q_gain"), ("a_k_gain", "a_k_gain"), ("b_q_gain", "b_q_gain"), ("b_k_gain", "b_k_gain")):
        put(name, np.tile(arr[key][0], 2))
    put("a_subln", arr["a_subln_gain"][0])
    put("lambda", np.broadcast_to(arr["a_lambda"][0].reshape(1, -1), (P, 4 * HD)))
    put("sink", np.broadcast_to(arr["b_sink"][0].reshape(1, -1), (P, B_Q_HEADS)))
    for l in range(DEPTH):
        put(f"g_mix{l}", lanes(arr["g_mix_2"][l]))
        put(f"b_gate{l}", lanes(arr["b_gate_2"][l]))
        put(f"g_qa{l}", arr["g_qa_2"][l])
        put(f"g_ka{l}", arr["g_ka_2"][l])
        put(f"g_kidx{l}", np.tile(arr["g_kidx_2"][l], 2))
        put(f"cb_w{l}", arr["cb_conv_w_2"][l].T.reshape(4, P, CB_TAPS).transpose(1, 0, 2))
        put(f"cb_b{l}", lanes(arr["cb_conv_b_2"][l]))
        put(f"ln_g{l}", lanes(arr["cb_ln_g_2"][l]))
        put(f"ln_b{l}", lanes(arr["cb_ln_b_2"][l]))
        put(f"cc_w{l}", arr["cc_conv_w_2"][l].T.reshape(4, P, CC_TAPS).transpose(1, 0, 2))
        put(f"g_ffn{l}", lanes(arr["g_ffn_2"][l]))
        put(f"ffn_w{l}", arr["ffn_conv_w_2"][l].T.reshape(FC, P, CC_TAPS).transpose(1, 0, 2))
    pos = np.ascontiguousarray(np.broadcast_to(arr["positions_2"].reshape(1, SEQ), (P, SEQ)))
    arrays = {"x_t": np.ascontiguousarray(x_t), "vecs": vecs, "consts": shape_constants(), "positions": pos}
    for name in INS:
        arrays[name] = np.ascontiguousarray(arr[name])
    return arrays


def kernel(**inputs):
    import concourse.bacc as bacc
    from concourse.bass_utils import run_bass_kernel_spmd

    arrays = lay_out(inputs)
    nc = bacc.Bacc("TRN2", target_bir_lowering=False, num_devices=1)
    args = [nc.dram_tensor(f"in_{n}", a.shape, mybir.dt.from_np(a.dtype), kind="ExternalInput").ap() for n, a in arrays.items()]
    out = nc.dram_tensor("out_t", (D, SEQ), F32, kind="ExternalOutput").ap()
    build(nc, *args, out)
    r = run_bass_kernel_spmd(nc, [{f"in_{n}": a for n, a in arrays.items()}], core_ids=[0])
    return np.ascontiguousarray(r.results[0]["out_t"].T).reshape(1, SEQ, D)
```

```python
import math
from collections import Counter

import numpy as np

import concourse.bass as bass
from concourse import mybir
from concourse.alu_op_type import AluOpType as ALU

F32 = mybir.dt.float32
F32R = mybir.dt.float32r
I32 = mybir.dt.int32
ACT = mybir.ActivationFunctionType
AX = mybir.AxisListType.X

P = 128
D = 1024
KC = D // P
SEQ = 256
CTX = 256
BOTH = SEQ + CTX
DEPTH = 2
D_FF = 2816
FC = D_FF // P
HALF = FC // 2
N_MOD = 9
MODC = N_MOD * KC
EPS = 1e-6
GRID_W = 64
A_HEADS = 8
B_Q_HEADS = 16
B_KV_HEADS = 4
B_GROUP = B_Q_HEADS // B_KV_HEADS
HD = 64
WINDOW = 128
HEADS2 = 4
TOPK = min(256, SEQ // 4)
CB_TAPS = 31
CC_TAPS = 3
NEG = -1e30
LOWEST = -3e38
LAM_INIT = 0.8 - 0.6 * math.exp(-0.3 * 0)
RING = 3
SLOT = KC * 2 * P
PER_MOD = KC // 2
NI = A_HEADS * 4
OFF = {}
_at = 0
for _name, _w in (("aq", 512), ("ak", 512), ("av", 512), ("iq", 256), ("ik", 64), ("iw", 4), ("glu", 1024),
                  ("cc", 1536), ("sb", 1536), ("gate", 4096)):
    OFF[_name] = _at
    _at += _w
N_IN = _at

VEC = {}
_at = 0


def _vec(name, width):
    global _at
    VEC[name] = (_at, width)
    _at += width


_vec("cond", KC * 2)
for _l in range(DEPTH):
    _vec(f"ada_b{_l}", MODC * 2)
for _name in ("a_q_gain", "a_k_gain", "a_subln", "b_q_gain", "b_k_gain"):
    _vec(_name, 1)
_vec("lambda", 4 * HD)
_vec("sink", B_Q_HEADS)
for _l in range(DEPTH):
    for _name, _w in (("g_mix", KC), ("b_gate", 4 * KC), ("g_qa", 1), ("g_ka", 1), ("g_kidx", 1),
                      ("cb_w", 4 * CB_TAPS), ("cb_b", 4), ("ln_g", 4), ("ln_b", 4), ("cc_w", 4 * CC_TAPS),
                      ("g_ffn", KC), ("ffn_w", FC * CC_TAPS)):
        _vec(f"{_name}{_l}", _w)
N_VEC = _at

CON = {}
_at = 0
for _name, _w in (("ident", P), ("ones", P), ("blocks", P), ("rot_axial", P), ("rot_part128", P), ("rot_part64", P),
                  ("swap", P), ("suffix", P), ("cos_axial", SEQ), ("sin_axial", SEQ), ("band", 2 * SEQ),
                  ("causal", 2 * SEQ), ("fold", 2), ("freq128", 1), ("freq64", 1), ("eps", 1)):
    CON[_name] = (_at, _w)
    _at += _w
N_CON = _at


def shape_constants():
    c = np.zeros((P, N_CON), np.float32)

    def put(name, a):
        o, w = CON[name]
        c[:, o:o + w] = np.asarray(a, np.float32).reshape(P, w)

    lane = np.arange(P)
    put("ident", np.eye(P))
    put("ones", np.ones((P, P)))
    put("blocks", (lane[:, None] // HD) == (lane[None, :] // HD))

    def rotation(half, group):
        r = np.zeros((P, P), np.float32)
        for g in range(0, P, group[0]):
            for b in range(0, group[1], 2 * half):
                for f in range(half):
                    r[g + b + half + f, g + b + f] = -1.0
                    r[g + b + f, g + b + half + f] = 1.0
        return r

    put("rot_axial", rotation(HD // 4, (HD, HD)))
    put("rot_part128", rotation(P // 8, (P, P // 4)))
    put("rot_part64", rotation(HD // 8, (HD, HD // 4)))
    put("swap", np.roll(np.eye(P), HD, axis=0))
    put("suffix", lane[:, None] >= lane[None, :])
    nf = HD // 4
    inv = (np.float32(10000.0) ** (-np.arange(nf, dtype=np.float32) / np.float32(nf))).astype(np.float32)
    t = np.arange(SEQ)
    row, col = (t // GRID_W).astype(np.float32), (t % GRID_W).astype(np.float32)
    ang = np.zeros((HD, SEQ), np.float32)
    for d in range(HD):
        ang[d] = (row if d // (HD // 2) == 0 else col) * inv[d % nf]
    ang = np.concatenate([ang, ang])
    put("cos_axial", np.cos(ang))
    put("sin_axial", np.sin(ang))
    band = np.zeros((P, 2, SEQ), np.float32)
    for q in range(2):
        band[:, q, :] = np.where(np.abs(t[None, :] - (q * P + lane[:, None])) <= WINDOW, 0.0, NEG)
    put("band", band)
    causal = np.zeros((P, 2, SEQ), np.float32)
    for q in range(2):
        causal[:, q, :] = np.where(t[None, :] <= q * P + lane[:, None], 0.0, LOWEST)
    put("causal", causal)
    put("fold", (lane[:, None] % 2 == np.arange(2)[None, :]) & (lane[:, None] < 4))
    for name, dim in (("freq128", P), ("freq64", HD)):
        rot = dim // 4
        half = rot // 2
        f = (np.float32(500000.0) ** (-(np.arange(half, dtype=np.float32) * np.float32(2.0)) / np.float32(rot)))
        v = np.zeros(P, np.float32)
        for g in range(0, P, dim):
            v[g:g + half] = f
            v[g + half:g + rot] = f
        put(name, v)
    put("eps", np.full(P, EPS))
    return c


class Run:

    def __init__(self, name, n, kc, cols, src, by, dmas=1):
        self.name, self.n, self.kc, self.cols, self.src, self.by = name, n, kc, cols, src, by
        self.dmas = dmas


class Unit:

    def __init__(self, run, j0, turn=None):
        self.run, self.j0, self.turn = run, j0, turn
        at = (lambda n: n) if turn is None else (lambda n: turn * RING + n)
        self.t0 = run.t0 + j0
        self.j = at(j0)
        self.slot = self.t0 % RING
        self.count = at(self.t0 + 1)
        self.out = at(run.f0 + j0 + 1)


def build(nc, x_t, vecs, consts, positions, ada_w, pre_wi, pre_wo, post_wi, post_wo, a_w_qkv, a_w_o, b_w_qkv, b_w_o,
          w_in, w_oa, w_ob, w_oc, w_od, w_merge, w_gate, w_up, w_down, out):
    def cols_of(w, col0, width, k0=0, kc=KC):
        def src(j):
            return [(0, w[k0 * P:(k0 + kc) * P, :].rearrange("(k p) m -> p k m", p=P)
                     [:, :, bass.ds(col0 + j * width, width)])]
        return src

    def two_of(wa, ca, wb, cb):
        def src(j):
            return [(0, wa.rearrange("(k p) m -> p k m", p=P)[:, :, bass.ds(ca + j * P, P)]),
                    (P, wb.rearrange("(k p) m -> p k m", p=P)[:, :, bass.ds(cb + j * P, P)])]
        return src

    unit_done, hi_ready, lo_ready = (nc.alloc_semaphore(n) for n in ("unit_done", "hi_ready", "lo_ready"))
    stages, runs, counts = [], [], {}
    units, psum_users = [], []

    class Stage:

        def __init__(self, kind, run=None, N=SEQ, h=None, name=None, l=None, gate=None, gain=None, waits=(), x=None, ready=None,
                     after=None, mod=None, layer=None, which=None, wi=None, wo=None, dim=None, dest=None, ch0=0, rot=None, cos=None,
                     sin=None, tiles=None, items=(), scale=None, v=None, out=None, per=None, swap=False,
                     pair=None, i=None, filler=None, steps=(), conv=None, next=None, early=0, runs=(), beside=None, late=None):
            self.late = late
            self.beside = beside
            self.depth = 3 if beside is None else 2
            self.kind, self.run, self.N, self.h, self.name, self.l, self.x = kind, run, N, h, name, l, x
            self.gate, self.gain, self.waits, self.ready, self.after, self.mod = gate, gain, waits, ready, after, mod
            self.layer, self.which, self.wi, self.wo, self.pair = layer, which, wi, wo, pair
            self.dim, self.dest, self.ch0, self.rot, self.cos, self.sin = dim, dest, ch0, rot, cos, sin
            self.tiles, self.items, self.scale, self.v, self.i = tiles, items, scale, v, i
            self.out, self.per, self.swap, self.filler, self.runs, self.steps, self.conv, self.next, self.early = out, per, swap, filler, runs, steps, conv, next, early
            self.b = Counter(counts)
            stages.append(self)

        def takes(self, **events):
            for name, n in events.items():
                counts[name] = counts.get(name, 0) + n
            return self

    def add(run):
        run.t0 = len(units)
        units.extend((run, j) for j in range(run.n))
        if run.by is None:
            run.free, run.f0 = None, 0
            psum_users.extend([None] * run.n)
        else:
            run.free = "psum_read_" + run.by
            run.f0 = counts.get(run.free, 0)
            psum_users.extend((run.free, run.f0 + j + 1) for j in range(run.n))
            counts[run.free] = run.f0 + run.n
        runs.append(run)
        return run

    def ada(layer, which, filler=False):
        run = Run("ada", len(which) * PER_MOD, KC, 2 * P, cols_of(ada_w[layer], which[0] * D, 2 * P), None)
        s = Stage("ada", layer=layer, which=which, run=add(run), filler=filler)
        s.steps = []
        for i, w in enumerate(which):
            for j in range(PER_MOD):
                s.steps.append(("row", i * PER_MOD + j, ("ada_rows", counts.get("ada_rows", 0) + i * PER_MOD + j + 1)))
            s.steps.append(("turn", w, ("mods_summed", counts.get("mods_summed", 0) + i + 1)))
        return s.takes(ada_rows=run.n, ada_turned=len(which), mods_summed=len(which),
                       mods_ready=sum(w in (1, 2, 4, 7, 8) for w in which))

    def share(s, i, n):
        todo = [(a, k) for a in s.filler or () for k in range(len(a.steps))]
        return todo[i * len(todo) // n:(i + 1) * len(todo) // n]

    def statistics(N, after):
        s = Stage("statistics", N=N, after=after)
        s.early = 0
        if after is not None and stages[-2].kind == "proj":
            s.early = KC - stages[-2].run.cols // P
            stages[-2].next = s
        return s.takes(squares_ready=KC, square_added=KC, square_summed=1,
                                                                     log_ready=1, rstd_ready=1)

    def norm(N, after, mod=None, gain=None, before="ffn_in"):
        if after is not None:
            statistics(N, after)
        s = Stage("norm", N=N, after=after, mod=mod, gain=gain, next=before)
        s.takes(h_lo=KC)
        s.takes(**(dict(h_scaled=KC, h_hi_act=KC) if mod is None else dict(scaled_ready=KC, h_modulated=KC, h_hi_dve=KC)))
        s.h = ("h_lo", s.b["h_lo"])
        norms.append(s.h)
        return s

    norms = []

    def residual_of(run, per):
        return lambda c: (run.free, run.f0 + c // per + 1)

    def ffn(N, wi, wo, gate, between=None):
        for half in range(2):
            wi_run = add(Run("wi", HALF, KC, 2 * P, two_of(wi, half * HALF * P, wi, D_FF + half * HALF * P), "dve", 2))
            first = Stage("ffn_in", N=N, run=wi_run, h=norms[-1]).takes(silu_ready=HALF, act_hi=HALF, act_lo=HALF)
            if between is not None and half == 0:
                between()
            wo_run = add(Run("wo", KC, HALF, P, cols_of(wo, 0, P, half * HALF, HALF), "dve"))
            Stage("proj", run=wo_run, N=N, gate=gate, x="act", ready=("act_lo", first.b["act_lo"]))
        return residual_of(wo_run, 1)

    def head_units(run, N, dim, dest, ch0, rot, cos, sin, gain, name=None):
        u = Stage("heads", run=add(run), name=name, N=N, dim=dim, dest=dest, ch0=ch0, rot=rot, cos=cos, sin=sin, gain=gain, h=norms[-1])
        n = run.n
        u.takes(head_tables=1 if gain else 0, head_kept=n, head_squares=n if dim else 0, head_sums=n if dim else 0,
                head_log=n if dim else 0, head_rstd=n if dim else 0, head_rotated=n, head_cos=n, head_summed=n, head_done=n)
        return u

    def value_units(run, tiles, dest):
        return Stage("values", run=add(run), tiles=tiles, dest=dest, h=norms[-1])

    def soft(items, scale, v, out, per, waits, swap=False, filler=None, beside=None):
        n = len(items)
        return Stage("soft", items=items, scale=scale, v=v, out=out, per=per, waits=waits, swap=swap, filler=filler, beside=beside).takes(
            s_scores=n, s_masked=n, s_max=n, s_neg=n, s_probs=n, s_sink=n if items[0]["sink"] is not None else 0,
            s_total=n if items[0]["sink"] is not None else 0, s_rcp=n, s_attn=n, s_turned=n,
            s_copied=n, s_chunk=n // per, s_hi=n // per, s_out=n // per, s_swap=2 if swap else 0, s_swapped=2 if swap else 0)

    def plan_layer0():
        statistics(BOTH, None)
        ada(0, range(0, 2))
        norm(BOTH, None, mod=(0, 0))
        x = ffn(BOTH, pre_wi[0], pre_wo[0], (0, 2), between=lambda: ada(0, range(2, 5)))
        norm(BOTH, x, mod=(0, 1), before="heads")
        head_units(Run("dq", 4, KC, 2 * P, cols_of(a_w_qkv[0], 0, 2 * P), "dve"), BOTH, HD, "qk", 0, "rot_axial",
                   "cos_axial", "sin_axial", "a_q_gain")
        dk = head_units(Run("dk", 4, KC, 2 * P, cols_of(a_w_qkv[0], D, 2 * P), "dve"), BOTH, HD, "qk", KC, "rot_axial",
                        "cos_axial", "sin_axial", "a_k_gain")
        dv = value_units(Run("dv", 4, KC, 2 * P, cols_of(a_w_qkv[0], 2 * D, 2 * P), "act"), 4, "v")
        fill = [ada(0, range(5, 9), True), ada(1, range(0, 5), True)]
        s = Stage("diff", waits=[("head_done", dk.b["head_done"] + 4), ("psum_read_act", dv.run.f0 + 4)], filler=fill)
        s.takes(scores_ready=2 * NI, score_max=NI, neg_max=NI, probs_ready=2 * NI, prob_sums=NI,
                prob2_scaled=NI, attn_ready=NI, attn_turned=NI, turned_copied=NI, out_head=A_HEADS, out_kept=A_HEADS,
                lam_step=4, lam_exp=1, out_squares=A_HEADS, out_sums=A_HEADS, out_log=A_HEADS, out_rstd=A_HEADS, out_full=A_HEADS, out_hi=A_HEADS, out_ready=A_HEADS)
        run = add(Run("dwo", 4, KC, 2 * P, cols_of(a_w_o[0], 0, 2 * P), "dve"))
        Stage("proj", run=run, N=BOTH, gate=(0, 5), x="h", ready=("out_ready", s.b["out_ready"]))
        norm(BOTH, residual_of(run, 2), mod=(0, 2))
        return ffn(BOTH, post_wi[0], post_wo[0], (0, 8))

    def plan_layer1(x):
        norm(BOTH, x, mod=(1, 0))
        x = ffn(BOTH, pre_wi[1], pre_wo[1], (1, 2))
        norm(BOTH, x, mod=(1, 1), before="heads")
        head_units(Run("gq", 4, KC, 2 * P, cols_of(b_w_qkv[0], 0, 2 * P), "dve"), SEQ, HD, "gq", 0, "rot_axial",
                   "cos_axial", "sin_axial", "b_q_gain")
        k = head_units(Run("gk", 1, KC, 2 * P, cols_of(b_w_qkv[0], D, 2 * P), "dve"), BOTH, HD, "gk", 0, "rot_axial",
                       "cos_axial", "sin_axial", "b_k_gain")
        v = value_units(Run("gv", 1, KC, 2 * P, cols_of(b_w_qkv[0], D + B_KV_HEADS * HD, 2 * P), "act"), 4, "gv")
        fill = [ada(1, range(5, 9), True)]
        items = []
        for h in range(B_Q_HEADS):
            kv, side = h // B_GROUP, h % 2
            half = slice(side * HD, (side + 1) * HD)
            kc = kv // 2 + (0 if kv % 2 == side else 2)
            for q in range(SEQ // P):
                items.append(dict(q=("gq", half, h // 2, q), k=("gk", half, kc, BOTH), mask=("band", q), sink=h,
                                  tiles=4, v=slice(kv * HD, (kv + 1) * HD), lanes=half))
        s = soft(items, HD ** -0.5, "gv", "h", 4, [("head_done", k.b["head_done"] + 1), ("psum_read_act", v.run.f0 + 1)],
                 swap=True, filler=fill)
        run = add(Run("gwo", 4, KC, 2 * P, cols_of(b_w_o[0], 0, 2 * P), "dve"))
        Stage("proj", run=run, N=SEQ, gate=(1, 5), x="h", ready=("s_out", s.b["s_out"]))
        norm(SEQ, residual_of(run, 2), mod=(1, 2))
        Stage("angles").takes(angle_step=4 * 8 + 3, angle_done=4)
        return ffn(SEQ, post_wi[1], post_wo[1], (1, 8))

    def plan_second(l, x):
        w = w_in[l]
        nt = SEQ // P
        norm(SEQ, x, gain=f"g_mix{l}", before="glu")
        h = norms[-1]
        g = Stage("glu", run=add(Run("glu", 4, KC, 2 * P, two_of(w, OFF["glu"], w, OFF["glu"] + 512), "dve", 2)), l=l, h=h)
        g.takes(glu_sig=4, conv_pad=1, conv_first=2 * CB_TAPS, conv_steps=CB_TAPS, conv_steps_product=CB_TAPS - 1)
        c = Stage("cc", pair=add(Run("cc", 4, KC, 2 * P, two_of(w, OFF["cc"] + 512, w, OFF["cc"] + 1024), "dve", 2)),
                  run=add(Run("cb", 2, KC, 2 * P, cols_of(w, OFF["cc"], 2 * P), "act")), l=l, h=h)
        c.conv = g
        c.takes(cc_gate=4, cc_pad=1, cc_steps=CC_TAPS, cc_steps_product=CC_TAPS - 1, cc_full=4, cc_hi=4, cc_out=4)
        head_units(Run("aq", 2, KC, 2 * P, cols_of(w, OFF["aq"], 2 * P), "dve"), SEQ, P, "aq", 0, "rot_part128", "cos128",
                   "sin128", f"g_qa{l}", "first")
        head_units(Run("ak", 2, KC, 2 * P, cols_of(w, OFF["ak"], 2 * P), "dve"), SEQ, P, "ak", 0, "rot_part128", "cos128",
                   "sin128", f"g_ka{l}")
        head_units(Run("iq", 1, KC, 2 * P, cols_of(w, OFF["iq"], 2 * P), "dve"), SEQ, None, "iq", 0, "rot_part64", "cos64",
                   "sin64", None)
        k = head_units(Run("ik", 1, KC, P, lambda j: [
            (col, w.rearrange("(k p) m -> p k m", p=P)[:, :, OFF["ik"]:OFF["ik"] + HD]) for col in (0, HD)], "dve", 2), SEQ, HD,
            "ik", 0, "rot_part64", "cos64", "sin64", f"g_kidx{l}")
        Stage("iw", run=add(Run("iw", 1, KC, HEADS2, cols_of(w, OFF["iw"], HEADS2), "act")), h=h)
        v = value_units(Run("av", 2, KC, 2 * P, cols_of(w, OFF["av"], 2 * P), "act"), 2, "av")
        sel = Stage("select", waits=[("head_done", k.b["head_done"] + 1), ("psum_read_act", v.run.f0 + 2)])
        sel.takes(iw_turned=1, iw_kept=1, idx_scores=nt * HEADS2, idx_relu=nt * HEADS2, idx_sum=nt * HEADS2, top_steps=nt * 22, sel_mask=nt)
        q = Stage("plain", run=add(Run("sq", 4, KC, 2 * P, cols_of(w, OFF["sb"], 2 * P), "act")), h=h,
                  waits=[("idx_relu", sel.b["idx_relu"] + nt * HEADS2)])
        v2 = value_units(Run("sv", 2, KC, 2 * P, cols_of(w, OFF["sb"] + 1024, 2 * P), "act"), 2, "sv")

        def gates_of(i):
            return add(Run("gate", 4, KC, 2 * P, cols_of(w, OFF["gate"] + i * D, 2 * P), "act"))

        gates = Stage("gates", run=gates_of(0), i=0, l=l, h=h)
        sel.runs = [q.run, v2.run, gates.run]
        q.filler = v2.filler = gates.filler = sel
        items = [dict(q=("aq", slice(0, P), hd, q_), k=("ak", slice(0, P), hd, SEQ), mask=("sel", q_), sink=None, tiles=2,
                      v=slice(hd * P, (hd + 1) * P), lanes=slice(0, P), needs=("sel_mask", sel.b["sel_mask"] + q_ + 1))
                 for hd in range(HEADS2) for q_ in range(nt)]
        g1 = Stage("beside", run=gates_of(1), i=1, l=l)
        a = soft(items, P ** -0.5, "av", "oa", nt, [(gates.run.free, gates.run.f0 + 4)], beside=g1)

        def branch_of(i, name, wo, kind="branch", **more):
            run = add(Run("wo", 4, 4, 2 * P, cols_of(wo[l], 0, 2 * P, 0, 4), "dve"))
            return Stage(kind, i=i, l=l, x=name, run=run, **more).takes(merged=4)

        first = branch_of(0, "oa", w_oa, "beside")
        t = Stage("stick", waits=[("s_out", a.b["s_out"] + HEADS2), (g1.run.free, g1.run.f0 + 4)], beside=first)
        t.takes(**{n: HEADS2 for n in ("z_ready", "z_kept", "z_neg", "z_exp", "z_log", "z_soft", "z_soft_m", "z_sums", "z_arg",
                                       "z_arg_m", "z_attn", "z_out", "od_hi", "od_out")})
        n = Stage("layernorm", l=l, waits=[("od_out", t.b["od_out"] + HEADS2), ("conv_steps", g.b["conv_steps"] + CB_TAPS),
                                           ("conv_first", g.b["conv_first"] + 2 * CB_TAPS), (first.run.free, first.run.f0 + 4)])
        n.takes(ln_sum=1, ln_mean=1, ln_mid=4, ln_sq=4, ln_var=1, ln_log=1, ln_rstd=1, ln_out=4, ln_act=4, ln_hi=4, ob_out=4)
        Stage("gates", run=gates_of(2), i=2, l=l, waits=[(first.run.free, first.run.f0 + 4)], h=h, late=g1).takes(late_gates=1)
        second = branch_of(1, "ob", w_ob, waits=[("ob_out", n.b["ob_out"] + 4)])
        Stage("gates", run=gates_of(3), i=3, l=l, waits=[(second.run.free, second.run.f0 + 4)], h=h)
        branch_of(2, "oc", w_oc, waits=[("cc_out", c.b["cc_out"] + 4)])
        br = branch_of(3, "od", w_od, waits=[("od_out", t.b["od_out"] + HEADS2)])
        m = Stage("merge", ready=("merged", br.b["merged"])).takes(m_hi=KC, m_lo=KC)
        run = add(Run("merge", 4, KC, 2 * P, cols_of(w_merge[l], 0, 2 * P), "dve"))
        Stage("proj", run=run, N=SEQ, x="h", ready=("m_lo", m.b["m_lo"]))
        norm(SEQ, residual_of(run, 2), gain=f"g_ffn{l}", before="conv_in")
        for half in range(2):
            wi_run = add(Run("wi", HALF, KC, 2 * P, two_of(w_gate[l], half * HALF * P, w_up[l], half * HALF * P), "dve", 2))
            f = Stage("conv_in", run=wi_run, l=l, i=half, h=norms[-1])
            f.takes(cin_pad=1, cin_ready=HALF, tap0=HALF, tap1=HALF, tap2=HALF, silu_ready=HALF, act_hi=HALF, act_lo=HALF)
            wo_run = add(Run("wd", KC, HALF, P, cols_of(w_down[l], 0, P, half * HALF, HALF), "dve"))
            Stage("proj", run=wo_run, N=SEQ, x="act", ready=("act_lo", f.b["act_lo"]))
        return residual_of(wo_run, 1)

    x_at = plan_layer1(plan_layer0())
    for l in range(DEPTH):
        x_at = plan_second(l, x_at)

    base = (nc.sbuf_base + 63) // 64 * 64
    at = [base]

    def place(name, shape, where=None, dt=F32):
        n = 1
        for d in shape:
            n *= d
        if where is None:
            where = at[0]
            at[0] += (n * 4 + 63) // 64 * 64
        t = nc.alloc_sbuf_tensor_at(name, [P, n], dt, offset=where)
        return t[:, :] if len(shape) == 1 else t[:, :].rearrange("p (a n) -> p a n", a=shape[0])

    raw = [place(f"raw{i}", (SLOT,)) for i in range(RING)]
    w_hi = [place(f"w_hi{i}", (SLOT,), dt=F32R) for i in range(RING)]
    w_lo = [place(f"w_lo{i}", (SLOT,), dt=F32R) for i in range(RING)]
    xs = place("xs", (KC, BOTH))
    h_at = at[0]
    h_hi, h_lo = place("h_hi", (KC, BOTH), dt=F32R), place("h_lo", (KC, BOTH), dt=F32R)
    vec_sb, con_sb = place("vec_sb", (N_VEC,)), place("con_sb", (N_CON,))
    mod_sb = [place(f"mod_sb{i}", (MODC, 2)) for i in range(DEPTH)]
    cond, cond_halves = place("cond", (KC, 2)), place("cond_halves", (KC, 4), dt=F32R)
    stats = place("stats", (64,))
    pos_i = place("pos_i", (1, SEQ), dt=I32)
    arena = at[0]
    ARENA = 48 * 1024

    def over(name, at_kb, shape, dt=F32):
        return place(name, shape, arena + int(at_kb * 1024), dt)

    act_hi, act_lo = over("act_hi", 0, (HALF, BOTH), F32R), over("act_lo", 22, (HALF, BOTH), F32R)
    qk, v_lat = over("qk", 0, (2 * KC, BOTH)), over("v_lat", 32, (4, D))
    gq, gk, gv = over("gq", 0, (KC, SEQ)), over("gk", 8, (4, BOTH)), over("gv", 16, (4, B_KV_HEADS * HD))
    gates_sb = over("gates_sb", 0, (2 * KC, SEQ))
    branch = {n: tuple(over(f"{n}_{half}", 16 + 8 * i + 4 * k, (4, SEQ), F32R) for k, half in enumerate(("hi", "lo")))
              for i, n in enumerate(("oa", "ob", "oc", "od"))}
    cb_in, cb_sum = over("cb_in", 16, (4, SEQ + CB_TAPS - 1)), over("cb_sum", 28, (4, SEQ))
    cc_b, cc_sum = over("cc_b", 32, (4, SEQ)), over("cc_sum", 36, (4, SEQ))
    cb_product, cc_product = over("cb_product", 36, (4, SEQ)), over("cc_product", 16, (4, SEQ))
    cc_in = over("cc_in", 40, (4, SEQ + CC_TAPS - 1))
    iq, ik, iw_sb = over("iq", 44.25, (2, SEQ)), over("ik", 46.25, (1, SEQ)), over("iw_sb", 47.25, (2, HEADS2))
    iw_rows = over("iw_rows", 24, (SEQ,))
    spare = [place(f"spare{i}", (KC, BOTH), h_at + i * KC * BOTH * 4)[:, :, SEQ:BOTH] for i in range(2)]
    sqk, aq, ak = spare[0], spare[1][:, 0:4, :], spare[1][:, 4:8, :]
    merged = spare[1]
    at[0] += ARENA
    temp = at[0]
    TEMP = 23040

    def tmp(name, at_kb, shape, dt=F32):
        return place(name, shape, temp + int(at_kb * 1024), dt)

    sq, rstd, scaled = tmp("sq", 0, (4, BOTH)), tmp("rstd", 8, (BOTH,)), tmp("scaled", 10, (2, BOTH))
    sil = tmp("sil", 0, (RING, BOTH))
    square_sum = scaled[:, 0, :]
    kept, hr, rope_t = tmp("kept", 8, (4, BOTH)), tmp("hr", 16, (2, BOTH)), tmp("rope_t", 20, (2, SEQ))
    rot_g, rows = tmp("rot_g", 22, (P,)), tmp("rows", 18, (D,))
    full = tmp("full", 14, (RING, BOTH))
    probs, attn, attn_t = tmp("probs", 0, (4, BOTH)), tmp("attn", 8, (2, BOTH)), tmp("attn_t", 12, (2, BOTH))
    prob2, logits = tmp("prob2", 16, (BOTH,)), tmp("logits", 4, (2, BOTH))
    lam_t = tmp("lam_t", 12, (2, HD))
    rel, idx, idx_work = tmp("rel", 0, (HEADS2, SEQ)), tmp("idx", 4, (2, SEQ)), tmp("idx_work", 6, (2, SEQ))
    sel_gt, sel_eq, sel_cum = tmp("sel_gt", 8, (2, SEQ)), tmp("sel_eq", 10, (2, SEQ)), tmp("sel_cum", 12, (2, SEQ))
    sel_mask = tmp("sel_mask", 16, (2, SEQ))
    z_s, z_e, z_l, z_m, z_a = (tmp(f"z_{i}", 4 * i, (2, BOTH)) for i in range(5))
    ln_t, ln_stat = tmp("ln_t", 0, (4, SEQ)), tmp("ln_stat", 4, (2, SEQ))
    tap_t, cin = tmp("tap_t", 6, (RING, SEQ)), tmp("cin", 16, (RING, SEQ + CC_TAPS - 1))
    gated_t = tmp("gated_t", 16, (2, SEQ))
    ang = tmp("ang", 14, (8, SEQ))
    at[0] += TEMP
    assert at[0] <= nc.sbuf_usable_end, (at[0], nc.sbuf_usable_end)

    ps = [nc.alloc_psum_tensor(f"ps{i}", [P, 2, 512], F32) for i in range(RING)]
    pm = nc.alloc_psum_tensor("pm", [P, 2, 512], F32)
    bank = [ps[i // 2][:, i % 2, :] for i in range(6)]
    beside_bank = [ps[2][:, i, :].rearrange("p (m n) -> p m n", m=2) for i in range(2)]
    ADA_BANKS, ADA_FILL_BANK = [pm[:, 1, :], pm[:, 0, :]], [bank[5]]

    def vec(name, c=None):
        o, w = VEC[name]
        return vec_sb[:, o:o + w] if c is None else vec_sb[:, o + c:o + c + 1]

    ANGLES = ["cos128", "sin128", "cos64", "sin64"]
    o = CON["cos_axial"][0]
    angles = con_sb[:, o:o + 4 * SEQ].rearrange("p (a n) -> p a n", a=4)

    def con(name):
        if name in ANGLES:
            return angles[:, ANGLES.index(name), :]
        o, w = CON[name]
        return con_sb[:, o:o + w]

    landed_sem = [nc.alloc_semaphore(f"raw_landed{i}") for i in range(RING)]
    S = {name: nc.alloc_semaphore(name) for name in counts}
    x_landed, vec_landed, con_landed, out_stored, cond_ready, cond_hi_ready, cond_lo_ready = (nc.alloc_semaphore(n) for n in (
        "x_landed", "vec_landed", "con_landed", "out_stored", "cond_ready", "cond_hi_ready", "cond_lo_ready"))

    landed, per_slot = [], [0] * RING
    for t, r in enumerate(r for r in runs for _ in range(r.n)):
        per_slot[t % RING] += 16 * r.dmas
        landed.append(per_slot[t % RING])

    def sweep(eng, run, body):
        turns = (run.n - RING - 2) // RING
        if turns < 2:
            for j in range(run.n):
                body(Unit(run, j))
            return
        for j in range(RING):
            body(Unit(run, j))
        with eng.Fori(0, turns) as turn:
            for r in range(RING):
                body(Unit(run, RING + r, turn))
        for j in range(RING + turns * RING, run.n):
            body(Unit(run, j))

    def landed_at(u):
        count = landed[u.t0]
        return count if u.turn is None else u.turn * (16 * u.run.dmas) + count

    def next_split(u):
        if u.t0 + 2 >= len(units):
            return None
        run, j = units[u.t0 + 2]
        assert u.turn is None or run is u.run
        return Unit(run, j, u.turn)

    BUF = dict(qk=qk, gq=gq, gk=gk, aq=aq, ak=ak, iq=iq, ik=ik)
    VALUES = dict(v=v_lat, gv=gv)
    XS_VALUES = dict(av=0, sv=4)

    def values_of(name, k, cols):
        if name in VALUES:
            return VALUES[name][:, k, cols]
        at_col = SEQ + cols.start % SEQ
        return xs[:, XS_VALUES[name] + 2 * k + cols.start // SEQ, at_col:at_col + cols.stop - cols.start]

    def x_of(s):
        return dict(h=(h_hi, h_lo), act=(act_hi, act_lo), **branch)[s.x or "h"]

    def dest_of(s, ch):
        return BUF[s.dest][:, s.ch0 + ch, :]

    def mask_of(item):
        kind, q = item["mask"]
        return sel_mask[:, q, :] if kind == "sel" else con("band")[:, q * SEQ:(q + 1) * SEQ]

    def out_of(s, chunk):
        return tuple(t[:, chunk, 0:SEQ] for t in ((h_hi, h_lo) if s.out == "h" else branch[s.out]))

    def waits_of(eng, s):
        for name, count in s.waits:
            eng.wait_ge(S[name], count)

    block = nc.Block()
    with block:
        @block.sync
        def _(sp):
            sp.dma_start(vec_sb, vecs[:, :]).then_inc(vec_landed, 16)

            def load(u):
                run = u.run
                if u.t0 >= RING:
                    sp.wait_ge(lo_ready, u.count - RING)
                dst = raw[u.slot][:, 0:run.kc * run.cols].rearrange("p (k m) -> p k m", k=run.kc)
                for c0, src in run.src(u.j):
                    sp.dma_start(dst[:, :, c0:c0 + src.shape[2]], src).then_inc(landed_sem[u.slot], 16)
                if u.turn is None and u.t0 == RING - 1:
                    sp.dma_start(xs, x_t.rearrange("(c p) n -> p c n", p=P)).then_inc(x_landed, 16)
                    sp.dma_start(con_sb, consts[:, :]).then_inc(con_landed, 16)
                    sp.dma_start(pos_i[:, 0, :], positions[:, :]).then_inc(con_landed, 16)

            for run in runs:
                sweep(sp, run, load)
            sp.wait_ge(S["psum_read_dve"], counts["psum_read_dve"])
            sp.dma_start(out.rearrange("(c p) n -> p c n", p=P), xs[:, :, 0:SEQ]).then_inc(out_stored, 16)
            sp.wait_ge(out_stored, 16)

        @block.tensor
        def _(pe):
            def open_unit(u):
                pe.wait_ge(lo_ready, u.count)
                if u.run.by is None or u.t0 < RING or psum_users[u.t0 - RING] is None:
                    return
                free, count = psum_users[u.t0 - RING]
                if u.turn is None:
                    pe.wait_ge(S[free], count)
                else:
                    pe.wait_ge(S[u.run.free], u.out - RING)

            def weights(buf, u, k, m0, width):
                at_k = k * u.run.cols + m0
                return buf[:, at_k:at_k + width]

            def dense(u, N, x, ready=None):
                run = u.run
                x_hi, x_lo = x
                open_unit(u)
                first = ready is not None and u.turn is None and u.j0 == 0
                blocks = range(run.cols // P)
                for k, m in [(k, m) for k in range(run.kc) for m in blocks] if first else [(k, m) for m in blocks for k in range(run.kc)]:
                    if first and m == 0:
                        pe.wait_ge(S[ready[0]], ready[1] + k + 1)
                    o = ps[u.slot][:, m, 0:N]
                    hi = weights(w_hi[u.slot], u, k, m * P, P)
                    pe.matmul(o, hi, x_hi[:, k, 0:N], start=k == 0, stop=False)
                    pe.matmul(o, hi, x_lo[:, k, 0:N], start=False, stop=False)
                    last = pe.matmul(o, weights(w_lo[u.slot], u, k, m * P, P), x_hi[:, k, 0:N], start=False, stop=k == run.kc - 1)
                last.then_inc(unit_done, 1)

            def beside(s, k):
                j, m = divmod(k, 2)
                run = s.beside.run
                u = Unit(run, j)
                x_hi, x_lo = x_of(s.beside)
                if m == 0:
                    pe.wait_ge(lo_ready, u.count)
                    if j >= 2:
                        pe.wait_ge(S[run.free], u.out - 2)
                o = beside_bank[j % 2][:, m, :]
                for k in range(run.kc):
                    hi = weights(w_hi[u.slot], u, k, m * P, P)
                    pe.matmul(o, hi, x_hi[:, k, 0:SEQ], start=k == 0, stop=False)
                    pe.matmul(o, hi, x_lo[:, k, 0:SEQ], start=False, stop=False)
                    last = pe.matmul(o, weights(w_lo[u.slot], u, k, m * P, P), x_hi[:, k, 0:SEQ], start=False, stop=k == run.kc - 1)
                if m == 1:
                    last.then_inc(unit_done, 1)

            def ada_step(s, k, banks):
                kind, j, _ = s.steps[k]
                o = banks[k % len(banks)]
                if k >= len(banks):
                    name, count = s.steps[k - len(banks)][2]
                    pe.wait_ge(S[name], count)
                elif s.b["mods_summed"]:
                    pe.wait_ge(S["mods_summed"], s.b["mods_summed"])
                if kind == "row":
                    u = Unit(s.run, j)
                    open_unit(u)
                    for c in range(KC):
                        hi, lo = (weights(w[u.slot], u, c, 0, 2 * P) for w in (w_hi, w_lo))
                        if c:
                            pe.matmul(o[0:2, 0:2 * P], cond_halves[:, c - 1, 0:2], lo_before, start=False, stop=False)
                        if c == KC - 1:
                            pe.matmul(o[0:2, 0:2 * P], cond_halves[:, c, 0:2], lo, start=False, stop=False)
                        last = pe.matmul(o[0:4, 0:2 * P], cond_halves[:, c, :], hi, start=c == 0, stop=c == KC - 1)
                        lo_before = lo
                    last.then_inc(unit_done, 1)
                    return
                name, count = s.steps[k - 1][2]
                pe.wait_ge(S[name], count)
                for c in range(KC):
                    last = pe.matmul(o[:, 2 * c:2 * c + 2], rows[0:4, c * P:(c + 1) * P], con("fold")[0:4, :], start=True, stop=True)
                last.then_inc(S["ada_turned"], 1)

            def ada(s):
                if not s.filler:
                    pe.wait_ge(cond_lo_ready, 1)
                    pe.wait_ge(con_landed, 32)
                    if s.b["log_ready"]:
                        pe.wait_ge(S["log_ready"], s.b["log_ready"])
                    for k in range(len(s.steps)):
                        ada_step(s, k, ADA_BANKS)

            def fill(s, i, n):
                for a, k in share(s, i, n):
                    ada_step(a, k, ADA_FILL_BANK)

            def statistics(s):
                N, b = s.N, s.b
                pe.wait_ge(con_landed, 32)
                if b["mods_summed"]:
                    pe.wait_ge(S["mods_summed"], b["mods_summed"])
                pe.wait_ge(S["square_added"], b["square_added"] + KC)
                pe.matmul(pm[:, 0, 0:N], con("ones"), square_sum[:, 0:N], start=True, stop=True).then_inc(S["square_summed"], 1)

            def dense_run(s):
                ready = s.h if s.ready is None else s.ready
                waits_of(pe, s)
                sweep(pe, s.run, lambda u: dense(u, s.N, x_of(s), ready))

            def heads(s):
                run, N, b = s.run, s.N, s.b
                nm = run.cols // P
                for j in range(run.n + 1):
                    if j < run.n:
                        dense(Unit(run, j), N, (h_hi, h_lo), s.h)
                    if not j:
                        continue
                    i = j - 1
                    if s.dim:
                        pe.wait_ge(S["head_squares"], b["head_squares"] + j)
                        if b["head_log"] + i:
                            pe.wait_ge(S["head_log"], b["head_log"] + i)
                        ones = con("blocks" if s.dim == HD else "ones")
                        for m in range(nm):
                            last = pe.matmul(pm[:, m, 0:N], ones, sq[:, 2 * ((b["head_done"] + i) % 2) + m, 0:N], start=True, stop=True)
                        last.then_inc(S["head_sums"], 1)
                    if s.gain and not i:
                        pe.wait_ge(S["head_tables"], b["head_tables"] + 1)
                    pe.wait_ge(S["head_kept"], b["head_kept"] + j)
                    for m in range(nm):
                        last = pe.matmul(ps[Unit(run, i).slot][:, 0, m * SEQ:(m + 1) * SEQ], rot_g if s.gain else con(s.rot),
                                         kept[:, 2 * ((b["head_done"] + i) % 2) + m, 0:SEQ], start=True, stop=True)
                    last.then_inc(S["head_rotated"], 1)

            def values(s):
                run = s.run
                for j in range(run.n):
                    u = Unit(run, j)
                    open_unit(u)
                    for i in range(s.tiles):
                        o = ps[u.slot][:, i // 2, (i % 2) * run.cols:(i % 2 + 1) * run.cols]
                        tok = slice(i * P, (i + 1) * P)
                        for k in range(KC):
                            hi, lo = (weights(w[u.slot], u, k, 0, run.cols) for w in (w_hi, w_lo))
                            pe.matmul(o, h_hi[:, k, tok], hi, start=k == 0, stop=False)
                            pe.matmul(o, h_hi[:, k, tok], lo, start=False, stop=False)
                            last = pe.matmul(o, h_lo[:, k, tok], hi, start=False, stop=k == KC - 1)
                    last.then_inc(unit_done, 1)

            def diff(s):
                b = s.b
                waits_of(pe, s)

                def keys(qt):
                    return slice(0, BOTH) if qt < 2 else slice(SEQ, BOTH)

                def scores(i):
                    h, qt = divmod(i, 4)
                    if i >= 2:
                        pe.wait_ge(S["probs_ready"], b["probs_ready"] + 2 * (i - 1))
                    for c in range(2):
                        half = slice(c * HD, (c + 1) * HD)
                        n = keys(qt).stop - keys(qt).start
                        pe.matmul(bank[2 * (i % 2) + c][:, 0:n], qk[half, h, qt * P:(qt + 1) * P],
                                  qk[half, KC + h, keys(qt)], start=True, stop=True).then_inc(S["scores_ready"], 1)

                def turn(i):
                    n = 4 if i % 4 < 2 else 2
                    pe.wait_ge(S["attn_ready"], b["attn_ready"] + i + 1)
                    if i:
                        pe.wait_ge(S["turned_copied"], b["turned_copied"] + i)
                    for k in range(n):
                        last = pe.transpose(bank[4][:, k * P:(k + 1) * P], attn[:, i % 2, k * P:(k + 1) * P], con("ident"))
                    last.then_inc(S["attn_turned"], 1)

                def weigh(i):
                    h, qt = divmod(i, 4)
                    pe.wait_ge(S["turned_copied"], b["turned_copied"] + i + 1)
                    if qt == 0 and h >= 2:
                        pe.wait_ge(S["out_log"], b["out_log"] + h - 1)
                    tiles = range(4) if qt < 2 else range(2, 4)
                    for n, k in enumerate(tiles):
                        last = pe.matmul(pm[:, h % 2, qt * P:(qt + 1) * P], v_lat[:, k, h * P:(h + 1) * P],
                                         attn_t[:, i % 2, n * P:(n + 1) * P], start=n == 0, stop=n == len(tiles) - 1)
                    if qt == 3:
                        last.then_inc(S["out_head"], 1)

                def head_out(i):
                    h, step = divmod(i - 7, 4)
                    if step == 0 and 0 <= h < A_HEADS:
                        pe.wait_ge(S["out_squares"], b["out_squares"] + h + 1)
                        pe.matmul(pm[:, h % 2, :], con("ones"), qk[:, KC + h, :], start=True, stop=True).then_inc(S["out_sums"], 1)

                scores(0)
                scores(1)
                for i in range(NI):
                    fill(s, i, NI)
                    if i + 2 < NI:
                        scores(i + 2)
                    head_out(i)
                    turn(i)
                    if i:
                        weigh(i - 1)
                weigh(NI - 1)
                for i in range(NI, 4 * A_HEADS + 4):
                    head_out(i)
                name, count = s.filler[-1].steps[-1][2]
                pe.wait_ge(S[name], count)

            def soft(s):
                b, items = s.b, s.items
                n = len(items)
                waits_of(pe, s)
                if s.swap:
                    for c in range(2):
                        pe.matmul(bank[c], con("swap"), gk[:, c, :], start=True, stop=True).then_inc(S["s_swap"], 1)
                    pe.wait_ge(S["s_swapped"], b["s_swapped"] + 2)

                def scores(i):
                    it = items[i]
                    (qb, lanes, qc, q), (kb, _, kc, nk) = it["q"], it["k"]
                    if i >= s.depth:
                        pe.wait_ge(S["s_masked"], b["s_masked"] + i + 1 - s.depth)
                    pe.matmul(bank[i % s.depth][:, 0:nk], BUF[qb][lanes, qc, q * P:(q + 1) * P], BUF[kb][lanes, kc, 0:nk],
                              start=True, stop=True).then_inc(S["s_scores"], 1)

                def turn(i):
                    pe.wait_ge(S["s_attn"], b["s_attn"] + i + 1)
                    if i >= 2:
                        pe.wait_ge(S["s_copied"], b["s_copied"] + i - 1)
                    for k in range(items[i]["tiles"]):
                        last = pe.transpose(bank[s.depth + i % 2][:, k * P:(k + 1) * P], attn[:, i % 2, k * P:(k + 1) * P],
                                            con("ident"))
                    last.then_inc(S["s_turned"], 1)

                def weigh(i):
                    it = items[i]
                    q = it["q"][3]
                    chunk = i // s.per
                    pe.wait_ge(S["s_copied"], b["s_copied"] + i + 1)
                    if i % s.per == 0 and chunk >= 2:
                        pe.wait_ge(S["s_out"], b["s_out"] + chunk - 1)
                    for k in range(it["tiles"]):
                        last = pe.matmul(pm[it["lanes"], chunk % 2, q * P:(q + 1) * P], values_of(s.v, k, it["v"]),
                                         attn_t[:, i % 2, k * P:(k + 1) * P], start=k == 0, stop=k == it["tiles"] - 1)
                    if i % s.per == s.per - 1:
                        last.then_inc(S["s_chunk"], 1)

                for i in range(min(2, n)):
                    scores(i)
                for i in range(n):
                    fill(s, i, n)
                    if s.beside:
                        beside(s, i)
                    if i + 2 < n:
                        scores(i + 2)
                    turn(i)
                    if i:
                        weigh(i - 1)
                weigh(n - 1)

            def iw(s):
                u = Unit(s.run, 0)
                open_unit(u)
                o = ps[u.slot][0:HEADS2, 0, 0:SEQ]
                for k in range(KC):
                    hi, lo = (weights(w[u.slot], u, k, 0, HEADS2) for w in (w_hi, w_lo))
                    pe.matmul(o, hi, h_hi[:, k, 0:SEQ], start=k == 0, stop=False)
                    pe.matmul(o, hi, h_lo[:, k, 0:SEQ], start=False, stop=False)
                    last = pe.matmul(o, lo, h_hi[:, k, 0:SEQ], start=False, stop=k == KC - 1)
                last.then_inc(unit_done, 1)

            def select(s):
                b = s.b
                waits_of(pe, s)
                for q in range(2):
                    last = pe.transpose(pm[:, 1, q * HEADS2:(q + 1) * HEADS2], iw_rows[0:HEADS2, q * P:(q + 1) * P],
                                        con("ident")[0:HEADS2, 0:HEADS2])
                last.then_inc(S["iw_turned"], 1)
                for q in range(2):
                    for h in range(HEADS2):
                        half = slice(h % 2 * HD, (h % 2 + 1) * HD)
                        if q:
                            pe.wait_ge(S["idx_relu"], b["idx_relu"] + h + 1)
                        pe.matmul(bank[h][:, 0:SEQ], iq[half, h // 2, q * P:(q + 1) * P], ik[half, 0, :], start=True,
                                  stop=True).then_inc(S["idx_scores"], 1)

            def cc(s):
                sweep(pe, s.pair, lambda u: dense(u, SEQ, (h_hi, h_lo)))
                sweep(pe, s.run, lambda u: dense(u, SEQ, (h_hi, h_lo)))

            def gates(s):
                sweep(pe, s.run, lambda u: dense(u, SEQ, (h_hi, h_lo)))

            def stick(s):
                b = s.b
                waits_of(pe, s)

                def scores(h):
                    if h >= 2:
                        pe.wait_ge(S["z_kept"], b["z_kept"] + h - 1)
                    for k in range(2):
                        last = pe.matmul(bank[h % 2][:, k * SEQ:(k + 1) * SEQ], sqk[:, 4 + h, k * P:(k + 1) * P], sqk[:, h, :],
                                         start=True, stop=True)
                    last.then_inc(S["z_ready"], 1)

                def sums(h):
                    pe.wait_ge(S["z_soft_m"], b["z_soft_m"] + h + 1)
                    if h >= 2:
                        pe.wait_ge(S["z_arg"], b["z_arg"] + h - 1)
                    m = z_m[:, h % 2, :]
                    o = bank[2 + h % 2]
                    pe.matmul(o[:, 0:SEQ], con("suffix"), m[:, 0:SEQ], start=True, stop=False)
                    pe.matmul(o[:, 0:SEQ], con("ones"), m[:, SEQ:], start=False, stop=True)
                    pe.matmul(o[:, SEQ:], con("suffix"), m[:, SEQ:], start=True, stop=True).then_inc(S["z_sums"], 1)

                def weigh(h):
                    pe.wait_ge(S["z_attn"], b["z_attn"] + h + 1)
                    if h >= 2:
                        pe.wait_ge(S["od_out"], b["od_out"] + h - 1)
                    for k in range(2):
                        last = pe.matmul(pm[:, h % 2, 0:SEQ], values_of("sv", k, slice(h * P, (h + 1) * P)),
                                         z_a[:, h % 2, k * SEQ:(k + 1) * SEQ], start=k == 0, stop=k == 1)
                    last.then_inc(S["z_out"], 1)

                scores(0)
                scores(1)
                for pair in range(0, HEADS2, 2):
                    beside(s, 2 * pair)
                    beside(s, 2 * pair + 1)
                    for h in range(pair + 2, min(pair + 4, HEADS2)):
                        scores(h)
                    sums(pair)
                    sums(pair + 1)
                    beside(s, 2 * pair + 2)
                    beside(s, 2 * pair + 3)
                    weigh(pair)
                    weigh(pair + 1)

            def layernorm(s):
                b = s.b
                waits_of(pe, s)
                for c in range(4):
                    last = pe.matmul(pm[:, 0, 0:SEQ], con("ones"), cb_sum[:, c, :], start=c == 0, stop=c == 3)
                last.then_inc(S["ln_sum"], 1)
                for c in range(4):
                    pe.wait_ge(S["ln_sq"], b["ln_sq"] + c + 1)
                    last = pe.matmul(pm[:, 1, 0:SEQ], con("ones"), ln_t[:, c, :], start=c == 0, stop=c == 3)
                last.then_inc(S["ln_var"], 1)

            def branch_out(s):
                waits_of(pe, s)
                sweep(pe, s.run, lambda u: dense(u, SEQ, x_of(s)))

            todo = dict(ada=ada, statistics=statistics, ffn_in=dense_run, proj=dense_run, heads=heads, values=values, diff=diff, soft=soft,
                        iw=iw, select=select, glu=dense_run, cc=cc, plain=dense_run, gates=gates, stick=stick,
                        layernorm=layernorm, branch=branch_out, conv_in=dense_run)
            for s in stages:
                if s.kind in todo:
                    todo[s.kind](s)

        @block.scalar
        def _(act):
            LOG_EXP = "natural_log_exp_and_others"

            def rsqrt(o, mean_square, log_signal, log_count, signal):
                nc.scalar.activation(o, mean_square, ACT.Ln, bias=con("eps")).then_inc(S[log_signal], 1)
                act.wait_ge(S[log_signal], log_count)
                nc.scalar.activation(o, o, ACT.Exp, scale=-0.5).then_inc(S[signal], 1)

            def split(u):
                if u is None:
                    return
                n = u.run.kc * u.run.cols
                act.wait_ge(landed_sem[u.slot], landed_at(u))
                if u.t0 >= RING:
                    act.wait_ge(unit_done, u.count - RING)
                nc.scalar.copy(w_hi[u.slot][:, 0:n], raw[u.slot][:, 0:n]).then_inc(hi_ready, 1)

            def split_ahead(u):
                split(next_split(u))

            def splits_only(s):
                sweep(act, s.run, split_ahead)

            def gate_out(s, u, products, function):
                act.wait_ge(unit_done, u.count)
                for m in range(2):
                    c = 2 * u.j + m
                    last = nc.scalar.activation(gates_sb[:, s.i % 2 * KC + c, :], products[:, m, :], function,
                                                bias=vec(f"b_gate{s.l}", s.i * KC + c))
                last.then_inc(S[s.run.free], 1)

            def ada_split(s, k):
                kind, j, _ = s.steps[k]
                if kind == "row":
                    split_ahead(Unit(s.run, j))

            def ada_row(s, k, banks):
                kind, j, _ = s.steps[k]
                if kind == "row":
                    act.wait_ge(unit_done, Unit(s.run, j).count)
                    i = j % PER_MOD
                    if i == 0 and s.b["ada_turned"] + j // PER_MOD:
                        act.wait_ge(S["ada_turned"], s.b["ada_turned"] + j // PER_MOD)
                    nc.scalar.copy(rows[0:4, i * 2 * P:(i + 1) * 2 * P], banks[k % len(banks)][0:4, 0:2 * P]).then_inc(S["ada_rows"], 1)

            def ada(s):
                if not s.filler:
                    for k in range(len(s.steps)):
                        ada_split(s, k)
                        ada_row(s, k, ADA_BANKS)

            def fill_split(s, i, n):
                for a, k in share(s, i, n)[:1]:
                    ada_split(a, k)

            def fill(s, i, n):
                for m, (a, k) in enumerate(share(s, i, n)):
                    if m:
                        ada_split(a, k)
                    ada_row(a, k, ADA_FILL_BANK)

            def statistics(s):
                N, b = s.N, s.b
                nc.scalar.preload_act_table_set(LOG_EXP)
                if s.after is None:
                    act.wait_ge(x_landed, 16)
                for c in range(KC):
                    if s.after is not None:
                        name, count = s.after(c)
                        act.wait_ge(S[name], count)
                    if c >= 4:
                        act.wait_ge(S["square_added"], b["square_added"] + c - 3)
                    nc.scalar.activation(sq[:, c % 4, 0:N], xs[:, c, 0:N], ACT.Square,
                                         scale=D ** -0.5).then_inc(S["squares_ready"], 1)
                act.wait_ge(S["square_summed"], b["square_summed"] + 1)
                rsqrt(rstd[:, 0:N], pm[:, 0, 0:N], "log_ready", b["log_ready"] + 1, "rstd_ready")

            def norm(s):
                N, b = s.N, s.b
                if s.next in ("ffn_in", "conv_in"):
                    nc.scalar.preload_act_table(ACT.Silu)
                elif s.next == "glu":
                    nc.scalar.preload_act_table(ACT.Sigmoid)
                if s.gain is not None:
                    for c in range(KC):
                        act.wait_ge(S["h_scaled"], b["h_scaled"] + c + 1)
                        nc.scalar.copy(h_hi[:, c, 0:N], full[:, c % RING, 0:N]).then_inc(S["h_hi_act"], 1)
                    return
                layer, which = s.mod
                act.wait_ge(S["mods_summed"], b["mods_summed"])
                act.wait_ge(S["mods_ready"], b["mods_ready"])
                for c in range(KC):
                    act.wait_ge(S["scaled_ready"], b["scaled_ready"] + c + 1)
                    if c >= RING:
                        act.wait_ge(S["h_lo"], b["h_lo"] + c - RING + 1)
                    for st in range(N // SEQ):
                        tok = slice(st * SEQ, (st + 1) * SEQ)
                        last = nc.scalar.activation(
                            full[:, c % RING, tok], scaled[:, c % 2, tok], ACT.Identity,
                            bias=mod_sb[layer][:, 3 * which * KC + c, st:st + 1],
                            scale=mod_sb[layer][:, (3 * which + 1) * KC + c, st:st + 1])
                    last.then_inc(S["h_modulated"], 1)

            def ffn_in(s):
                N, b, run = s.N, s.b, s.run

                def silu(u):
                    split_ahead(u)
                    act.wait_ge(unit_done, u.count)
                    if u.j0 >= RING:
                        act.wait_ge(S["act_lo"], u.j + (b["act_lo"] + 1 - RING))
                    nc.scalar.activation(sil[:, u.j0 % RING, 0:N], ps[u.slot][:, 0, 0:N],
                                         ACT.Silu).then_inc(S["silu_ready"], 1)

                sweep(act, run, silu)

            def heads(s):
                run, N, b = s.run, s.N, s.b
                nm = run.cols // P

                def deviation(i):
                    act.wait_ge(S["head_sums"], b["head_sums"] + i + 1)
                    if b["head_done"] + i:
                        act.wait_ge(S["head_done"], b["head_done"] + i)
                    rsqrt(hr[:, 0:nm, 0:N], pm[:, 0:nm, 0:N], "head_log", b["head_log"] + i + 1, "head_rstd")

                if s.name == "first":
                    nc.scalar.preload_act_table_set(LOG_EXP)
                for j in range(run.n):
                    u = Unit(run, j)
                    split_ahead(u)
                    act.wait_ge(unit_done, u.count)
                    g = b["head_done"] + j
                    if g >= 2:
                        act.wait_ge(S["head_done"], g - 1)
                    two = slice(2 * (g % 2), 2 * (g % 2) + nm)
                    nc.scalar.copy(kept[:, two, 0:N], ps[u.slot][:, 0:nm, 0:N]).then_inc(S["head_kept"], 1)
                    if s.dim:
                        act.wait_ge(S["head_kept"], b["head_kept"] + j + 1)
                        nc.scalar.activation(sq[:, two, 0:N], kept[:, two, 0:N], ACT.Square,
                                             scale=s.dim ** -0.5).then_inc(S["head_squares"], 1)
                    if s.dim and j:
                        deviation(j - 1)
                if s.dim:
                    deviation(run.n - 1)

            def values(s):
                run = s.run
                for j in range(run.n):
                    u = Unit(run, j)
                    split_ahead(u)
                    act.wait_ge(unit_done, u.count)
                    for i in range(s.tiles // 2):
                        src = ps[u.slot][:, i, :].rearrange("p (t c) -> p t c", t=2)
                        if s.dest in XS_VALUES:
                            dst = xs[:, XS_VALUES[s.dest] + j:XS_VALUES[s.dest] + 4:2, SEQ:BOTH]
                        else:
                            dst = VALUES[s.dest][:, 2 * i:2 * i + 2, j * run.cols:(j + 1) * run.cols]
                        last = nc.scalar.copy(dst, src)
                    last.then_inc(S[run.free], 1)

            def diff(s):
                b = s.b
                act.wait_ge(S["lam_step"], b["lam_step"] + 2)
                nc.scalar.activation(stats[:, 2:4], stats[:, 0:2], ACT.Exp).then_inc(S["lam_exp"], 1)

                def turned(i):
                    n = BOTH if i % 4 < 2 else CTX
                    act.wait_ge(S["attn_turned"], b["attn_turned"] + i + 1)
                    nc.scalar.copy(attn_t[:, i % 2, 0:n], bank[4][:, 0:n]).then_inc(S["turned_copied"], 1)
                    if i % 4 == 0 and i >= 4:
                        keep(i // 4 - 1)

                def keep(h):
                    act.wait_ge(S["out_head"], b["out_head"] + h + 1)
                    nc.scalar.copy(qk[:, h, :], pm[:, h % 2, :]).then_inc(S["out_kept"], 1)

                def head_out(i):
                    h, step = divmod(i - 6, 4)
                    if step == 0 and 0 <= h < A_HEADS:
                        act.wait_ge(S["out_kept"], b["out_kept"] + h + 1)
                        nc.scalar.activation(qk[:, KC + h, :], qk[:, h, :], ACT.Square, scale=P ** -0.5).then_inc(S["out_squares"], 1)
                    h, step = divmod(i - 8, 4)
                    if step == 0 and 0 <= h < A_HEADS:
                        act.wait_ge(S["out_sums"], b["out_sums"] + h + 1)
                        rsqrt(qk[:, KC + h, :], pm[:, h % 2, :], "out_log", b["out_log"] + h + 1, "out_rstd")

                for i in range(NI):
                    n = BOTH if i % 4 < 2 else CTX
                    act.wait_ge(S["neg_max"], b["neg_max"] + i + 1)
                    if i >= 2:
                        act.wait_ge(S["attn_ready"], b["attn_ready"] + i - 1)
                    for c in range(2):
                        r = 2 * (i % 2) + c
                        nc.scalar.activation(probs[:, r, 0:n], bank[r][:, 0:n], ACT.Exp, bias=stats[:, 16 + r:17 + r],
                                             scale=HD ** -0.5, accum_out=stats[:, 20 + r:21 + r]).then_inc(S["probs_ready"], 1)
                    if i:
                        turned(i - 1)
                    fill_split(s, i, NI)
                    fill(s, i, NI)
                    head_out(i)
                turned(NI - 1)
                keep(A_HEADS - 1)
                for i in range(NI, 4 * A_HEADS + 5):
                    head_out(i)

            def angles_(s):
                for i in range(4):
                    act.wait_ge(S["angle_step"], 3 + 8 * (i + 1))
                    nc.scalar.activation(angles[:, i, :], ang[:, 2 + i, :], ACT.Sin).then_inc(S["angle_done"], 1)

            def soft(s):
                b, n = s.b, len(s.items)
                if s.out == "oa":
                    nc.scalar.preload_act_table_set(LOG_EXP)

                def copied(i):
                    nk = s.items[i]["k"][3]
                    act.wait_ge(S["s_turned"], b["s_turned"] + i + 1)
                    nc.scalar.copy(attn_t[:, i % 2, 0:nk], bank[s.depth + i % 2][:, 0:nk]).then_inc(S["s_copied"], 1)

                for i in range(n):
                    it = s.items[i]
                    nk = it["k"][3]
                    act.wait_ge(S["s_neg"], b["s_neg"] + i + 1)
                    if i >= 2:
                        act.wait_ge(S["s_attn"], b["s_attn"] + i - 1)
                    nc.scalar.activation(probs[:, i % 2, 0:nk], logits[:, i % 2, 0:nk], ACT.Exp, bias=stats[:, 10 + i % 2:11 + i % 2],
                                         accum_out=stats[:, 12 + i % 2:13 + i % 2]).then_inc(S["s_probs"], 1)
                    if it["sink"] is not None:
                        nc.scalar.activation(stats[:, 14 + i % 2:15 + i % 2], vec("sink", it["sink"]), ACT.Exp,
                                             bias=stats[:, 10 + i % 2:11 + i % 2]).then_inc(S["s_sink"], 1)
                    fill_split(s, i, n)
                    if s.beside and i % 2 == 0:
                        split_ahead(Unit(s.beside.run, i // 2))
                    if i:
                        copied(i - 1)
                    fill(s, i, n)
                    if s.beside and i % 2:
                        gate_out(s.beside, Unit(s.beside.run, i // 2), beside_bank[i // 2 % 2], ACT.Identity)
                copied(n - 1)

            def iw(s):
                u = Unit(s.run, 0)
                split_ahead(u)
                act.wait_ge(unit_done, u.count)
                nc.scalar.copy(iw_rows[0:HEADS2, :], ps[u.slot][0:HEADS2, 0, 0:SEQ]).then_inc(S[s.run.free], 1)

            def select(s):
                b = s.b
                act.wait_ge(S["iw_turned"], b["iw_turned"] + 1)
                nc.scalar.copy(iw_sb, pm[:, 1, 0:2 * HEADS2].rearrange("p (t h) -> p t h", t=2)).then_inc(S["iw_kept"], 1)
                for q in range(2):
                    for h in range(HEADS2):
                        i = q * HEADS2 + h
                        act.wait_ge(S["idx_scores"], b["idx_scores"] + i + 1)
                        if q:
                            act.wait_ge(S["idx_sum"], b["idx_sum"] + h + 1)
                        nc.scalar.activation(rel[:, h, :], bank[h][:, 0:SEQ], ACT.Relu,
                                             scale=(HD * HEADS2) ** -0.5).then_inc(S["idx_relu"], 1)

            def glu(s):
                b = s.b

                def gate(u):
                    split_ahead(u)
                    act.wait_ge(unit_done, u.count)
                    if u.j >= RING:
                        act.wait_ge(S[s.run.free], u.out - RING)
                    nc.scalar.activation(sil[:, u.j % RING, 0:SEQ], ps[u.slot][:, 1, 0:SEQ], ACT.Sigmoid).then_inc(S["glu_sig"], 1)

                sweep(act, s.run, gate)

            def cc(s):
                b = s.b

                def first(u):
                    split_ahead(u)
                    act.wait_ge(unit_done, u.count)
                    if u.j < RING:
                        name, count = s.pair.free, s.pair.f0
                    else:
                        name, count = s.pair.free, u.out - RING
                    act.wait_ge(S[name], count)
                    nc.scalar.copy(sil[:, u.j % RING, 0:SEQ], ps[u.slot][:, 0, 0:SEQ]).then_inc(S["cc_gate"], 1)

                def outer(u):
                    split_ahead(u)
                    act.wait_ge(unit_done, u.count)
                    nc.scalar.copy(cc_b[:, 2 * u.j:2 * u.j + 2, :], ps[u.slot][:, :, 0:SEQ]).then_inc(S[s.run.free], 1)

                sweep(act, s.pair, first)
                sweep(act, s.run, outer)

            def plain(s):
                def keep(u):
                    split_ahead(u)
                    act.wait_ge(unit_done, u.count)
                    nc.scalar.copy(sqk[:, 2 * u.j:2 * u.j + 2, :], ps[u.slot][:, :, 0:SEQ]).then_inc(S[s.run.free], 1)

                sweep(act, s.run, keep)

            def stick(s):
                b = s.b

                def kept(h):
                    r = h % 2
                    act.wait_ge(S["z_ready"], b["z_ready"] + h + 1)
                    if h >= 2:
                        act.wait_ge(S["z_arg"], b["z_arg"] + h - 1)
                    nc.scalar.activation(z_s[:, r, :], bank[r], ACT.Copy, scale=P ** -0.5).then_inc(S["z_kept"], 1)

                def exp(h):
                    r = h % 2
                    act.wait_ge(S["z_neg"], b["z_neg"] + h + 1)
                    nc.scalar.activation(z_e[:, r, :], z_e[:, r, :], ACT.Exp).then_inc(S["z_exp"], 1)

                def log(h):
                    r = h % 2
                    act.wait_ge(S["z_exp"], b["z_exp"] + h + 1)
                    if h >= 2:
                        act.wait_ge(S["z_soft_m"], b["z_soft_m"] + h - 1)
                    nc.scalar.activation(z_l[:, r, :], z_e[:, r, :], ACT.Ln, bias=1.0).then_inc(S["z_log"], 1)

                def weights_(h):
                    act.wait_ge(S["z_arg_m"], b["z_arg_m"] + h + 1)
                    if h >= 2:
                        act.wait_ge(S["z_out"], b["z_out"] + h - 1)
                    nc.scalar.activation(z_a[:, h % 2, :], z_e[:, h % 2, :], ACT.Exp).then_inc(S["z_attn"], 1)

                kept(0)
                kept(1)
                for pair in range(0, HEADS2, 2):
                    split_ahead(Unit(s.beside.run, pair))
                    for step in (exp, log):
                        step(pair)
                        step(pair + 1)
                    split_ahead(Unit(s.beside.run, pair + 1))
                    for h in range(pair + 2, min(pair + 4, HEADS2)):
                        kept(h)
                    weights_(pair)
                    weights_(pair + 1)

            def layernorm(s):
                b = s.b
                for c in range(4):
                    act.wait_ge(S["ln_mid"], b["ln_mid"] + c + 1)
                    nc.scalar.activation(ln_t[:, c, :], cb_sum[:, c, :], ACT.Square,
                                         scale=512 ** -0.5).then_inc(S["ln_sq"], 1)
                act.wait_ge(S["ln_var"], b["ln_var"] + 1)
                rsqrt(ln_stat[:, 1, :], pm[:, 1, 0:SEQ], "ln_log", b["ln_log"] + 1, "ln_rstd")
                for c in range(4):
                    act.wait_ge(S["ln_out"], b["ln_out"] + c + 1)
                    nc.scalar.activation(cb_sum[:, c, :], cb_sum[:, c, :], ACT.Silu, bias=vec(f"ln_b{s.l}", c),
                                         scale=vec(f"ln_g{s.l}", c)).then_inc(S["ln_act"], 1)

            def gates(s):
                waits_of(act, s)
                if s.late is not None:
                    late = gates_sb[:, s.late.i * KC:(s.late.i + 1) * KC, :]
                    act.wait_ge(S[s.late.run.free], s.late.run.f0 + 4)
                    nc.scalar.activation(late, late, ACT.Sigmoid).then_inc(S["late_gates"], 1)

                def gate(u):
                    split_ahead(u)
                    gate_out(s, u, ps[u.slot][:, :, 0:SEQ], ACT.Sigmoid)

                sweep(act, s.run, gate)

            def merge(s):
                for c in range(KC):
                    act.wait_ge(S["merged"], s.ready[1] + c // 2 + 1)
                    nc.scalar.copy(h_hi[:, c, 0:SEQ], merged[:, c, :]).then_inc(S["m_hi"], 1)

            def conv_in(s):
                b, run = s.b, s.run

                def keep(u):
                    split_ahead(u)
                    act.wait_ge(unit_done, u.count)
                    if u.j0 >= RING:
                        act.wait_ge(S["act_lo"], u.j + (b["act_lo"] + 1 - RING))
                    r = u.j0 % RING
                    nc.scalar.copy(cin[:, r, CC_TAPS - 1:], ps[u.slot][:, 0, 0:SEQ]).then_inc(S["cin_ready"], 1)
                    act.wait_ge(S["tap2"], u.j + (b["tap2"] + 1))
                    nc.scalar.activation(sil[:, r, 0:SEQ], tap_t[:, r, :], ACT.Silu).then_inc(S["silu_ready"], 1)

                sweep(act, run, keep)

            todo = dict(ada=ada, statistics=statistics, norm=norm, ffn_in=ffn_in, heads=heads, values=values, diff=diff, angles=angles_, soft=soft,
                        iw=iw, select=select, glu=glu, cc=cc, plain=plain, stick=stick, layernorm=layernorm, gates=gates,
                        conv_in=conv_in, proj=splits_only, branch=splits_only, merge=merge)
            act.wait_ge(vec_landed, 16)
            nc.scalar.activation(cond, vec("cond").rearrange("p (c s) -> p c s", s=2), ACT.Silu).then_inc(cond_ready, 1)
            act.wait_ge(cond_ready, 1)
            nc.scalar.copy(cond_halves[:, :, 0:2], cond).then_inc(cond_hi_ready, 1)
            split(Unit(*units[0]))
            split(Unit(*units[1]))
            for s in stages:
                if s.kind in todo:
                    todo[s.kind](s)

        @block.vector
        def _(dve):
            def split(u):
                if u is None:
                    return
                n = u.run.kc * u.run.cols
                dve.wait_ge(hi_ready, u.count)
                nc.vector.tensor_tensor(w_lo[u.slot][:, 0:n], raw[u.slot][:, 0:n], w_hi[u.slot][:, 0:n].bitcast(F32),
                                        ALU.subtract).then_inc(lo_ready, 1)

            def split_ahead(u):
                split(next_split(u))

            def splits_only(s):
                if s.filler is None:
                    sweep(dve, s.run, split_ahead)

            def add_branch(s, u, products):
                b, run = s.b, s.run
                dve.wait_ge(unit_done, u.count)
                two = slice(2 * u.j, 2 * u.j + 2)
                o = merged[:, two, :] if s.i == 0 else gated_t
                gate = gates_sb[:, s.i % 2 * KC + 2 * u.j:s.i % 2 * KC + 2 * u.j + 2, :]
                nc.vector.tensor_tensor(o, gate, products, ALU.mult).then_inc(S[run.free], 1)
                dve.wait_ge(S[run.free], u.out)
                if s.i == 0:
                    dve.sem_inc(S["merged"], 1)
                else:
                    nc.vector.tensor_tensor(merged[:, two, :], merged[:, two, :], gated_t, ALU.add).then_inc(S["merged"], 1)
                    dve.wait_ge(S["merged"], b["merged"] + u.j + 1)

            def halves(o, src, hi_signal, lo_signal, count):
                hi, lo = o
                nc.vector.tensor_copy(hi, src).then_inc(S[hi_signal], 1)
                dve.wait_ge(S[hi_signal], count)
                nc.vector.tensor_tensor(lo, src, hi.bitcast(F32), ALU.subtract).then_inc(S[lo_signal], 1)

            def ada_mods(s, k, banks):
                kind, which, done = s.steps[k]
                if kind == "row":
                    split_ahead(Unit(s.run, which))
                    return
                at_w = s.which.index(which)
                bias = vec(f"ada_b{s.layer}").rearrange("p (c s) -> p c s", s=2)
                part = slice(which * KC, (which + 1) * KC)
                one = mod_sb[s.layer][:, part, :]
                dve.wait_ge(S["ada_turned"], s.b["ada_turned"] + at_w + 1)
                nc.vector.tensor_tensor(one, banks[k % len(banks)][:, 0:2 * KC].rearrange("p (c s) -> p c s", s=2),
                                        bias[:, part, :], ALU.add).then_inc(S["mods_summed"], 1)
                if which in (1, 2, 4, 7, 8):
                    dve.wait_ge(S["mods_summed"], done[1])
                if which % 3 == 1:
                    nc.vector.tensor_scalar(one, one, 1.0, None, ALU.add).then_inc(S["mods_ready"], 1)
                elif which in (2, 8):
                    nc.vector.tensor_scalar(one, one, 0.5, None, ALU.mult).then_inc(S["mods_ready"], 1)

            def ada(s):
                if not s.filler:
                    dve.wait_ge(vec_landed, 16)
                    for k in range(len(s.steps)):
                        ada_mods(s, k, ADA_BANKS)

            def fill(s, i, n):
                for a, k in share(s, i, n):
                    ada_mods(a, k, ADA_FILL_BANK)

            def add_squares(s, chunks):
                N, b = s.N, s.b
                for c in chunks:
                    dve.wait_ge(S["squares_ready"], b["squares_ready"] + c + 1)
                    if c:
                        dve.wait_ge(S["square_added"], b["square_added"] + c)
                        ins = nc.vector.tensor_tensor(square_sum[:, 0:N], square_sum[:, 0:N], sq[:, c % 4, 0:N], ALU.add)
                    else:
                        ins = nc.vector.tensor_copy(square_sum[:, 0:N], sq[:, 0, 0:N])
                    ins.then_inc(S["square_added"], 1)

            def statistics(s):
                add_squares(s, range(s.early, KC))

            def norm(s):
                N, b = s.N, s.b
                if s.after is None:
                    dve.wait_ge(x_landed, 16)
                else:
                    name, count = s.after(KC - 1)
                    dve.wait_ge(S[name], count)
                dve.wait_ge(S["rstd_ready"], b["rstd_ready"])
                if s.gain is not None:
                    for c in range(KC + 2):
                        if c < KC:
                            if c >= RING:
                                dve.wait_ge(S["h_lo"], b["h_lo"] + c - RING + 1)
                            nc.vector.scalar_tensor_tensor(full[:, c % RING, 0:N], xs[:, c, 0:N], vec(s.gain, c), rstd[:, 0:N],
                                                           ALU.mult, ALU.mult).then_inc(S["h_scaled"], 1)
                        if c >= 2:
                            dve.wait_ge(S["h_hi_act"], b["h_hi_act"] + c - 1)
                            nc.vector.tensor_tensor(h_lo[:, c - 2, 0:N], full[:, (c - 2) % RING, 0:N],
                                                    h_hi[:, c - 2, 0:N].bitcast(F32), ALU.subtract).then_inc(S["h_lo"], 1)
                    return
                for c in range(KC + 1):
                    if c < KC:
                        if c >= 2:
                            dve.wait_ge(S["h_modulated"], b["h_modulated"] + c - 1)
                        nc.vector.tensor_tensor(scaled[:, c % 2, 0:N], xs[:, c, 0:N], rstd[:, 0:N],
                                                ALU.mult).then_inc(S["scaled_ready"], 1)
                    if c:
                        dve.wait_ge(S["h_modulated"], b["h_modulated"] + c)
                        nc.vector.tensor_copy(h_hi[:, c - 1, 0:N], full[:, (c - 1) % RING, 0:N]).then_inc(S["h_hi_dve"], 1)

            def proj(s):
                run = s.run
                if s.gate is not None:
                    dve.wait_ge(S["mods_summed"], s.b["mods_summed"])
                    dve.wait_ge(S["mods_ready"], s.b["mods_ready"])

                def add_on(u):
                    split_ahead(u)
                    per = run.cols // P
                    if s.next is not None and u.j0 == run.n - 1:
                        add_squares(s.next, range(s.next.early))
                    dve.wait_ge(unit_done, u.count)
                    if s.gate is None:
                        xc = xs[:, bass.ds(u.j * per, per), 0:SEQ]
                        nc.vector.tensor_tensor(xc, ps[u.slot][:, 0:per, 0:SEQ], xc, ALU.add).then_inc(S[run.free], 1)
                        return
                    layer, which = s.gate
                    for m in range(per):
                        c = u.j * per + m
                        for st in range(s.N // SEQ):
                            tok = slice(st * SEQ, (st + 1) * SEQ)
                            xc = xs[:, bass.ds(c, 1), tok].rearrange("p c n -> p (c n)")
                            g = mod_sb[layer][:, bass.ds(c + which * KC, 1), st:st + 1].rearrange("p c n -> p (c n)")
                            last = nc.vector.scalar_tensor_tensor(xc, ps[u.slot][:, m, tok], g, xc, ALU.mult, ALU.add)
                    last.then_inc(S[run.free], 1)

                sweep(dve, run, add_on)

            def ffn_in(s):
                N, b, run = s.N, s.b, s.run

                def gated(u):
                    split_ahead(u)
                    r = u.j0 % RING
                    dve.wait_ge(S["silu_ready"], u.j + (b["silu_ready"] + 1))
                    nc.vector.tensor_tensor(sil[:, r, 0:N], sil[:, r, 0:N], ps[u.slot][:, 1, 0:N], ALU.mult).then_inc(S[run.free], 1)
                    dve.wait_ge(S[run.free], u.out)
                    nc.vector.tensor_copy(act_hi[:, bass.ds(u.j, 1), 0:N].rearrange("p c n -> p (c n)"),
                                          sil[:, r, 0:N]).then_inc(S["act_hi"], 1)

                sweep(dve, run, gated)

            def heads(s):
                run, N, b = s.run, s.N, s.b
                nm = run.cols // P
                if s.cos in ANGLES:
                    dve.wait_ge(S["angle_done"], 4)
                if s.gain:
                    nc.vector.tensor_scalar(rot_g, con(s.rot), vec(s.gain), None, ALU.mult).then_inc(S["head_tables"], 1)
                for i in range(run.n):
                    u = Unit(run, i)
                    split_ahead(u)
                    two = 2 * ((b["head_done"] + i) % 2)
                    dve.wait_ge(S["head_kept"], b["head_kept"] + i + 1)
                    for m in range(nm):
                        o, x = dest_of(s, i * nm + m)[:, 0:SEQ], kept[:, two + m, 0:SEQ]
                        if s.gain:
                            last = nc.vector.scalar_tensor_tensor(o, x, vec(s.gain), con(s.cos), ALU.mult, ALU.mult)
                        else:
                            last = nc.vector.tensor_tensor(o, x, con(s.cos), ALU.mult)
                    last.then_inc(S["head_cos"], 1)
                    if s.dim:
                        dve.wait_ge(S["head_rstd"], b["head_rstd"] + i + 1)
                    dve.wait_ge(S["head_rotated"], b["head_rotated"] + i + 1)
                    for m in range(nm):
                        last = nc.vector.tensor_tensor(rope_t[:, m, :], ps[u.slot][:, 0, m * SEQ:(m + 1) * SEQ], con(s.sin),
                                                       ALU.mult)
                    last.then_inc(S[run.free], 1)
                    dve.wait_ge(S[run.free], u.out)
                    ch = s.ch0 + i * nm
                    o = BUF[s.dest][:, ch:ch + nm, 0:SEQ]
                    ins = nc.vector.tensor_tensor(o, o, rope_t[:, 0:nm, :], ALU.add)
                    if not s.dim:
                        ins.then_inc(S["head_summed"], 1)
                        dve.wait_ge(S["head_summed"], b["head_summed"] + i + 1)
                        dve.sem_inc(S["head_done"], 1)
                        continue
                    ins.then_inc(S["head_summed"], 1)
                    for m in range(nm if N > SEQ else 0):
                        nc.vector.scalar_tensor_tensor(dest_of(s, i * nm + m)[:, SEQ:N], kept[:, two + m, SEQ:N], vec(s.gain),
                                                       hr[:, m, SEQ:N], ALU.mult, ALU.mult)
                    dve.wait_ge(S["head_summed"], b["head_summed"] + i + 1)
                    nc.vector.tensor_tensor(o, o, hr[:, 0:nm, 0:SEQ], ALU.mult).then_inc(S["head_done"], 1)

            def diff(s):
                b = s.b
                lam = vec("lambda").rearrange("p (a d) -> p a d", a=4)
                steps = [b["lam_step"]]

                def step(ins):
                    steps[0] += 1
                    ins.then_inc(S["lam_step"], 1)
                    dve.wait_ge(S["lam_step"], steps[0])

                waits_of(dve, s)
                step(nc.vector.tensor_tensor(lam_t, lam[:, 0:4:2, :], lam[:, 1:4:2, :], ALU.mult))
                step(nc.vector.tensor_reduce(stats[:, 0:2], lam_t, AX, ALU.add))
                dve.wait_ge(S["lam_exp"], b["lam_exp"] + 1)
                step(nc.vector.scalar_tensor_tensor(stats[:, 4:5], stats[:, 2:3], LAM_INIT, stats[:, 3:4], ALU.add, ALU.subtract))
                step(nc.vector.tensor_scalar(stats[:, 5:6], vec("a_subln"), 1.0 - LAM_INIT, None, ALU.mult))

                def maxima(i):
                    n = BOTH if i % 4 < 2 else CTX
                    r = 2 * (i % 2)
                    dve.wait_ge(S["scores_ready"], b["scores_ready"] + 2 * i + 2)
                    nc.vector.tensor_reduce(stats[:, 8 + r:10 + r], ps[i % 2][:, :, 0:n], AX, ALU.max).then_inc(S["score_max"], 1)

                def negative(i):
                    r = 2 * (i % 2)
                    dve.wait_ge(S["score_max"], b["score_max"] + i + 1)
                    nc.vector.tensor_scalar(stats[:, 16 + r:18 + r], stats[:, 8 + r:10 + r], -(HD ** -0.5), None,
                                            ALU.mult).then_inc(S["neg_max"], 1)

                def reciprocals(i):
                    r = 2 * (i % 2)
                    dve.wait_ge(S["probs_ready"], b["probs_ready"] + 2 * i + 2)
                    nc.vector.reciprocal(stats[:, 24 + r:26 + r], stats[:, 20 + r:22 + r]).then_inc(S["prob_sums"], 1)

                def combine(i):
                    n = BOTH if i % 4 < 2 else CTX
                    r = 2 * (i % 2)
                    dve.wait_ge(S["prob_sums"], b["prob_sums"] + i + 1)
                    nc.vector.tensor_scalar(prob2[:, 0:n], probs[:, r + 1, 0:n], stats[:, 25 + r:26 + r], stats[:, 4:5],
                                            ALU.mult, ALU.mult).then_inc(S["prob2_scaled"], 1)
                    dve.wait_ge(S["prob2_scaled"], b["prob2_scaled"] + i + 1)
                    if i >= 2:
                        dve.wait_ge(S["attn_turned"], b["attn_turned"] + i - 1)
                    nc.vector.scalar_tensor_tensor(attn[:, i % 2, 0:n], probs[:, r, 0:n], stats[:, 24 + r:25 + r],
                                                   prob2[:, 0:n], ALU.mult, ALU.subtract).then_inc(S["attn_ready"], 1)

                def head_out(i):
                    h, step = divmod(i - 9, 4)
                    if step == 0 and 0 <= h < A_HEADS:
                        dve.wait_ge(S["out_rstd"], b["out_rstd"] + h + 1)
                        nc.vector.scalar_tensor_tensor(qk[:, h, :], qk[:, h, :], stats[:, 5:6], qk[:, KC + h, :], ALU.mult,
                                                       ALU.mult).then_inc(S["out_full"], 1)
                        dve.wait_ge(S["out_full"], b["out_full"] + h + 1)
                        nc.vector.tensor_copy(h_hi[:, h, :], qk[:, h, :]).then_inc(S["out_hi"], 1)

                maxima(0)
                negative(0)
                for i in range(NI):
                    if i + 1 < NI:
                        maxima(i + 1)
                    reciprocals(i)
                    if i + 1 < NI:
                        negative(i + 1)
                    combine(i)
                    head_out(i)
                    fill(s, i, NI)
                for i in range(NI, 4 * A_HEADS + 6):
                    head_out(i)

            def merge(s):
                for c in range(KC):
                    dve.wait_ge(S["m_hi"], s.b["m_hi"] + c + 1)
                    nc.vector.tensor_tensor(h_lo[:, c, 0:SEQ], merged[:, c, :], h_hi[:, c, 0:SEQ].bitcast(F32),
                                            ALU.subtract).then_inc(S["m_lo"], 1)

            def angles_(s):
                count = [0]

                def step(ins):
                    ins.then_inc(S["angle_step"], 1)
                    count[0] += 1
                    dve.wait_ge(S["angle_step"], count[0])

                turn = 2 * math.pi
                parts = [6.28125, 0.0019350051879882812]
                parts.append(turn - parts[0] - parts[1])
                magic = 1.5 * 2.0 ** 23
                dve.wait_ge(S["h_lo"], s.b["h_lo"])
                step(nc.vector.tensor_copy(ang[:, 0, :], pos_i[:, 0, :]))
                step(nc.vector.tensor_scalar(ang[:, 6, :], ang[:, 0, :], con("freq128"), None, ALU.mult))
                step(nc.vector.tensor_scalar(ang[:, 7, :], ang[:, 0, :], con("freq64"), None, ALU.mult))
                for i in range(4):
                    a, r, k = ang[:, 6 + i // 2, :], ang[:, 2 + i, :], ang[:, 1, :]
                    quarter = 0.25 if i % 2 == 0 else 0.0
                    step(nc.vector.tensor_scalar(k, a, 1.0 / turn, quarter, ALU.mult, ALU.add))
                    step(nc.vector.tensor_scalar(k, k, magic, None, ALU.add))
                    step(nc.vector.tensor_scalar(k, k, magic, None, ALU.subtract))
                    step(nc.vector.scalar_tensor_tensor(r, k, -parts[0], a, ALU.mult, ALU.add))
                    step(nc.vector.scalar_tensor_tensor(r, k, -parts[1], r, ALU.mult, ALU.add))
                    step(nc.vector.scalar_tensor_tensor(r, k, -parts[2], r, ALU.mult, ALU.add))
                    step(nc.vector.tensor_scalar(r, r, quarter * turn, None, ALU.add))
                    step(nc.vector.tensor_scalar(r, r, 3.1415925, -3.1415925, ALU.min, ALU.max))

            def soft(s):
                b, n = s.b, len(s.items)
                if s.swap:
                    for c in range(2):
                        dve.wait_ge(S["s_swap"], b["s_swap"] + c + 1)
                        nc.vector.tensor_copy(gk[:, 2 + c, :], bank[c]).then_inc(S["s_swapped"], 1)

                def masked(i):
                    it = s.items[i]
                    nk, r = it["k"][3], i % 2
                    dve.wait_ge(S["s_scores"], b["s_scores"] + i + 1)
                    if i >= 2:
                        dve.wait_ge(S["s_probs"], b["s_probs"] + i - 1)
                    if "needs" in it:
                        dve.wait_ge(S[it["needs"][0]], it["needs"][1])
                    if nk > SEQ:
                        nc.vector.tensor_scalar(logits[:, r, SEQ:nk], bank[i % s.depth][:, SEQ:nk], s.scale, None, ALU.mult)
                    nc.vector.scalar_tensor_tensor(logits[:, r, 0:SEQ], bank[i % s.depth][:, 0:SEQ], s.scale, mask_of(it), ALU.mult,
                                                   ALU.add).then_inc(S["s_masked"], 1)

                def maximum(i):
                    nk, r = s.items[i]["k"][3], i % 2
                    dve.wait_ge(S["s_masked"], b["s_masked"] + i + 1)
                    nc.vector.tensor_reduce(stats[:, 8 + r:9 + r], logits[:, r, 0:nk], AX, ALU.max).then_inc(S["s_max"], 1)

                def negative(i):
                    it, r = s.items[i], i % 2
                    dve.wait_ge(S["s_max"], b["s_max"] + i + 1)
                    if it["sink"] is not None:
                        nc.vector.tensor_scalar(stats[:, 10 + r:11 + r], stats[:, 8 + r:9 + r], vec("sink", it["sink"]), -1.0,
                                                ALU.max, ALU.mult).then_inc(S["s_neg"], 1)
                    else:
                        nc.vector.tensor_scalar(stats[:, 10 + r:11 + r], stats[:, 8 + r:9 + r], -1.0, None,
                                                ALU.mult).then_inc(S["s_neg"], 1)

                def total(i):
                    it, r = s.items[i], i % 2
                    dve.wait_ge(S["s_probs"], b["s_probs"] + i + 1)
                    if it["sink"] is not None:
                        dve.wait_ge(S["s_sink"], b["s_sink"] + i + 1)
                        nc.vector.tensor_tensor(stats[:, 16 + r:17 + r], stats[:, 12 + r:13 + r], stats[:, 14 + r:15 + r],
                                                ALU.add).then_inc(S["s_total"], 1)

                def reciprocal(i):
                    r = i % 2
                    whole = stats[:, 12 + r:13 + r]
                    if s.items[i]["sink"] is not None:
                        dve.wait_ge(S["s_total"], b["s_total"] + i + 1)
                        whole = stats[:, 16 + r:17 + r]
                    nc.vector.reciprocal(stats[:, 18 + r:19 + r], whole).then_inc(S["s_rcp"], 1)

                def normed(i):
                    nk, r = s.items[i]["k"][3], i % 2
                    dve.wait_ge(S["s_rcp"], b["s_rcp"] + i + 1)
                    if i >= 2:
                        dve.wait_ge(S["s_turned"], b["s_turned"] + i - 1)
                    nc.vector.tensor_scalar(attn[:, r, 0:nk], probs[:, r, 0:nk], stats[:, 18 + r:19 + r], None,
                                            ALU.mult).then_inc(S["s_attn"], 1)

                def chunk_out(chunk):
                    dve.wait_ge(S["s_chunk"], b["s_chunk"] + chunk + 1)
                    halves(out_of(s, chunk), pm[:, chunk % 2, 0:SEQ], "s_hi", "s_out", b["s_hi"] + chunk + 1)

                if s.out == "oa":
                    dve.wait_ge(S["cc_out"], b["cc_out"])
                for step in (masked, maximum, negative):
                    step(0)
                for i in range(n):
                    for following, step in ((masked, total), (maximum, reciprocal), (negative, normed)):
                        if i + 1 < n:
                            following(i + 1)
                        step(i)
                    fill(s, i, n)
                    if s.beside and i % 2 == 0:
                        split_ahead(Unit(s.beside.run, i // 2))
                    if i >= 2 and (i - 2) % s.per == s.per - 1:
                        chunk_out((i - 2) // s.per)
                for chunk in range((n - 2) // s.per, n // s.per):
                    chunk_out(chunk)

            def iw(s):
                split_ahead(Unit(s.run, 0))

            def select(s):
                b = s.b
                dve.wait_ge(S["iw_kept"], b["iw_kept"] + 1)
                for q in range(2):
                    for h in range(HEADS2):
                        i = q * HEADS2 + h
                        dve.wait_ge(S["idx_relu"], b["idx_relu"] + i + 1)
                        before = con("causal")[:, q * SEQ:(q + 1) * SEQ] if h == 0 else idx[:, q, :]
                        nc.vector.scalar_tensor_tensor(idx[:, q, :], rel[:, h, :], iw_sb[:, q, h:h + 1], before, ALU.mult,
                                                       ALU.add).then_inc(S["idx_sum"], 1)
                        dve.wait_ge(S["idx_sum"], b["idx_sum"] + i + 1)
                count = [b["top_steps"]]
                last = [0, 0]

                def step(q, ins):
                    count[0] += 1
                    last[q] = count[0]
                    ins.then_inc(S["top_steps"], 1)

                def wait_last(q):
                    if last[q]:
                        dve.wait_ge(S["top_steps"], last[q])

                behind = [Unit(run, j) for run in s.runs for j in range(run.n)]
                turns = [0]

                def each(body):
                    for q in range(2):
                        wait_last(q)
                        step(q, body(q))
                    turns[0] += 1
                    if turns[0] % 2 == 0 and turns[0] // 2 <= len(behind):
                        split_ahead(behind[turns[0] // 2 - 1])

                top = [stats[:, 24 + 8 * q:32 + 8 * q] for q in range(2)]
                cur = [idx[:, q, :] for q in range(2)]
                work = [idx_work[:, q, :] for q in range(2)]
                for r in range(TOPK // 8):
                    each(lambda q: nc.vector.max(top[q], cur[q]))
                    if r < TOPK // 8 - 1:
                        each(lambda q: nc.vector.match_replace(work[q], top[q], cur[q], LOWEST))
                        cur = work
                least = [top[q][:, 7:8] for q in range(2)]
                above = [stats[:, 40 + q:41 + q] for q in range(2)]
                need = [stats[:, 42 + q:43 + q] for q in range(2)]
                gt, eq, cum = ([t[:, q, :] for q in range(2)] for t in (sel_gt, sel_eq, sel_cum))
                each(lambda q: nc.vector.tensor_scalar(gt[q], idx[:, q, :], least[q], None, ALU.is_gt, ALU.add, accum_out=above[q]))
                each(lambda q: nc.vector.tensor_scalar(eq[q], idx[:, q, :], least[q], None, ALU.is_equal))
                each(lambda q: nc.vector.tensor_tensor_scan(cum[q], eq[q], eq[q], 0.0, ALU.add, ALU.max))
                each(lambda q: nc.vector.tensor_scalar(need[q], above[q], -1.0, float(TOPK), ALU.mult, ALU.add))
                each(lambda q: nc.vector.scalar_tensor_tensor(eq[q], cum[q], need[q], eq[q], ALU.is_le, ALU.mult))
                each(lambda q: nc.vector.tensor_tensor(gt[q], gt[q], eq[q], ALU.add))
                each(lambda q: nc.vector.tensor_scalar(gt[q], gt[q], -NEG, NEG, ALU.mult, ALU.add))
                for u in behind[turns[0] // 2:]:
                    split_ahead(u)
                for q in range(2):
                    wait_last(q)
                    nc.vector.tensor_tensor(sel_mask[:, q, :], gt[q], con("causal")[:, q * SEQ:(q + 1) * SEQ],
                                            ALU.add).then_inc(S["sel_mask"], 1)

            def glu(s):
                def gated(u):
                    split_ahead(u)
                    dve.wait_ge(S["glu_sig"], s.b["glu_sig"] + u.j + 1)
                    nc.vector.tensor_tensor(cb_in[:, u.j, CB_TAPS - 1:], sil[:, u.j % RING, 0:SEQ], ps[u.slot][:, 0, 0:SEQ],
                                            ALU.mult).then_inc(S[s.run.free], 1)

                sweep(dve, s.run, gated)

            def cc(s):
                units = s.pair.n + s.run.n
                share = -(-CB_TAPS // units)

                def conv_taps(i):
                    l, base = s.l, s.conv.b["conv_first"]
                    for w in range(i * share, min((i + 1) * share, CB_TAPS)):
                        for c in range(2):
                            x, wcol = cb_in[:, c, w:w + SEQ], vec(f"cb_w{l}", c * CB_TAPS + w)
                            if w == 0:
                                ins = nc.vector.tensor_scalar(cb_sum[:, c, :], x, wcol, vec(f"cb_b{l}", c), ALU.mult, ALU.add)
                            else:
                                dve.wait_ge(S["conv_first"], base + 2 * (w - 1) + c + 1)
                                ins = nc.vector.scalar_tensor_tensor(cb_sum[:, c, :], x, wcol, cb_sum[:, c, :], ALU.mult, ALU.add)
                            ins.then_inc(S["conv_first"], 1)

                def gated(u):
                    split_ahead(u)
                    dve.wait_ge(S["cc_gate"], s.b["cc_gate"] + u.j + 1)
                    nc.vector.tensor_tensor(cc_in[:, u.j, CC_TAPS - 1:], sil[:, u.j % RING, 0:SEQ], ps[u.slot][:, 1, 0:SEQ],
                                            ALU.mult).then_inc(S[s.pair.free], 1)
                    conv_taps(u.j)

                def outer(u):
                    split_ahead(u)
                    conv_taps(s.pair.n + u.j)

                conv = s.conv
                dve.wait_ge(S["conv_pad"], conv.b["conv_pad"] + 1)
                dve.wait_ge(S[conv.run.free], conv.run.f0 + conv.run.n)
                sweep(dve, s.pair, gated)
                sweep(dve, s.run, outer)

            def stick(s):
                b = s.b

                def negative(h):
                    r = h % 2
                    dve.wait_ge(S["z_kept"], b["z_kept"] + h + 1)
                    if h >= 2:
                        dve.wait_ge(S["z_attn"], b["z_attn"] + h - 1)
                    nc.vector.scalar_tensor_tensor(z_e[:, r, :], z_s[:, r, :], -1.0, z_s[:, r, :], ALU.mult,
                                                   ALU.min).then_inc(S["z_neg"], 1)

                def softplus(h):
                    r = h % 2
                    dve.wait_ge(S["z_log"], b["z_log"] + h + 1)
                    nc.vector.scalar_tensor_tensor(z_l[:, r, :], z_s[:, r, :], 0.0, z_l[:, r, :], ALU.max,
                                                   ALU.add).then_inc(S["z_soft"], 1)

                def argument(h):
                    r = h % 2
                    dve.wait_ge(S["z_sums"], b["z_sums"] + h + 1)
                    nc.vector.tensor_tensor(z_e[:, r, :], z_s[:, r, :], bank[2 + r], ALU.subtract).then_inc(S["z_arg"], 1)

                def keep(h):
                    dve.wait_ge(S["z_out"], b["z_out"] + h + 1)
                    halves(tuple(t[:, h, :] for t in branch["od"]), pm[:, h % 2, 0:SEQ], "od_hi", "od_out", b["od_hi"] + h + 1)

                def beside(j):
                    u = Unit(s.beside.run, j)
                    split_ahead(u)
                    add_branch(s.beside, u, beside_bank[j % 2])

                dve.wait_ge(S["cc_out"], s.b["cc_out"])
                negative(0)
                negative(1)
                for pair in range(0, HEADS2, 2):
                    beside(pair)
                    for step in (softplus, argument):
                        step(pair)
                        step(pair + 1)
                    for h in range(pair + 2, min(pair + 4, HEADS2)):
                        negative(h)
                    beside(pair + 1)
                    keep(pair)
                    keep(pair + 1)

            def layernorm(s):
                b = s.b
                ob = cb_sum
                mean, dev = ln_stat[:, 0, :], ln_stat[:, 1, :]
                dve.wait_ge(S["ln_sum"], b["ln_sum"] + 1)
                nc.vector.tensor_scalar(mean, pm[:, 0, 0:SEQ], 1.0 / 512, None, ALU.mult).then_inc(S["ln_mean"], 1)
                dve.wait_ge(S["ln_mean"], b["ln_mean"] + 1)
                for c in range(4):
                    nc.vector.tensor_tensor(ob[:, c, :], ob[:, c, :], mean, ALU.subtract).then_inc(S["ln_mid"], 1)
                dve.wait_ge(S["ln_rstd"], b["ln_rstd"] + 1)
                for c in range(4):
                    nc.vector.tensor_tensor(ob[:, c, :], ob[:, c, :], dev, ALU.mult).then_inc(S["ln_out"], 1)
                for c in range(4):
                    dve.wait_ge(S["ln_act"], b["ln_act"] + c + 1)
                    hi, lo = (t[:, c, :] for t in branch["ob"])
                    halves((hi, lo), ob[:, c, :], "ln_hi", "ob_out", b["ln_hi"] + c + 1)

            def branch_out(s):
                def weigh(u):
                    split_ahead(u)
                    add_branch(s, u, ps[u.slot][:, :, 0:SEQ])

                if s.i == 1:
                    dve.wait_ge(S["late_gates"], s.b["late_gates"])
                sweep(dve, s.run, weigh)

            def conv_in(s):
                b, l, run = s.b, s.l, s.run
                dve.wait_ge(S["h_lo"], s.h[1] + KC)
                nc.vector.memset(cin[:, :, 0:CC_TAPS - 1], 0.0).then_inc(S["cin_pad"], 1)
                dve.wait_ge(S["cin_pad"], b["cin_pad"] + 1)
                o = VEC[f"ffn_w{l}"][0] + s.i * HALF * CC_TAPS

                def taps(u):
                    split_ahead(u)
                    r = u.j0 % RING
                    dve.wait_ge(S["cin_ready"], u.j + (b["cin_ready"] + 1))
                    for w in range(CC_TAPS):
                        wcol = vec_sb[:, bass.ds(u.j * CC_TAPS + (o + w), 1)]
                        x = cin[:, r, w:w + SEQ]
                        if w == 0:
                            ins = nc.vector.tensor_scalar(tap_t[:, r, :], x, wcol, None, ALU.mult)
                        else:
                            dve.wait_ge(S[f"tap{w - 1}"], u.j + (b[f"tap{w - 1}"] + 1))
                            ins = nc.vector.scalar_tensor_tensor(tap_t[:, r, :], x, wcol, tap_t[:, r, :], ALU.mult, ALU.add)
                        ins.then_inc(S[f"tap{w}"], 1)
                    dve.wait_ge(S["silu_ready"], u.j + (b["silu_ready"] + 1))
                    nc.vector.tensor_tensor(sil[:, r, 0:SEQ], sil[:, r, 0:SEQ], ps[u.slot][:, 1, 0:SEQ],
                                            ALU.mult).then_inc(S[run.free], 1)
                    dve.wait_ge(S[run.free], u.out)
                    nc.vector.tensor_copy(act_hi[:, bass.ds(u.j, 1), 0:SEQ].rearrange("p c n -> p (c n)"),
                                          sil[:, r, 0:SEQ]).then_inc(S["act_hi"], 1)

                sweep(dve, run, taps)

            todo = dict(ada=ada, statistics=statistics, norm=norm, ffn_in=ffn_in, proj=proj, heads=heads, diff=diff, angles=angles_, soft=soft,
                        select=select, glu=glu, cc=cc, stick=stick, layernorm=layernorm, branch=branch_out, conv_in=conv_in, values=splits_only,
                        iw=iw, plain=splits_only, gates=splits_only, merge=merge)
            dve.wait_ge(cond_hi_ready, 1)
            nc.vector.tensor_tensor(cond_halves[:, :, 2:4], cond, cond_halves[:, :, 0:2].bitcast(F32),
                                    ALU.subtract).then_inc(cond_lo_ready, 1)
            split(Unit(*units[0]))
            split(Unit(*units[1]))
            for s in stages:
                if s.kind in todo:
                    todo[s.kind](s)

        @block.gpsimd
        def _(pool):
            def rest(o, whole, hi, signal):
                nc.gpsimd.tensor_tensor(o, whole, hi.bitcast(F32), ALU.subtract).then_inc(S[signal], 1)

            def norm(s):
                N, b = s.N, s.b
                if s.mod is None:
                    return
                for c in range(KC):
                    pool.wait_ge(S["h_hi_dve"], b["h_hi_dve"] + c + 1)
                    rest(h_lo[:, c, 0:N], full[:, c % RING, 0:N], h_hi[:, c, 0:N], "h_lo")

            def act_lows(s):
                N, b = s.N, s.b

                def lows(u):
                    pool.wait_ge(S["act_hi"], u.j + (b["act_hi"] + 1))
                    o, hi = (t[:, bass.ds(u.j, 1), 0:N].rearrange("p c n -> p (c n)") for t in (act_lo, act_hi))
                    rest(o, sil[:, u.j0 % RING, 0:N], hi, "act_lo")

                sweep(pool, s.run, lows)

            def diff(s):
                for h in range(A_HEADS):
                    pool.wait_ge(S["out_hi"], s.b["out_hi"] + h + 1)
                    rest(h_lo[:, h, :], qk[:, h, :], h_hi[:, h, :], "out_ready")

            def conv(src, dst, product, chunks, weights_of, bias_of, taps, signal, base):
                for w in range(taps):
                    if w:
                        pool.wait_ge(S[signal], base + w)
                    for c in range(chunks.start, chunks.stop):
                        x = src[:, c, w:w + SEQ]
                        if w == 0 and bias_of is not None:
                            ins = nc.gpsimd.tensor_scalar(dst[:, c, :], x, weights_of(c, w), bias_of(c), ALU.mult, ALU.add)
                        else:
                            ins = nc.gpsimd.tensor_scalar((product if w else dst)[:, c, :], x, weights_of(c, w), None, ALU.mult)
                    if not w:
                        ins.then_inc(S[signal], 1)
                        continue
                    ins.then_inc(S[signal + "_product"], 1)
                    pool.wait_ge(S[signal + "_product"], base // taps * (taps - 1) + w)
                    nc.gpsimd.tensor_tensor(dst[:, chunks, :], dst[:, chunks, :], product[:, chunks, :],
                                            ALU.add).then_inc(S[signal], 1)

            def glu(s):
                b, l = s.b, s.l
                pool.wait_ge(S[s.run.free], s.run.f0 + 1)
                nc.gpsimd.memset(cb_in[:, :, 0:CB_TAPS - 1], 0.0).then_inc(S["conv_pad"], 1)
                pool.wait_ge(S["conv_pad"], b["conv_pad"] + 1)
                pool.wait_ge(S[s.run.free], s.run.f0 + 4)
                conv(cb_in, cb_sum, cb_product, slice(2, 4), lambda c, w: vec(f"cb_w{l}", c * CB_TAPS + w), lambda c: vec(f"cb_b{l}", c), CB_TAPS,
                     "conv_steps", b["conv_steps"])

            def cc(s):
                b, l = s.b, s.l
                nc.gpsimd.memset(cc_in[:, :, 0:CC_TAPS - 1], 0.0).then_inc(S["cc_pad"], 1)
                pool.wait_ge(S["cc_pad"], b["cc_pad"] + 1)
                pool.wait_ge(S[s.pair.free], s.pair.f0 + 4)
                pool.wait_ge(S["conv_first"], s.conv.b["conv_first"] + 2 * CB_TAPS)
                conv(cc_in, cc_sum, cc_product, slice(0, 4), lambda c, w: vec(f"cc_w{l}", c * CC_TAPS + w), None, CC_TAPS, "cc_steps", b["cc_steps"])
                pool.wait_ge(S[s.run.free], s.run.f0 + 2)
                for c in range(4):
                    pool.wait_ge(S["cc_steps"], b["cc_steps"] + CC_TAPS)
                    hi, lo = (t[:, c, :] for t in branch["oc"])
                    nc.gpsimd.tensor_tensor(cc_sum[:, c, :], cc_sum[:, c, :], cc_b[:, c, :], ALU.mult).then_inc(S["cc_full"], 1)
                    pool.wait_ge(S["cc_full"], b["cc_full"] + c + 1)
                    nc.gpsimd.tensor_copy(hi, cc_sum[:, c, :]).then_inc(S["cc_hi"], 1)
                    pool.wait_ge(S["cc_hi"], b["cc_hi"] + c + 1)
                    rest(lo, cc_sum[:, c, :], hi, "cc_out")

            def stick(s):
                b = s.b

                def mask(dst, src, fill, signal):
                    nc.gpsimd.affine_select(out=dst.rearrange("p (k t) -> p k t", k=2), in_=src.rearrange("p (k t) -> p k t", k=2),
                                            pattern=[[-P, 2], [1, SEQ]], compare_op=ALU.is_gt, fill=fill, base=0,
                                            channel_multiplier=-1).then_inc(S[signal], 1)

                for pair in range(0, HEADS2, 2):
                    for h in (pair, pair + 1):
                        pool.wait_ge(S["z_soft"], b["z_soft"] + h + 1)
                        if h >= 2:
                            pool.wait_ge(S["z_sums"], b["z_sums"] + h - 1)
                        mask(z_m[:, h % 2, :], z_l[:, h % 2, :], 0.0, "z_soft_m")
                    for h in (pair, pair + 1):
                        pool.wait_ge(S["z_arg"], b["z_arg"] + h + 1)
                        mask(z_e[:, h % 2, :], z_e[:, h % 2, :], NEG, "z_arg_m")

            todo = dict(norm=norm, ffn_in=act_lows, conv_in=act_lows, diff=diff, glu=glu, cc=cc, stick=stick)
            for s in stages:
                if s.kind in todo:
                    todo[s.kind](s)


INS = ["ada_w", "ffn_pre_wi", "ffn_pre_wo", "ffn_post_wi", "ffn_post_wo", "a_w_qkv", "a_w_o", "b_w_qkv", "b_w_o",
       "w_in_2", "w_oa_2", "w_ob_2", "w_oc_2", "w_od_2", "w_merge_2", "w_ffn_gate_2", "w_ffn_up_2", "w_ffn_down_2"]


def lay_out(inputs):
    arr = {k: np.asarray(v) for k, v in inputs.items()}
    x_t = np.concatenate([arr["x"][0].T, arr["ctx"][0].T], axis=1)
    vecs = np.zeros((P, N_VEC), np.float32)

    def put(name, a):
        o, w = VEC[name]
        vecs[:, o:o + w] = np.ascontiguousarray(a).reshape(P, w)

    def lanes(a):
        return a.reshape(-1, P).T

    put("cond", np.stack([lanes(arr["c"][0]), lanes(arr["c_ctx"])], axis=-1))
    for l in range(DEPTH):
        put(f"ada_b{l}", np.repeat(lanes(arr["ada_b"][l])[:, :, None], 2, axis=2))
    for name, key in (("a_q_gain", "a_q_gain"), ("a_k_gain", "a_k_gain"), ("b_q_gain", "b_q_gain"), ("b_k_gain", "b_k_gain")):
        put(name, np.tile(arr[key][0], 2))
    put("a_subln", arr["a_subln_gain"][0])
    put("lambda", np.broadcast_to(arr["a_lambda"][0].reshape(1, -1), (P, 4 * HD)))
    put("sink", np.broadcast_to(arr["b_sink"][0].reshape(1, -1), (P, B_Q_HEADS)))
    for l in range(DEPTH):
        put(f"g_mix{l}", lanes(arr["g_mix_2"][l]))
        put(f"b_gate{l}", lanes(arr["b_gate_2"][l]))
        put(f"g_qa{l}", arr["g_qa_2"][l])
        put(f"g_ka{l}", arr["g_ka_2"][l])
        put(f"g_kidx{l}", np.tile(arr["g_kidx_2"][l], 2))
        put(f"cb_w{l}", arr["cb_conv_w_2"][l].T.reshape(4, P, CB_TAPS).transpose(1, 0, 2))
        put(f"cb_b{l}", lanes(arr["cb_conv_b_2"][l]))
        put(f"ln_g{l}", lanes(arr["cb_ln_g_2"][l]))
        put(f"ln_b{l}", lanes(arr["cb_ln_b_2"][l]))
        put(f"cc_w{l}", arr["cc_conv_w_2"][l].T.reshape(4, P, CC_TAPS).transpose(1, 0, 2))
        put(f"g_ffn{l}", lanes(arr["g_ffn_2"][l]))
        put(f"ffn_w{l}", arr["ffn_conv_w_2"][l].T.reshape(FC, P, CC_TAPS).transpose(1, 0, 2))
    pos = np.ascontiguousarray(np.broadcast_to(arr["positions_2"].reshape(1, SEQ), (P, SEQ)))
    arrays = {"x_t": np.ascontiguousarray(x_t), "vecs": vecs, "consts": shape_constants(), "positions": pos}
    for name in INS:
        arrays[name] = np.ascontiguousarray(arr[name])
    return arrays


def kernel(**inputs):
    import concourse.bacc as bacc
    from concourse.bass_utils import run_bass_kernel_spmd

    arrays = lay_out(inputs)
    nc = bacc.Bacc("TRN2", target_bir_lowering=False, num_devices=1)
    args = [nc.dram_tensor(f"in_{n}", a.shape, mybir.dt.from_np(a.dtype), kind="ExternalInput").ap() for n, a in arrays.items()]
    out = nc.dram_tensor("out_t", (D, SEQ), F32, kind="ExternalOutput").ap()
    build(nc, *args, out)
    r = run_bass_kernel_spmd(nc, [{f"in_{n}": a for n, a in arrays.items()}], core_ids=[0])
    return np.ascontiguousarray(r.results[0]["out_t"].T).reshape(1, SEQ, D)
```
